# Optimizing a Trainium2 kernel written in Bass

```python
import jax, jax.numpy as jnp
from jax import lax
import numpy as np

D_MODEL = 2048
BATCH = 1
SEQ = 256
DEPTH = 1
DEC_BATCH = 8
DEC_SEQ = 4
PAST_LEN = 1024
PAGE_SIZE = 128

HEAD_DIM = 128
N_MIX_HEADS = D_MODEL // HEAD_DIM
MEM_HEADS = 4
FOX_HEADS = (N_MIX_HEADS - MEM_HEADS) // 2
HGRN_HEADS = N_MIX_HEADS - MEM_HEADS - FOX_HEADS
FOX_W = FOX_HEADS * HEAD_DIM
HGRN_W = HGRN_HEADS * HEAD_DIM
MEM_W = MEM_HEADS * HEAD_DIM
MIX_W = FOX_W + HGRN_W + MEM_W
IN_W = 3 * FOX_W + FOX_HEADS + 4 * HGRN_W + MEM_W
MEM_TOKENS = 256
Q_BLOCK = 128
HGRN_CHUNK = 64
N_GROUPS = 4
EXPERTS_PER_GROUP = 8
N_EXPERTS = N_GROUPS * EXPERTS_PER_GROUP
EXPERT_FF = D_MODEL // 4
TOP_K = 2
MOE_BLOCK = 128
EPS = 1e-6
FOX_FORGET_BIAS = 2.0

kernel_name = 'hymba_fox_hgrn2_hier_moe_step'

def rms_norm(x, g):
    xf = x.astype(jnp.float32)
    y = xf * lax.rsqrt(jnp.mean(xf * xf, axis=-1, keepdims=True) + EPS)
    return (y * g.astype(jnp.float32)).astype(x.dtype)

def project(xn, w_in, b_f, g_fq, g_fk, lb, g_mq):
    B, L, _ = xn.shape
    sizes = (FOX_W, FOX_W, FOX_W, FOX_HEADS, HGRN_W, HGRN_W, HGRN_W, HGRN_W)
    cuts, acc = [], 0
    for s in sizes:
        acc += s
        cuts.append(acc)
    fq, fk, fv, ff, hq, hf, hi, hg, mq = jnp.split(xn @ w_in, cuts, axis=-1)
    heads = lambda t, n: t.reshape(B, L, n, HEAD_DIM)
    fox_q = rms_norm(heads(fq, FOX_HEADS), g_fq)
    fox_k = rms_norm(heads(fk, FOX_HEADS), g_fk)
    fox_v = heads(fv, FOX_HEADS)
    fox_logf = jax.nn.log_sigmoid((ff + b_f).astype(jnp.float32))
    z = heads(hf, HGRN_HEADS).astype(jnp.float32)
    hgrn_logf = jnp.logaddexp(jnp.log(lb), jnp.log1p(-lb) + jax.nn.log_sigmoid(z))
    hgrn_k = -jnp.expm1(hgrn_logf)
    hgrn_q = jax.nn.silu(heads(hq, HGRN_HEADS)) * HEAD_DIM ** -0.5
    hgrn_v = heads(hi, HGRN_HEADS)
    mem_q = rms_norm(heads(mq, MEM_HEADS), g_mq)
    return fox_q, fox_k, fox_v, fox_logf, hgrn_q, hgrn_k, hgrn_v, hgrn_logf, hg, mem_q

def fox_attend(q, k, v, c_q, c_k, q_pos, k_pos):
    s = jnp.einsum('bqhd,bkhd->bhqk', q, k).astype(jnp.float32) * HEAD_DIM ** -0.5
    s = s + (jnp.swapaxes(c_q, 1, 2)[..., :, None] - jnp.swapaxes(c_k, 1, 2)[..., None, :])
    s = jnp.where(k_pos[None, :] <= q_pos[:, None], s, -jnp.inf)
    p = jax.nn.softmax(s, axis=-1).astype(v.dtype)
    return jnp.einsum('bhqk,bkhd->bqhd', p, v)

def fox_prompt(q, k, v, logf):
    B, S, H, Dh = q.shape
    nb = S // Q_BLOCK
    c = jnp.cumsum(logf, axis=1)
    k_pos = jnp.arange(S)
    qb = jnp.moveaxis(q.reshape(B, nb, Q_BLOCK, H, Dh), 1, 0)
    cb = jnp.moveaxis(c.reshape(B, nb, Q_BLOCK, H), 1, 0)

    def block(args):
        i, q_i, c_i = args
        q_pos = i * Q_BLOCK + jnp.arange(Q_BLOCK)
        return fox_attend(q_i, k, v, c_i, c, q_pos, k_pos)

    o = lax.map(block, (jnp.arange(nb), qb, cb))
    return jnp.moveaxis(o, 0, 1).reshape(B, S, H, Dh)

def hgrn2_chunked(q, k, v, logf, S0):
    B, L, H, Dk = q.shape
    out_dtype, st_dtype = v.dtype, S0.dtype
    q, k, v, logf = (a.astype(jnp.float32) for a in (q, k, v, logf))
    C = HGRN_CHUNK if L % HGRN_CHUNK == 0 else L
    n = L // C
    to_chunks = lambda a: jnp.moveaxis(a.reshape(B, n, C, *a.shape[2:]), 1, 0)
    tri = jnp.tril(jnp.ones((C, C), bool))[None, :, :, None, None]

    def step(S, inp):
        qc, kc, vc, gc = inp
        b = jnp.cumsum(gc, axis=1)
        o_inter = jnp.einsum('bthk,bhkv->bthv', qc * jnp.exp(b), S)
        diff = b[:, :, None] - b[:, None, :]
        decay = jnp.exp(jnp.where(tri, diff, -jnp.inf))
        A = jnp.einsum('bthk,btshk,bshk->bhts', qc, decay, kc)
        o_intra = jnp.einsum('bhts,bshv->bthv', A, vc)
        b_last = b[:, -1]
        S_new = S * jnp.exp(b_last)[..., None] + jnp.einsum(
            'bshk,bshv->bhkv', kc * jnp.exp(b_last[:, None] - b), vc)
        return S_new, o_inter + o_intra

    S_fin, o = lax.scan(step, S0.astype(jnp.float32),
                        (to_chunks(q), to_chunks(k), to_chunks(v), to_chunks(logf)))
    o = jnp.moveaxis(o, 0, 1).reshape(B, L, H, -1)
    return o.astype(out_dtype), S_fin.astype(st_dtype)

def memory_kv(mem, g_mem, w_mkv, g_mk):
    B, M, _ = mem.shape
    mk, mv = jnp.split(rms_norm(mem, g_mem) @ w_mkv, 2, axis=-1)
    mk = rms_norm(mk.reshape(B, M, MEM_HEADS, HEAD_DIM), g_mk)
    return mk, mv.reshape(B, M, MEM_HEADS, HEAD_DIM)

def memory_attend(q, mk, mv):
    s = jnp.einsum('bqhd,bmhd->bhqm', q, mk).astype(jnp.float32) * HEAD_DIM ** -0.5
    p = jax.nn.softmax(s, axis=-1).astype(mv.dtype)
    return jnp.einsum('bhqm,bmhd->bqhd', p, mv)

def merge_heads(fox_o, hgrn_o, hg, mem_o, g_hn, w_out):
    B, L = fox_o.shape[:2]
    hgrn_o = rms_norm(hgrn_o, g_hn).reshape(B, L, HGRN_W) * jax.nn.silu(hg)
    cat = jnp.concatenate([fox_o.reshape(B, L, FOX_W), hgrn_o, mem_o.reshape(B, L, MEM_W)], axis=-1)
    return cat @ w_out

def expert_dispatch(x, expert, gate, w_gate, w_up, w_down):
    T, D = x.shape
    A = T * TOP_K
    n_blocks = -(-(A + N_EXPERTS * (MOE_BLOCK - 1)) // MOE_BLOCK)
    cap = n_blocks * MOE_BLOCK
    flat_e = expert.reshape(A)
    flat_t = jnp.repeat(jnp.arange(T, dtype=jnp.int32), TOP_K)
    flat_g = gate.reshape(A)
    order = jnp.argsort(flat_e)
    e_sorted = flat_e[order]
    counts = jnp.zeros((N_EXPERTS,), jnp.int32).at[flat_e].add(1)
    padded = (counts + MOE_BLOCK - 1) // MOE_BLOCK * MOE_BLOCK
    pad_start = jnp.cumsum(padded) - padded
    start = jnp.cumsum(counts) - counts
    dest = pad_start[e_sorted] + jnp.arange(A, dtype=jnp.int32) - start[e_sorted]
    slot_tok = jnp.full((cap,), T, jnp.int32).at[dest].set(flat_t[order])
    slot_gate = jnp.zeros((cap,), jnp.float32).at[dest].set(flat_g[order])
    block_first = jnp.arange(n_blocks, dtype=jnp.int32) * MOE_BLOCK
    block_e = jnp.minimum(jnp.searchsorted(jnp.cumsum(padded), block_first, side='right'), N_EXPERTS - 1)
    x_pad = jnp.concatenate([x, jnp.zeros((1, D), x.dtype)], axis=0)

    def run(args):
        e, tok = args
        xb = x_pad[tok]
        return (jax.nn.silu(xb @ w_gate[e]) * (xb @ w_up[e])) @ w_down[e]

    y = lax.map(run, (block_e, slot_tok.reshape(n_blocks, MOE_BLOCK))).reshape(cap, D)
    y = y * slot_gate[:, None].astype(y.dtype)
    return jnp.zeros((T + 1, D), y.dtype).at[slot_tok].add(y)[:T]

def hier_moe(xn, w_rg, b_rg, w_re, b_re, w_gate, w_up, w_down):
    B, L, D = xn.shape
    T = B * L
    x = xn.reshape(T, D)
    g_logits = (x @ w_rg + b_rg).astype(jnp.float32)
    g_sel = jnp.argmax(g_logits, axis=-1)
    g_prob = jnp.take_along_axis(jax.nn.softmax(g_logits, axis=-1), g_sel[:, None], axis=1)
    e_logits = (x @ w_re + b_re).astype(jnp.float32).reshape(T, N_GROUPS, EXPERTS_PER_GROUP)
    e_in = jnp.take_along_axis(e_logits, g_sel[:, None, None], axis=1)[:, 0]
    top_v, top_i = lax.top_k(e_in, TOP_K)
    gate = g_prob * jax.nn.softmax(top_v, axis=-1)
    expert = (g_sel[:, None] * EXPERTS_PER_GROUP + top_i).astype(jnp.int32)
    return expert_dispatch(x, expert, gate, w_gate, w_up, w_down).reshape(B, L, D)

def setup_inputs(seed: int = 0) -> dict:
    key = jax.random.key(seed)
    ks = iter(jax.random.split(key, 40))
    nrm = lambda shape, scale=1.0: jax.random.normal(next(ks), shape, jnp.float32) * scale
    gain = lambda shape: 1.0 + 0.02 * nrm(shape)
    n_pages = PAST_LEN // PAGE_SIZE
    n_used = DEC_BATCH * n_pages
    n_pool = n_used + max(1, n_used // 4)
    page_table = jax.random.permutation(next(ks), n_pool)[:n_used].reshape(DEC_BATCH, n_pages).astype(jnp.int32)
    return {
        'x_prompt': nrm((BATCH, SEQ, D_MODEL)),
        'x_sample': nrm((DEC_BATCH, DEC_SEQ, D_MODEL)),
        'cache_fox_k': nrm((DEPTH, n_pool, PAGE_SIZE, FOX_HEADS, HEAD_DIM)),
        'cache_fox_v': nrm((DEPTH, n_pool, PAGE_SIZE, FOX_HEADS, HEAD_DIM)),
        'cache_fox_logf': jax.nn.log_sigmoid(FOX_FORGET_BIAS + nrm((DEPTH, n_pool, PAGE_SIZE, FOX_HEADS))),
        'cache_mem_k': nrm((DEPTH, DEC_BATCH, MEM_TOKENS, MEM_HEADS, HEAD_DIM)),
        'cache_mem_v': nrm((DEPTH, DEC_BATCH, MEM_TOKENS, MEM_HEADS, HEAD_DIM)),
        'state_hgrn': nrm((DEPTH, DEC_BATCH, HGRN_HEADS, HEAD_DIM, HEAD_DIM), 0.5),
        'page_table': page_table,
        'mem_prompt': nrm((BATCH, MEM_TOKENS, D_MODEL)),
        'g_attn_norm': gain((DEPTH, D_MODEL)),
        'w_in': nrm((DEPTH, D_MODEL, IN_W), D_MODEL ** -0.5),
        'b_fox_f': FOX_FORGET_BIAS + 0.1 * nrm((DEPTH, FOX_HEADS)),
        'g_fox_q': gain((DEPTH, HEAD_DIM)),
        'g_fox_k': gain((DEPTH, HEAD_DIM)),
        'lb_logits': nrm((DEPTH + 1, HGRN_W), 0.1),
        'g_hgrn_out': gain((DEPTH, HEAD_DIM)),
        'g_mem_norm': gain((DEPTH, D_MODEL)),
        'w_mem_kv': nrm((DEPTH, D_MODEL, 2 * MEM_W), D_MODEL ** -0.5),
        'g_mem_q': gain((DEPTH, HEAD_DIM)),
        'g_mem_k': gain((DEPTH, HEAD_DIM)),
        'w_out': nrm((DEPTH, MIX_W, D_MODEL), MIX_W ** -0.5),
        'g_ffn_norm': gain((DEPTH, D_MODEL)),
        'w_router_group': nrm((DEPTH, D_MODEL, N_GROUPS), D_MODEL ** -0.5),
        'b_router_group': nrm((DEPTH, N_GROUPS), 0.01),
        'w_router_expert': nrm((DEPTH, D_MODEL, N_EXPERTS), D_MODEL ** -0.5),
        'b_router_expert': nrm((DEPTH, N_EXPERTS), 0.01),
        'w_gate_e': nrm((DEPTH, N_EXPERTS, D_MODEL, EXPERT_FF), D_MODEL ** -0.5),
        'w_up_e': nrm((DEPTH, N_EXPERTS, D_MODEL, EXPERT_FF), D_MODEL ** -0.5),
        'w_down_e': nrm((DEPTH, N_EXPERTS, EXPERT_FF, D_MODEL), EXPERT_FF ** -0.5),
    }

def reference(x_prompt, x_sample, cache_fox_k, cache_fox_v, cache_fox_logf, cache_mem_k, cache_mem_v,
              state_hgrn, page_table, mem_prompt, g_attn_norm, w_in, b_fox_f, g_fox_q, g_fox_k,
              lb_logits, g_hgrn_out, g_mem_norm, w_mem_kv, g_mem_q, g_mem_k, w_out, g_ffn_norm,
              w_router_group, b_router_group, w_router_expert, b_router_expert,
              w_gate_e, w_up_e, w_down_e):
    Bp = x_prompt.shape[0]
    Bd, L = x_sample.shape[:2]
    P = page_table.shape[1] * cache_fox_k.shape[2]
    lbs = jnp.cumsum(jax.nn.softmax(lb_logits.astype(jnp.float32), axis=0), axis=0)
    hp, hs = x_prompt, x_sample
    fkp, fvp, flp, hsp, mkp, mvp, fks, fvs, fls, hss = ([] for _ in range(10))
    for l in range(DEPTH):
        lb = lbs[l].reshape(HGRN_HEADS, HEAD_DIM)
        fq, fk, fv, flf, hq, hk, hv, hlf, hg, mq = project(
            rms_norm(hp, g_attn_norm[l]), w_in[l], b_fox_f[l], g_fox_q[l], g_fox_k[l], lb, g_mem_q[l])
        fox_o = fox_prompt(fq, fk, fv, flf)
        S0 = jnp.zeros((Bp, HGRN_HEADS, HEAD_DIM, HEAD_DIM), jnp.float32)
        hgrn_o, S_p = hgrn2_chunked(hq, hk, hv, hlf, S0)
        mk, mv = memory_kv(mem_prompt, g_mem_norm[l], w_mem_kv[l], g_mem_k[l])
        mem_o = memory_attend(mq, mk, mv)
        hp = hp + merge_heads(fox_o, hgrn_o, hg, mem_o, g_hgrn_out[l], w_out[l])
        hp = hp + hier_moe(rms_norm(hp, g_ffn_norm[l]), w_router_group[l], b_router_group[l],
                           w_router_expert[l], b_router_expert[l], w_gate_e[l], w_up_e[l], w_down_e[l])
        fkp.append(fk); fvp.append(fv); flp.append(flf); hsp.append(S_p); mkp.append(mk); mvp.append(mv)
        fq, fk, fv, flf, hq, hk, hv, hlf, hg, mq = project(
            rms_norm(hs, g_attn_norm[l]), w_in[l], b_fox_f[l], g_fox_q[l], g_fox_k[l], lb, g_mem_q[l])
        k_all = jnp.concatenate([cache_fox_k[l][page_table].reshape(Bd, P, FOX_HEADS, HEAD_DIM), fk], axis=1)
        v_all = jnp.concatenate([cache_fox_v[l][page_table].reshape(Bd, P, FOX_HEADS, HEAD_DIM), fv], axis=1)
        lf_past = cache_fox_logf[l][page_table].reshape(Bd, P, FOX_HEADS).astype(jnp.float32)
        c_all = jnp.cumsum(jnp.concatenate([lf_past, flf], axis=1), axis=1)
        c_all = c_all - c_all[:, -1:]
        fox_o = fox_attend(fq, k_all, v_all, c_all[:, P:], c_all, P + jnp.arange(L), jnp.arange(P + L))
        hgrn_o, S_s = hgrn2_chunked(hq, hk, hv, hlf, state_hgrn[l])
        mem_o = memory_attend(mq, cache_mem_k[l], cache_mem_v[l])
        hs = hs + merge_heads(fox_o, hgrn_o, hg, mem_o, g_hgrn_out[l], w_out[l])
        hs = hs + hier_moe(rms_norm(hs, g_ffn_norm[l]), w_router_group[l], b_router_group[l],
                           w_router_expert[l], b_router_expert[l], w_gate_e[l], w_up_e[l], w_down_e[l])
        fks.append(fk); fvs.append(fv); fls.append(flf); hss.append(S_s)
    return (hp, hs,
            jnp.stack(fkp), jnp.stack(fvp), jnp.stack(flp), jnp.stack(hsp), jnp.stack(mkp), jnp.stack(mvp),
            jnp.stack(fks), jnp.stack(fvs), jnp.stack(fls), jnp.stack(hss))


_drawn_inputs = setup_inputs


def setup_inputs(seed=0):
    import zlib

    import numpy as np

    out = dict(_drawn_inputs(seed))
    spreads = {}
    factors = {'g_fox_q': 14.61,
     'g_fox_k': 8.123,
     'g_hgrn_out': 11.51,
     'g_mem_norm': 2.795,
     'g_mem_q': 8.0,
     'g_mem_k': 2.946,
     'b_router_group': 28.227,
     'b_router_expert': 18.03,
     'g_ffn_norm': 3.879,
     'cache_fox_logf': 2.779}
    for name, (base, spread) in spreads.items():
        noise = np.random.default_rng([zlib.crc32(name.encode()), seed]).standard_normal(out[name].shape)
        drawn = base * np.exp(spread * noise) if base else spread * noise
        out[name] = __import__('jax').numpy.asarray(drawn.astype(out[name].dtype))
    for name, factor in factors.items():
        out[name] = (out[name] * factor).astype(out[name].dtype)
    return out
```

```python
from contextlib import ExitStack

import concourse.bass as bass
from concourse import mybir

D = 2048
P = 128
KC = D // P
SEQ = 256
NB, NL = 8, 4
NS = NB * NL
T = SEQ + NS
TILES = [(0, P), (P, P), (SEQ, NS)]
MEM = 256
HF, HG, HM = 6, 6, 4
FW, MW = HF * P, HM * P
IN_W = 7 * FW + HF + MW
FF_COL = 3 * FW
NPG, PG = 8, 128
POOL = 80
PAST = NPG * PG
KEYS = PAST + NS
CH = 16
NCH = SEQ // CH
NE, NG, EPG = 32, 4, 8
FFW = 512
FB = FFW // P
EPS = 1e-6
SCALE = float(P) ** -0.5
NEG = -1.0e30
HQ, HFG, HI, HGT, FQ, FK, FV, MQ = 0, 6, 12, 18, 24, 30, 36, 42
NBLK = 46


def build(nc, x_prompt, x_sample, cache_fox_k, cache_fox_v, cache_fox_logf, cache_mem_k, cache_mem_v,
          state_hgrn, page_table, mem_prompt, g_attn_norm, w_in, b_fox_f, g_fox_q, g_fox_k, lb_logits,
          g_hgrn_out, g_mem_norm, w_mem_kv, g_mem_q, g_mem_k, w_out, g_ffn_norm, w_router_group,
          b_router_group, w_router_expert, b_router_expert, w_gate_e, w_up_e, w_down_e,
          y_prompt, y_sample, fox_k_p, fox_v_p, fox_logf_p, hgrn_state_p, mem_k_p, mem_v_p,
          fox_k_s, fox_v_s, fox_logf_s, hgrn_state_s, dbg=None):
    f32, i32 = mybir.dt.float32, mybir.dt.int32
    ALU, ACT, AX = mybir.AluOpType, mybir.ActivationFunctionType, mybir.AxisListType
    ds = bass.ds

    x_tok_d = [x_prompt[0, 0:P, :], x_prompt[0, P:SEQ, :], x_sample.rearrange("b l d -> (b l) d")]
    mem_tok_d = [mem_prompt[0, 0:P, :], mem_prompt[0, P:MEM, :]]
    w_in_d = w_in[0].rearrange("(k p) n -> p k n", p=P)
    w_kv_d = w_mem_kv[0].rearrange("(k p) n -> p k n", p=P)
    w_out_d = w_out[0].rearrange("(k p) n -> p k n", p=P)
    w_gate_d = w_gate_e[0].rearrange("e (k p) n -> e p k n", p=P)
    w_up_d = w_up_e[0].rearrange("e (k p) n -> e p k n", p=P)
    w_down_d = w_down_e[0].rearrange("e (k p) n -> e p k n", p=P)
    w_rg_d = w_router_group[0].rearrange("(k p) n -> p k n", p=P)
    w_re_d = w_router_expert[0].rearrange("(k p) n -> p k n", p=P)
    y_tok_d = [y_prompt[0, 0:P, :], y_prompt[0, P:SEQ, :], y_sample.rearrange("b l d -> (b l) d")]
    logf_d = cache_fox_logf[0].rearrange("g t h -> g (t h)")
    k_pages = cache_fox_k[0].rearrange("g t h d -> g t (h d)")
    v_pages = cache_fox_v[0].rearrange("g t h d -> g t (h d)")

    ctx = ExitStack()
    with ctx:
        ctx.enter_context(nc.allow_non_contiguous_dma(reason="small vectors and column blocks"))

        def sb(name, shape, dt=f32):
            return ctx.enter_context(nc.sbuf_tensor(name, shape, dt))

        def sem(name):
            return ctx.enter_context(nc.semaphore(name))

        ident = sb("ident", [P, P])
        ones = sb("ones", [P, P])
        tri_le = sb("tri_le", [P, P])
        tri_gt = sb("tri_gt", [P, P])
        causal = sb("causal", [P, P])
        head_row = sb("head_row", [HF, HF, P])
        sel48 = sb("sel48", [NB * HF, NB, HF, NL])
        causal4 = sb("causal4", [NL, NB, NS])
        rep4 = sb("rep4", [NL, HF, NL])
        batch_of = sb("batch_of", [NS, NB])
        chunk_of = sb("chunk_of", [P, P // CH])
        rows = sb("rows", [65, P])
        cols = sb("cols", [P, 65])
        eps_t = sb("eps_t", [P, 1])
        one_t = sb("one_t", [P, 1])
        lbw = sb("lbw", [P, 6, HG])
        gq = sb("gq", [P, 5])
        ssq = sb("ssq", [P, 8])
        rstd = sb("rstd", [P, 8])
        b_f = sb("b_f", [HF, 1])
        G_ATT, G_MEM, G_FFN = cols[:, 0:KC], cols[:, KC:2 * KC], cols[:, 2 * KC:3 * KC]
        g_fq, g_fk, g_hn, g_mq, g_mk = (cols[:, 48 + n:49 + n] for n in range(5))
        lb0, lb1 = cols[:, 53:59], cols[:, 59:65]
        LB, LB1 = lbw[:, 4, :], lbw[:, 5, :]

        arena = sb("arena", [P, 45960])

        def view(off, *dims):
            n = 1
            for d in dims:
                n *= d
            a = arena[:, off:off + n]
            if len(dims) == 2:
                return a.rearrange("p (a b) -> p a b", b=dims[1])
            if len(dims) == 3:
                return a.rearrange("p (a b c) -> p a b c", b=dims[1], c=dims[2])
            return a

        RAW = 0
        CAT = RAW + NBLK * T
        MRAW = CAT + KC * T
        MTOK = MRAW + 8 * MEM
        TOK = MTOK + 2 * 1024
        WORK = TOK + 9 * FW
        raw = view(RAW, NBLK, T)
        x_tok = view(RAW, 3, D)
        mem_tok_in = view(RAW + 3 * D, 2, D)
        junk = view(CAT, D)
        cat = view(CAT, KC, T)
        mraw = view(MRAW, 8, MEM)
        mtok = view(MTOK, 2, 1024)
        memT = view(TOK, KC, MEM)
        ktok, vtok = (view(TOK + n * 3 * FW, 3, FW) for n in range(2))
        xT = view(WORK, KC, T)
        wslot = [view(WORK + KC * T + n * KC * 384, KC, 384) for n in range(2)]
        w_ff = view(WORK + KC * T + 2 * KC * 384, KC, HF)
        WEND = WORK + KC * T + 2 * KC * 384 + KC * HF

        def heads2(n):
            return view(TOK + n * 2 * T, 2, T)

        gQ, gF, gV, gO, gKT, gTmp = (heads2(n) for n in range(6))
        gW = [heads2(6), heads2(7)]
        gQW = [heads2(8), heads2(9)]
        gS = view(TOK + 10 * 2 * T, 160)
        decays = sb("decays", [P, HG, NCH + NB])
        vpar = view(TOK, 2, 2, FW)
        vsam = view(TOK + 4 * FW, FW)[0:NS]
        states = view(TOK + 5 * FW, NCH, P)
        vmask = [view(TOK + 5 * FW + NCH * P + n * 4 * P, 4, P)[0:NS] for n in range(2)]
        s_in = [view(MTOK + n * NB * P, NB, P) for n in range(2)]
        ktil = sb("ktil", [P, 3, P])
        parity = sb("parity", [P, 2])
        probs = view(WORK, 2, SEQ)
        probsT = view(WORK + 2 * SEQ, 2, 2, P)
        kring = view(WORK, 4, FW)
        vpages = view(WORK + 4 * FW, NPG, FW)
        keysT = view(WORK + 12 * FW, HF, PAST)
        dprob = view(WORK + 12 * FW + HF * PAST, KEYS)
        mk_in = view(MRAW, 2, MW)
        mv_in = view(MRAW + 2 * MW, 2, MW)
        mkeysT = view(MRAW + 4 * MW, HM, MEM)
        mprob = view(MRAW + 4 * MW + HM * MEM, MEM)
        dprobT = view(MRAW + 4 * MW + HM * MEM + MEM, 248)
        dpT = dprobT[:, 0:192].rearrange("p (g r) -> p g r", r=24)
        mpT = dprobT[:, 192:224].rearrange("p (g r) -> p g r", r=16)
        npT = dprobT[0:NS, 224:248]
        wo_slot = [view(o, KC, 256) for o in (RAW, WORK, WORK + 4096)]
        attnT = view(WORK + 9216, 2, T)
        h_tok = view(TOK, 3, D)
        UNIT = 4096
        unit = [view(n * UNIT, UNIT) for n in range(5)] + [view(TOK + 3 * D, UNIT)]
        wg_u = [unit[n].rearrange("p (k n) -> p k n", k=KC) for n in (0, 2)]
        wu_u = [unit[n].rearrange("p (k n) -> p k n", k=KC) for n in (1, 3)]
        wd_u = [unit[n].rearrange("p (k n) -> p k n", k=FB) for n in (4, 5)]
        MOE = TOK + 3 * D + UNIT
        xnT = view(MOE, KC, T)
        yT = view(MOE + KC * T, KC, T)
        hT = view(MOE + 2 * KC * T, FB, T)
        LATE = MOE + 2 * KC * T + FB * T

        def late(*dims):
            nonlocal LATE
            n = 1
            for d in dims:
                n *= d
            LATE += n
            return view(LATE - n, *dims)

        gbc = late(T)
        gcol = late(3, P)
        hS = late(2, T)
        logits = late(3, NG + NE)
        w_rt = view(MOE + 2 * KC * T, KC, NG + NE)
        h_scaled = view(0, 3, D)
        b_rt = late(NG + NE)[0:1]
        rw = late(3, 2 * NE)
        gates = late(3, NE)
        choice = late(3, 2, NE)
        c1g = late(3, NE)
        HTF = [(t, c, 4) for t in range(2) for c in range(0, KC, 4)] + [(2, 0, KC)]
        HT_FILLS = len(HTF)

        def ht_out(f):
            t, c, m = HTF[f]
            return PS[:, 4 * (f % 2), :].rearrange("p (c t) -> p c t", c=m)[:, :, 0:TILES[t][1]]

        q_rows = sb("q_rows", [P, HF * 28])
        mq_rows = sb("mq_rows", [P, HM * 20])
        sel_b = sb("sel_b", [NB * HF, HF * NL])
        causal_b = view(WORK + 12 * FW + HF * PAST + KEYS, NS)[0:NL]
        nmax = sb("nmax", [P, 4])
        psum_p = sb("psum_p", [P, 4])
        ptab_row = sb("ptab_row", [1, NB * NPG], i32)

        ffz = sb("ffz", [HF, T])
        ffw = sb("ffw", [HF, T])
        lfT = sb("lfT", [HF, T])
        lftok = sb("lftok", [P, 3, HF])
        negc = sb("negc", [HF, SEQ])
        ptab = sb("ptab", [NB * NPG, 1], i32)
        lfpages = view(MTOK, PG * HF)[0:NB * NPG]
        lfp = sb("lfp", [P, NPG, NB, HF])
        lfs = sb("lfs", [P, NPG, NB, HF])
        lfm = sb("lfm", [NS, NB, HF])
        decay = sb("decay", [NB * HF, KEYS])

        sq = sb("sq", [P, 2, T])
        rs = sb("rs", [P, 2, T])

        PS = ctx.enter_context(nc.psum_tensor("PS", [P, 8, 512], f32))

        consts_set = sem("consts_set")
        rows_in = sem("rows_in")
        cols_filled = sem("cols_filled")
        cols_set = sem("cols_set")
        gains_set = sem("gains_set")
        tok_in = [sem(f"tok_in{n}") for n in range(5)]
        ssq_clear = sem("ssq_clear")
        ssq_done = sem("ssq_done")
        sqrt_done = sem("sqrt_done")
        rstd_done = sem("rstd_done")
        scaled = sem("scaled")
        tT_filled = sem("tT_filled")
        tT_drained = sem("tT_drained")
        w_in_slot = [sem(f"w_in_slot{n}") for n in range(2)]
        wff_in = sem("wff_in")
        blk_filled = sem("blk_filled")
        blk_drained = sem("blk_drained")
        hn_sq = sem("hn_sq")
        hn_sum = sem("hn_sum")
        hn_sqrt = sem("hn_sqrt")
        hn_rcp = sem("hn_rcp")
        hn_done = sem("hn_done")
        tk_filled = sem("tk_filled")
        tk_drained = sem("tk_drained")
        lf_act = sem("lf_act")
        lf_done = sem("lf_done")
        lft_filled = sem("lft_filled")
        lft_drained = sem("lft_drained")
        c_filled = sem("c_filled")
        negc_set = sem("negc_set")
        ptab_in = sem("ptab_in")
        lfpages_in = sem("lfpages_in")
        lfp_filled = sem("lfp_filled")
        lfp_drained = sem("lfp_drained")
        lfs_done = sem("lfs_done")
        lfm_done = sem("lfm_done")
        dec_filled = sem("dec_filled")
        decay_set = sem("decay_set")
        out_done = sem("out_done")
        wo_in = [sem(f"wo_in{n}") for n in range(3)]
        x_again = sem("x_again")
        wo_filled = sem("wo_filled")
        wo_drained = sem("wo_drained")
        at_filled = sem("at_filled")
        h_added = sem("h_added")
        rt_in = sem("rt_in")
        h_ssq = sem("h_ssq")
        h_sqrt = sem("h_sqrt")
        h_scl = sem("h_scl")
        ht_filled = sem("ht_filled")
        ht_drained = sem("ht_drained")
        lg_filled = sem("lg_filled")
        rt_sub = sem("rt_sub")
        rt_exp = sem("rt_exp")
        gates_set = sem("gates_set")
        unit_in = [sem(f"unit_in{n}") for n in range(6)]
        y_clear = sem("y_clear")
        gcol_set = sem("gcol_set")
        gb_filled = sem("gb_filled")
        gb_copied = sem("gb_copied")
        mg_filled = sem("mg_filled")
        mu_filled = sem("mu_filled")
        silu_done = sem("silu_done")
        hs_done = sem("hs_done")
        hT_done = sem("hT_done")
        md_filled = sem("md_filled")
        y_added = sem("y_added")
        yt_filled = sem("yt_filled")
        y_done = sem("y_done")
        y_out = sem("y_out")
        lb_diff = sem("lb_diff")
        lb_exp = sem("lb_exp")
        lb_set = sem("lb_set")
        hg_prep = sem("hg_prep")
        hg_step = sem("hg_step")
        qw_ready = sem("qw_ready")
        intra_filled = sem("intra_filled")
        intra_used = sem("intra_used")
        hg_done = sem("hg_done")
        parity_set = sem("parity_set")
        vt_filled = sem("vt_filled")
        vt_drained = sem("vt_drained")
        kt2_filled = sem("kt2_filled")
        kt2_drained = sem("kt2_drained")
        s_loaded = [sem(f"s_loaded{n}") for n in range(2)]
        os_filled = sem("os_filled")
        ds_filled = sem("ds_filled")
        ds_used = sem("ds_used")
        sm_set = sem("sm_set")
        oi_filled = sem("oi_filled")
        o_added = sem("o_added")
        sig_done = sem("sig_done")
        gate_done = sem("gate_done")
        st_step = sem("st_step")
        stp_out = sem("stp_out")
        sts_out = [sem(f"sts_out{n}") for n in range(2)]
        pa_scored = sem("pa_scored")
        pa_max = sem("pa_max")
        pa_exp = sem("pa_exp")
        pa_prob = sem("pa_prob")
        pa_t = sem("pa_t")
        pa_tc = sem("pa_tc")
        pa_pv = sem("pa_pv")
        pa_out = sem("pa_out")
        ptrow_in = sem("ptrow_in")
        k_in = [sem(f"k_in{n}") for n in range(4)]
        mk_loaded = sem("mk_loaded")
        v_loaded = sem("v_loaded")
        kt_filled = sem("kt_filled")
        kt_act = sem("kt_act")
        kt_dve = sem("kt_dve")
        q_clear = sem("q_clear")
        q_set = sem("q_set")
        d_scored = sem("d_scored")
        d_max = sem("d_max")
        d_exp = sem("d_exp")
        d_rcp = sem("d_rcp")
        d_prob = sem("d_prob")
        d_t = sem("d_t")
        d_tc = sem("d_tc")
        d_pv = sem("d_pv")
        d_out = sem("d_out")
        dve_step = sem("dve_step")
        pool_step = sem("pool_step")

        NORM = [(mem_tok_in[:, 0], P, 3), (mem_tok_in[:, 1], P, 4),
                (x_tok[:, 0], P, 0), (x_tok[:, 1], P, 1), (x_tok[:, 2], NS, 2)]
        FILLS = [(n, c, 4) for n in range(4) for c in range(0, KC, 4)] + [(4, 0, KC)]

        def fill_out(f, w):
            n, c, m = FILLS[f]
            return PS[:, f % 8, :].rearrange("p (c t) -> p c t", c=m)[:, :, 0:w]

        NORMS = [(raw[:, FQ + h, :], T, 0) for h in range(HF)] + [(raw[:, FK + h, :], T, 1) for h in range(HF)] + \
                [(raw[:, MQ + h, :], T, 2) for h in range(HM)] + [(mraw[:, h, :], MEM, 3) for h in range(HM)]
        NORMS += [(cat[:, 6 + h, :], T, 4) for h in range(HG)]
        NN = len(NORMS)

        TOKF = []
        for dst, b0 in ((ktok, FK), (vtok, FV)):
            for t, (t0, n) in enumerate(TILES):
                for h0, m in ((0, 4), (4, 2)):
                    TOKF.append((dst[0:n, t, h0 * P:(h0 + m) * P], n,
                                 [raw[:, b0 + h, t0:t0 + n] for h in range(h0, h0 + m)]))
        for t in range(2):
            for h0 in (0, 4):
                TOKF.append((mtok[:, t, h0 * P:(h0 + 4) * P], P,
                             [mraw[:, h, t * P:(t + 1) * P] for h in range(h0, h0 + 4)]))
        NTF = len(TOKF)

        UNITS = [(True, h, qb) for h in range(HF) for qb in range(2)] + \
                [(False, h, qb) for h in range(HM) for qb in range(2)]
        NU = len(UNITS)

        def width(u):
            fox, h, qb = UNITS[u]
            return (qb + 1) * P if fox else MEM

        ORDER = [3, 4, 5, 0, 1, 2]
        LAST = [FV + h for h in range(HF)] + [MQ + h for h in range(HM)]

        block = ctx.enter_context(nc.Block())

        @block.sync
        def _(sp):
            for n, d in ((0, mem_tok_d[0]), (1, mem_tok_d[1])):
                sp.dma_start(NORM[n][0], d).then_inc(tok_in[n], 16)
            sp.dma_start(rows[0:16, :], g_attn_norm[0].rearrange("(k p) -> k p", p=P)).then_inc(rows_in, 16)
            sp.dma_start(rows[16:32, :], g_mem_norm[0].rearrange("(k p) -> k p", p=P)).then_inc(rows_in, 16)
            sp.dma_start(rows[32:48, :], g_ffn_norm[0].rearrange("(k p) -> k p", p=P)).then_inc(rows_in, 16)
            for n, g in enumerate((g_fox_q, g_fox_k, g_hgrn_out, g_mem_q, g_mem_k)):
                sp.dma_start(rows[48 + n:49 + n, :], g).then_inc(rows_in, 16)
            sp.dma_start(rows[53:65, :], lb_logits.rearrange("l (h p) -> (l h) p", p=P)).then_inc(rows_in, 16)
            sp.dma_start(wslot[0], w_kv_d[:, :, 0:384]).then_inc(w_in_slot[0], 16)
            for n in range(3):
                sp.dma_start(NORM[2 + n][0][0:NORM[2 + n][1]], x_tok_d[n]).then_inc(tok_in[2 + n], 16)
            sp.dma_start(wslot[1], w_kv_d[:, :, 384:768]).then_inc(w_in_slot[1], 16)
            sp.dma_start(b_f[:, :], b_fox_f.rearrange("a h -> h a")).then_inc(rows_in, 16)
            sp.dma_start(w_ff, w_in_d[:, :, FF_COL:FF_COL + HF]).then_inc(wff_in, 16)
            sp.wait_ge(blk_filled, 3)
            sp.dma_start(wslot[0][:, :, 0:256], w_kv_d[:, :, 768:1024]).then_inc(w_in_slot[0], 16)
            for i0, ni, col in ((0, 4, FF_COL + HF), (4, 3, 0)):
                with sp.Fori(0, ni) as i:
                    sp.wait_ge(blk_filled, i * 6 + (6 * i0 + 6))
                    sp.dma_start(wslot[1], w_in_d[:, :, ds(i * FW + col, 384)]).then_inc(w_in_slot[1], 16)
                    sp.wait_ge(blk_filled, i * 6 + (6 * i0 + 8))
                    sp.dma_start(wslot[0], w_in_d[:, :, ds(i * FW + (col + 384), 384)]).then_inc(w_in_slot[0], 16)
            mq0 = IN_W - MW
            sp.wait_ge(blk_filled, 47)
            sp.dma_start(wslot[1][:, :, 0:256], w_in_d[:, :, mq0:mq0 + 256]).then_inc(w_in_slot[1], 16)
            sp.wait_ge(blk_filled, 50)
            sp.dma_start(wslot[0][:, :, 0:256], w_in_d[:, :, mq0 + 256:mq0 + 512]).then_inc(w_in_slot[0], 16)

            no = 0
            sp.wait_ge(tk_drained, NTF)
            for dst_p, dst_s, src in ((fox_k_p, fox_k_s, ktok), (fox_v_p, fox_v_s, vtok)):
                sp.dma_start(dst_p[0, 0].rearrange("(a t) h d -> t a (h d)", t=P), src[:, 0:2, :]).then_inc(out_done, 16)
                sp.dma_start(dst_s[0].rearrange("b l h d -> (b l) (h d)"), src[0:NS, 2, :]).then_inc(out_done, 16)
                no += 2
            for dst, c in ((mem_k_p, 0), (mem_v_p, 512)):
                sp.dma_start(dst[0, 0].rearrange("(a t) h d -> t a (h d)", t=P), mtok[:, :, c:c + 512]).then_inc(out_done, 16)
                no += 1
            sp.wait_ge(lft_drained, 1)
            sp.dma_start(fox_logf_p[0, 0].rearrange("(a t) h -> t a h", t=P), lftok[:, 0:2, :]).then_inc(out_done, 16)
            sp.dma_start(fox_logf_s[0].rearrange("b l h -> (b l) h"), lftok[0:NS, 2, :]).then_inc(out_done, 16)
            no += 2
            sp.dma_start(ptab_row[:, :], page_table.rearrange("(a b) g -> a (b g)", a=1)).then_inc(ptrow_in, 16)
            sp.wait_ge(ptrow_in, 16)
            sp.wait_ge(pa_out, NU)

            def decode_loads(b, first=False):
                for g in range(NPG):
                    page = sp.value_load(ptab_row[0:1, ds(b * NPG + g, 1)], min_val=0, max_val=POOL - 1)
                    if g >= 4:
                        sp.wait_ge(kt_filled, b * 9 + (g - 3))
                    elif not first:
                        sp.wait_ge(kt_filled, b * 9 + (g - 4))
                    sp.dma_start(kring[:, g % 4, :], k_pages[ds(page, 1)].rearrange("g t n -> t (g n)")).then_inc(k_in[g % 4], 16)
                    if g == 3:
                        if not first:
                            sp.wait_ge(kt_filled, b * 9)
                        sp.dma_start(mk_in, cache_mem_k[0][ds(b, 1)].rearrange("b (a t) h d -> t (b a) (h d)", t=P)).then_inc(mk_loaded, 16)
                for g in range(NPG):
                    page = sp.value_load(ptab_row[0:1, ds(b * NPG + g, 1)], min_val=0, max_val=POOL - 1)
                    if not first:
                        sp.wait_ge(d_pv, b)
                    sp.dma_start(vpages[:, g, :], v_pages[ds(page, 1)].rearrange("g t n -> t (g n)")).then_inc(v_loaded, 16)
                if not first:
                    sp.wait_ge(d_pv, b)
                sp.dma_start(mv_in, cache_mem_v[0][ds(b, 1)].rearrange("b (a t) h d -> t (b a) (h d)", t=P)).then_inc(v_loaded, 16)

            decode_loads(0, True)
            with sp.Fori(0, NB - 1) as i:
                decode_loads(i + 1)

            sp.wait_ge(hn_done, NN)
            sp.dma_start(wo_slot[0], w_out_d[:, :, 0:256]).then_inc(wo_in[0], 16)
            sp.wait_ge(d_pv, NB)
            for n in (1, 2):
                sp.dma_start(wo_slot[n], w_out_d[:, :, n * 256:(n + 1) * 256]).then_inc(wo_in[n], 16)
            sp.wait_ge(out_done, 16 * no)
            for t, (t0, n) in enumerate(TILES):
                sp.dma_start(h_tok[0:n, t, :], x_tok_d[t]).then_inc(x_again, 16)
            sp.dma_start(b_rt[:, 0:NG], b_router_group).then_inc(rt_in, 16)
            sp.dma_start(b_rt[:, NG:NG + NE], b_router_expert).then_inc(rt_in, 16)
            for n in range(3, 8):
                sp.wait_ge(wo_filled, 2 * (n - 2))
                sp.dma_start(wo_slot[n % 3], w_out_d[:, :, n * 256:(n + 1) * 256]).then_inc(wo_in[n % 3], 16)
            sp.dma_start(w_rt[:, :, 0:NG], w_rg_d).then_inc(rt_in, 16)
            sp.dma_start(w_rt[:, :, NG:NG + NE], w_re_d).then_inc(rt_in, 16)
            sp.wait_ge(ht_filled, HT_FILLS)

            def expert_loads(e, first=False):
                for c in range(2):
                    cols = slice(c * 256, (c + 1) * 256)
                    if not first:
                        sp.wait_ge(mg_filled, e * 4 + (2 * c - 2))
                    sp.dma_start(wg_u[c], w_gate_d[ds(e, 1), :, :, cols].rearrange("e p k n -> p (e k) n")).then_inc(unit_in[2 * c], 16)
                    if not first:
                        sp.wait_ge(mu_filled, e * 4 + (2 * c - 2))
                    sp.dma_start(wu_u[c], w_up_d[ds(e, 1), :, :, cols].rearrange("e p k n -> p (e k) n")).then_inc(unit_in[2 * c + 1], 16)
                for c in range(2):
                    cols = slice(c * 1024, (c + 1) * 1024)
                    if not first:
                        sp.wait_ge(md_filled, e * 16 + (8 * c - 7))
                    sp.dma_start(wd_u[c], w_down_d[ds(e, 1), :, :, cols].rearrange("e p k n -> p (e k) n")).then_inc(unit_in[4 + c], 16)

            expert_loads(0, True)
            with sp.Fori(0, NE - 1) as e:
                expert_loads(e + 1)
            for t, (t0, n) in enumerate(TILES):
                sp.wait_ge(y_done, 4 * t + 4)
                sp.dma_start(y_tok_d[t], h_tok[0:n, t, :]).then_inc(y_out, 16)
            sp.wait_ge(y_out, 48)

        @block.gpsimd
        def _(pool):
            n_set = 0

            def fill(ap, v):
                nonlocal n_set
                pool.memset(ap, v).then_inc(consts_set, 1)
                n_set += 1

            def pick(ap, op, value, base, pattern, cm):
                nonlocal n_set
                pool.wait_ge(consts_set, n_set)
                pool.affine_select(out=ap, in_=ap, compare_op=op, fill=value, base=base, pattern=pattern,
                                   channel_multiplier=cm).then_inc(consts_set, 1)
                n_set += 1

            fill(ident[:, :], 0.0)
            fill(ones[:, :], 1.0)
            pick(ident[:, :], ALU.not_equal, 1.0, 0, [[-1, P]], 1)
            fill(eps_t[:, :], EPS)
            fill(one_t[:, :], 1.0)
            fill(tri_le[:, :], 1.0)
            fill(tri_gt[:, :], 1.0)
            fill(causal[:, :], 0.0)
            fill(head_row[:, :, :], 0.0)
            fill(sel48[:, :, :, :], 0.0)
            fill(causal4[:, :, :], 0.0)
            fill(rep4[:, :, :], 0.0)
            fill(batch_of[:, :], 1.0)
            fill(chunk_of[:, :], 1.0)
            pick(tri_le[:, :], ALU.is_ge, 0.0, 0, [[1, P]], -1)
            pick(tri_gt[:, :], ALU.is_gt, 0.0, 0, [[-1, P]], 1)
            pick(causal[:, :], ALU.is_ge, NEG, 0, [[-1, P]], 1)
            pick(head_row[:, :, :], ALU.not_equal, 1.0, 0, [[-1, HF], [0, P]], 1)
            pick(sel48[:, :, :, :], ALU.not_equal, 1.0, 0, [[-HF, NB], [-1, HF], [0, NL]], 1)
            pick(causal4[:, :, :], ALU.is_ge, NEG, 0, [[-NL, NB], [1, NS]], 0)
            pick(causal4[:, :, :], ALU.is_ge, NEG, 0, [[NL, NB], [-1, NS]], 1)
            pick(rep4[:, :, :], ALU.not_equal, 1.0, 0, [[0, HF], [-1, NL]], 1)
            pick(batch_of[:, :], ALU.is_ge, 0.0, 0, [[-NL, NB]], 1)
            pick(batch_of[:, :], ALU.is_ge, 0.0, NL - 1, [[NL, NB]], -1)
            pick(chunk_of[:, :], ALU.is_ge, 0.0, 0, [[-CH, P // CH]], 1)
            pick(chunk_of[:, :], ALU.is_ge, 0.0, CH - 1, [[CH, P // CH]], -1)
            assert n_set == N_CONSTS, n_set
            pool.dma_start(ptab[:, :], page_table.rearrange("b (g a) -> (b g) a", a=1)).then_inc(ptab_in, 16)
            pool.wait_ge(ptab_in, 16)
            pool.indirect_dma_start(out=lfpages, out_offset=None, in_=logf_d,
                                    in_offset=bass.IndirectOffsetOnAxis(ap=ptab[:, 0:1], axis=0)).then_inc(lfpages_in, 16)
            pool.wait_ge(lfp_filled, 1)
            for h in range(2):
                pool.dma_start(s_in[h], state_hgrn[0, :, h].rearrange("b k v -> k b v")).then_inc(s_loaded[h], 16)
            def states_out(h):
                pool.wait_ge(ds_used, 10 * h + 8)
                pool.dma_start(hgrn_state_p[0, 0, h], states[:, NCH - 1, :]).then_inc(stp_out, 16)
                pool.wait_ge(ds_used, 10 * h + 10)
                pool.dma_start(hgrn_state_s[0, :, h].rearrange("b k v -> k b v"), s_in[h % 2]).then_inc(sts_out[h % 2], 16)
                if h + 2 < HG:
                    pool.wait_ge(sts_out[h % 2], 16 * (h // 2 + 1))
                    pool.dma_start(s_in[h % 2], state_hgrn[0, :, h + 2].rearrange("b k v -> k b v")).then_inc(s_loaded[h % 2], 16)

            pool.wait_ge(vt_drained, 6)
            for h in range(HG):
                for c in range(2):
                    if h:
                        pool.wait_ge(ds_filled, 10 * (h - 1) + 9 + c)
                    pool.tensor_tensor(vmask[c], vsam[:, h * P:(h + 1) * P].rearrange("p (a v) -> p a v", a=1).to_broadcast([NS, 4, P]),
                                       batch_of[:, 4 * c:4 * c + 4].rearrange("p (b a) -> p b a", a=1).to_broadcast([NS, 4, P]),
                                       ALU.mult).then_inc(sm_set, 1)
                if h:
                    states_out(h - 1)
            states_out(HG - 1)
            pool.wait_ge(stp_out, 16 * HG)
            for n in range(2):
                pool.wait_ge(sts_out[n], 16 * HG // 2)

        @block.scalar
        def _(act):
            act.wait_ge(consts_set, N_CONSTS)
            act.wait_ge(ssq_clear, 1)
            for n, (src, m, c) in enumerate(NORM):
                act.wait_ge(tok_in[n], 16)
                if n:
                    act.wait_ge(ssq_done, n)
                act.activation(junk[0:m, :], src[0:m], ACT.Square, accum_out=ssq[0:m, c:c + 1]).then_inc(ssq_done, 1)
                act.wait_ge(ssq_done, n + 1)
                act.activation(rstd[0:m, c:c + 1], ssq[0:m, c:c + 1], ACT.Sqrt, bias=eps_t[0:m, :], scale=1.0 / D).then_inc(sqrt_done, 1)
            act.wait_ge(lb_diff, 1)
            act.activation(lbw[:, 2:4, :], lbw[:, 0:2, :], ACT.Exp).then_inc(lb_exp, 1)
            for j in range(8):
                act.wait_ge(blk_filled, j + 1)
                act.activation(mraw[:, j, :], PS[:, j, 0:MEM], ACT.Copy).then_inc(blk_drained, 1)
            with act.Fori(0, 3) as i:
                for n, j in enumerate(ORDER):
                    act.wait_ge(blk_filled, i * 6 + (8 + n + 1))
                    act.activation(raw[:, ds(i * 6 + n, 1), :], PS[:, j:j + 1, 0:T], ACT.Copy).then_inc(blk_drained, 1)
            act.wait_ge(blk_drained, 26)
            with act.Fori(0, 3) as g:
                act.wait_ge(hg_done, g + 1)
                zq, zf = raw[:, ds(g * 2 + HQ, 2), :], raw[:, ds(g * 2 + HFG, 2), :]
                act.activation(gQ, zq, ACT.Sigmoid)
                act.activation(gF, zf, ACT.Sigmoid)
                act.activation(gW[0], zf, ACT.Sigmoid, scale=-1.0)
                act.activation(gV, raw[:, ds(g * 2 + HI, 2), :], ACT.Copy).then_inc(hg_prep, 1)
                for n, j in enumerate(ORDER):
                    act.wait_ge(blk_filled, g * 6 + (26 + n + 1))
                    act.activation(raw[:, ds(g * 6 + (HGT + n), 1), :], PS[:, j:j + 1, 0:T], ACT.Copy).then_inc(blk_drained, 1)

            def block_out(n):
                act.wait_ge(blk_filled, 44 + n + 1)
                act.activation(raw[:, LAST[n], :], PS[:, n % 4, 0:T], ACT.Copy).then_inc(blk_drained, 1)

            act.wait_ge(parity_set, 1)
            act.wait_ge(hg_done, 4)
            for f in range(6):
                t, c, m = f // 2, (f % 2) * 4, 4 - 2 * (f % 2)
                act.wait_ge(vt_filled, f + 1)
                src = PS[:, 6 + f % 2, 0:m * P]
                if t < 2:
                    act.activation(vpar[:, 0, t, c * P:(c + m) * P], src, ACT.Copy, scale=parity[:, 0:1])
                    act.activation(vpar[:, 1, t, c * P:(c + m) * P], src, ACT.Copy, scale=parity[:, 1:2]).then_inc(vt_drained, 1)
                else:
                    act.activation(vsam[:, c * P:(c + m) * P], src[0:NS], ACT.Copy).then_inc(vt_drained, 1)
            block_out(0)
            for h in range(HG):
                act.wait_ge(kt2_filled, h + 1)
                if h:
                    act.wait_ge(ds_filled, 10 * h)
                act.activation(ktil[:, 0:2, :], PS[:, 6, 0:2 * P].rearrange("p (a k) -> p a k", a=2), ACT.Copy)
                act.activation(ktil[0:NS, 2, :], PS[0:NS, 6, 2 * P:3 * P], ACT.Copy).then_inc(kt2_drained, 1)
                if h >= 2:
                    act.wait_ge(gate_done, h - 1)
                act.activation(sq[:, h % 2, :], raw[:, HGT + h, :], ACT.Sigmoid).then_inc(sig_done, 1)
                block_out(h + 1)
            for n in range(7, 10):
                block_out(n)
            act.wait_ge(blk_filled, 55)
            act.wait_ge(rows_in, 160)
            act.activation(ffz[:, :], PS[0:HF, 2, 0:T], ACT.Identity, bias=b_f[:, :]).then_inc(blk_drained, 1)

            def head_sqrt(n):
                src, w, g = NORMS[n]
                act.wait_ge(hn_sum, n + 1)
                if n >= 2:
                    act.wait_ge(hn_done, n - 1)
                act.activation(rs[:, n % 2, 0:w], PS[:, n % 2, 0:w], ACT.Sqrt, bias=eps_t[:, :], scale=1.0 / P).then_inc(hn_sqrt, 1)

            act.wait_ge(blk_drained, 55)
            act.wait_ge(gate_done, HG)
            act.wait_ge(o_added, HG)
            for n, (src, w, g) in enumerate(NORMS):
                if n >= 2:
                    act.wait_ge(hn_sum, n - 1)
                act.activation(sq[:, n % 2, 0:w], src, ACT.Square).then_inc(hn_sq, 1)
                if n:
                    head_sqrt(n - 1)
            head_sqrt(NN - 1)

            act.activation(ffw[:, :], ffz[:, :], ACT.Abs).then_inc(lf_act, 1)
            act.wait_ge(lf_act, 1)
            act.activation(ffw[:, :], ffw[:, :], ACT.Exp, scale=-1.0).then_inc(lf_act, 1)
            act.wait_ge(lf_act, 2)
            act.activation(ffw[:, :], ffw[:, :], ACT.Ln, bias=one_t[0:HF, :]).then_inc(lf_act, 1)

            act.wait_ge(stp_out, 16 * HG)
            for n in range(2):
                act.wait_ge(sts_out[n], 16 * HG // 2)
            for n, (dst, m, srcs) in enumerate(TOKF):
                act.wait_ge(tk_filled, n + 1)
                act.activation(dst, PS[0:m, 2 + n % 2, 0:len(srcs) * P], ACT.Copy).then_inc(tk_drained, 1)
            act.wait_ge(c_filled, 1)
            act.activation(negc[:, :], PS[0:HF, 5, 0:SEQ], ACT.Copy, scale=-1.0).then_inc(negc_set, 1)
            act.wait_ge(dec_filled, 1)
            act.activation(decay[:, :], PS[0:NB * HF, 0:3, :].rearrange("p a b -> p (a b)")[:, 0:KEYS], ACT.Copy).then_inc(decay_set, 1)

            for s in range(NU + 2):
                if s < NU:
                    act.wait_ge(pa_max, s + 1)
                    if s >= 2:
                        act.wait_ge(pa_t, s - 1)
                    act.activation(probs[:, s % 2, 0:width(s)], PS[:, s % 2, 0:width(s)], ACT.Exp, bias=nmax[:, s % 2:s % 2 + 1],
                                   accum_out=psum_p[:, s % 2:s % 2 + 1]).then_inc(pa_exp, 1)
                if s >= 2:
                    fox, h, qb = UNITS[s - 2]
                    act.wait_ge(pa_pv, s - 1)
                    act.activation(cat[:, h if fox else 12 + h, qb * P:(qb + 1) * P], PS[:, 4 + s % 2, 0:P], ACT.Copy).then_inc(pa_out, 1)

            def keys_out(b, u, first=False):
                for g in range(9):
                    bank = 2 * ((u + g) % 2)
                    if g == 0 and not first:
                        act.wait_ge(d_scored, b)
                    act.wait_ge(kt_filled, b * 9 + (g + 1))
                    src = PS[:, bank, :].rearrange("p (h t) -> p h t", t=P)
                    if g < NPG:
                        act.activation(keysT[:, 0:4, g * P:(g + 1) * P], src, ACT.Copy).then_inc(kt_act, 1)
                    else:
                        act.activation(mkeysT[:, 0:2, :], PS[:, bank, :].rearrange("p (h t) -> p h t", t=MEM), ACT.Copy).then_inc(kt_act, 1)

            def decode_exp(b, first=False):
                act.wait_ge(d_max, b + 1)
                if not first:
                    act.wait_ge(d_t, b)
                act.activation(dprob[0:24, :], PS[0:24, 4:7, :].rearrange("p a b -> p (a b)")[:, 0:KEYS], ACT.Exp, bias=nmax[0:24, 2:3],
                               accum_out=psum_p[0:24, 2:3])
                act.activation(mprob[0:16, :], PS[0:16, 6, 64:64 + MEM], ACT.Exp, bias=nmax[0:16, 3:4],
                               accum_out=psum_p[0:16, 3:4]).then_inc(d_exp, 1)

            def decode_out(b):
                act.wait_ge(d_pv, b + 1)
                act.activation(cat[:, 0:HF, ds(b * NL + SEQ, NL)], PS[:, 7, 256:280].rearrange("p (h q) -> p h q", q=NL), ACT.Copy)
                act.activation(cat[:, 12:16, ds(b * NL + SEQ, NL)], PS[:, 7, 280:296].rearrange("p (h q) -> p h q", q=NL), ACT.Copy).then_inc(d_out, 1)

            keys_out(0, 0, True)
            decode_exp(0, True)
            keys_out(1, 1)
            decode_out(0)
            with act.Fori(0, 3) as i:
                for u in range(2):
                    decode_exp(i * 2 + (u + 1))
                    keys_out(i * 2 + (u + 2), u)
                    decode_out(i * 2 + (u + 1))
            decode_exp(NB - 1)
            decode_out(NB - 1)

            for n in range(KC):
                act.wait_ge(wo_filled, n + 1)
                if n >= 2:
                    act.wait_ge(at_filled, n - 1)
                act.activation(attnT[:, n % 2, :], PS[:, n % 2, 0:T], ACT.Copy).then_inc(wo_drained, 1)
            act.wait_ge(h_added, 3 * KC)
            for t, (t0, n) in enumerate(TILES):
                if t:
                    act.wait_ge(h_ssq, t)
                act.activation(h_scaled[0:n, t, :], h_tok[0:n, t, :], ACT.Square, accum_out=ssq[0:n, 5 + t:6 + t]).then_inc(h_ssq, 1)
            act.wait_ge(h_ssq, 3)
            for t, (t0, n) in enumerate(TILES):
                act.activation(rstd[0:n, 5 + t:6 + t], ssq[0:n, 5 + t:6 + t], ACT.Sqrt, bias=eps_t[0:n, :], scale=1.0 / D).then_inc(h_sqrt, 1)
            for n, (o, i) in enumerate(((rw[:, :, 0:NG], rw[:, :, 0:NG]), (rw[:, :, 60:61], rw[:, :, 60:61]))):
                act.wait_ge(rt_sub, n + 1)
                act.activation(o, i, ACT.Exp).then_inc(rt_exp, 1)
            with act.Fori(0, NE) as e:
                act.wait_ge(gb_filled, e + 2)
                act.activation(gbc[:, :], PS[:, 6, 0:T], ACT.Copy).then_inc(gb_copied, 1)
                for j in range(FB):
                    act.wait_ge(mg_filled, e * 4 + (j + 1))
                    act.wait_ge(hs_done, e * 4 + (j + 1))
                    act.activation(hS[:, j % 2, :], PS[:, j % 2, 0:T], ACT.Silu).then_inc(silu_done, 1)

        @block.vector
        def _(dve):
            steps = [0]

            def step(ins):
                steps[0] += 1
                ins.then_inc(dve_step, 1)
                dve.wait_ge(dve_step, steps[0])

            dve.memset(ssq[:, :], 1.0).then_inc(ssq_clear, 1)
            dve.wait_ge(cols_filled, 1)
            dve.tensor_copy(cols[:, :], PS[:, 7, 0:65]).then_inc(cols_set, 1)
            dve.wait_ge(cols_set, 1)
            dve.tensor_scalar(gq[:, 0:1], g_fq, SCALE, None, ALU.mult).then_inc(gains_set, 1)
            dve.tensor_scalar(gq[:, 2:3], g_mq, SCALE, None, ALU.mult).then_inc(gains_set, 1)
            dve.tensor_copy(gq[:, 1:2], g_fk).then_inc(gains_set, 1)
            dve.tensor_copy(gq[:, 3:4], g_mk).then_inc(gains_set, 1)

            dve.tensor_copy(gq[:, 4:5], g_hn).then_inc(gains_set, 1)
            step(dve.tensor_tensor(lbw[:, 2, :], lb0, lb1, ALU.max))
            dve.tensor_tensor(lbw[:, 0, :], lb0, lbw[:, 2, :], ALU.subtract)
            dve.tensor_tensor(lbw[:, 1, :], lb1, lbw[:, 2, :], ALU.subtract).then_inc(lb_diff, 1)

            def drain(f):
                n, c, m = FILLS[f]
                w = NORM[n][1]
                dst, g = (memT, G_MEM) if n < 2 else (xT, G_ATT)
                t0 = (n if n < 2 else n - 2) * P
                dve.wait_ge(tT_filled, f + 1)
                dve.tensor_tensor(dst[:, c:c + m, t0:t0 + w], fill_out(f, w),
                                  g[:, c:c + m].rearrange("p (c a) -> p c a", a=1).to_broadcast([P, m, w]),
                                  ALU.mult).then_inc(tT_drained, 1)

            for n, (src, m, c) in enumerate(NORM):
                dve.wait_ge(sqrt_done, n + 1)
                step(dve.reciprocal(rstd[0:m, c:c + 1], rstd[0:m, c:c + 1]))
                dve.tensor_scalar(src[0:m], src[0:m], rstd[0:m, c:c + 1], None, ALU.mult).then_inc(scaled, 1)
                if n:
                    for f in range(4 * n - 4, 4 * n):
                        drain(f)
            drain(16)

            dve.wait_ge(lfp_filled, 1)
            dve.tensor_copy(lfp[:, :, :, :].rearrange("p g b h -> p h b g"),
                            PS[:, 6, 0:HF * 64].rearrange("p (h b g) -> p h b g", h=HF, b=NB)).then_inc(lfp_drained, 1)
            dve.wait_ge(lfp_drained, 1)
            step(dve.memset(lfs[:, NPG - 1, :, :], 0.0))
            for g in range(NPG - 2, -1, -1):
                step(dve.tensor_tensor(lfs[:, g, :, :], lfs[:, g + 1, :, :], lfp[:, g + 1, :, :], ALU.add))
            dve.wait_ge(lb_exp, 1)
            step(dve.tensor_tensor(lbw[:, 0, :], lbw[:, 2, :], lbw[:, 3, :], ALU.add))
            step(dve.reciprocal(lbw[:, 1, :], lbw[:, 0, :]))
            dve.tensor_tensor(LB, lbw[:, 2, :], lbw[:, 1, :], ALU.mult).then_inc(lb_set, 1)
            dve.tensor_tensor(LB1, lbw[:, 3, :], lbw[:, 1, :], ALU.mult).then_inc(lb_set, 1)
            for n in range(2):
                dve.tensor_reduce(parity[:, n:n + 1], chunk_of[:, :].rearrange("p (a b) -> p b a", b=2)[:, n, :], AX.X, ALU.add)
            dve.memset(nmax[:, :], 0.0).then_inc(parity_set, 1)
            dve.memset(psum_p[:, 0:1], 0.0).then_inc(hg_done, 1)
            dve.memset(psum_p[:, 1:2], 0.0).then_inc(intra_used, 1)
            dve.wait_ge(lb_set, 2)

            def pr(a):
                return a[:, :, 0:SEQ].rearrange("p h (n t) -> p h n t", t=CH)

            def sa(a):
                return a[:, :, SEQ:T].rearrange("p h (n t) -> p h n t", t=NL)

            def packed(buf, j):
                return buf.rearrange("p h t -> p (h t)")[:, 0:2 * NCH * (CH - j)].rearrange("p (h n t) -> p h n t", h=2, n=NCH)

            S_OFF = [0, 64, 112, 144]

            def spacked(a, j):
                return a[:, S_OFF[j]:S_OFF[j] + 16 * (NL - j)].rearrange("p (h n t) -> p h n t", h=2, n=NB)

            with dve.Fori(0, 3) as g:
                n_step = 0

                def gstep(ins):
                    nonlocal n_step
                    n_step += 1
                    ins.then_inc(hg_step, 1)
                    dve.wait_ge(hg_step, g * G_STEPS + n_step)

                hg = ds(g * 2, 2)
                lb1b = lbw[:, 5, hg].rearrange("p (h a) -> p h a", a=1).to_broadcast([P, 2, T])
                lbb = lbw[:, 4, hg].rearrange("p (h a) -> p h a", a=1).to_broadcast([P, 2, T])
                dve.wait_ge(hg_prep, g + 1)
                dve.scalar_tensor_tensor(out=gQ, in0=raw[:, ds(g * 2 + HQ, 2), :], scalar=SCALE, in1=gQ, op0=ALU.mult, op1=ALU.mult)
                dve.tensor_tensor(gW[0], gW[0], lb1b, ALU.mult)
                gstep(dve.tensor_tensor(gF, gF, lb1b, ALU.mult))
                gstep(dve.tensor_tensor(gF, gF, lbb, ALU.add))

                def add_distance(j):
                    dve.wait_ge(intra_filled, g * 17 + (j + 1))
                    o = gO if j == 0 else gTmp
                    dve.tensor_tensor(pr(o)[:, :, :, j:CH], packed(PS[:, 6 + j % 2, :].rearrange("p (h t) -> p h t", h=2), j),
                                      pr(gV)[:, :, :, 0:CH - j], ALU.mult).then_inc(intra_used, 1)
                    dve.wait_ge(intra_used, g * 17 + (j + 2))
                    if j:
                        gstep(dve.tensor_tensor(pr(gO)[:, :, :, j:CH], pr(gO)[:, :, :, j:CH], pr(gTmp)[:, :, :, j:CH], ALU.add))

                for j in range(CH):
                    w, w0 = gW[j % 2], gW[(j + 1) % 2]
                    if j:
                        if j < NL:
                            dve.tensor_tensor(sa(w)[:, :, :, j:NL], sa(gF)[:, :, :, j:NL], sa(w0)[:, :, :, j - 1:NL - 1], ALU.mult)
                        gstep(dve.tensor_tensor(pr(w)[:, :, :, j:CH], pr(gF)[:, :, :, j:CH], pr(w0)[:, :, :, j - 1:CH - 1], ALU.mult))
                    dve.tensor_copy(pr(gKT)[:, :, :, CH - 1 - j:CH - j], pr(w)[:, :, :, CH - 1:CH])
                    if j < NL:
                        dve.tensor_copy(sa(gKT)[:, :, :, NL - 1 - j:NL - j], sa(w)[:, :, :, NL - 1:NL])
                        dve.tensor_tensor(spacked(gS, j), sa(gQ)[:, :, :, j:NL], sa(w)[:, :, :, j:NL], ALU.mult)
                    if j >= 2:
                        dve.wait_ge(intra_filled, g * 17 + (j - 1))
                    dve.tensor_tensor(packed(gQW[j % 2], j), pr(gQ)[:, :, :, j:CH], pr(w)[:, :, :, j:CH], ALU.mult).then_inc(qw_ready, 1)
                    if j:
                        add_distance(j - 1)
                add_distance(CH - 1)
                dve.wait_ge(intra_filled, g * 17 + 17)
                for j in range(NL):
                    o = gO if j == 0 else gTmp
                    ins = dve.tensor_tensor(sa(o)[:, :, :, j:NL], spacked(PS[:, 6, :], j), sa(gV)[:, :, :, 0:NL - j], ALU.mult)
                    if j == NL - 1:
                        ins.then_inc(intra_used, 1)
                        dve.wait_ge(intra_used, g * 17 + 18)
                    else:
                        gstep(ins)
                    if j:
                        gstep(dve.tensor_tensor(sa(gO)[:, :, :, j:NL], sa(gO)[:, :, :, j:NL], sa(gTmp)[:, :, :, j:NL], ALU.add))
                keep, start = gW
                gstep(dve.tensor_copy(keep, gF))
                gstep(dve.memset(start, 0.0))
                for v in (pr, sa):
                    dve.memset(v(keep)[:, :, :, 0:1], 0.0)
                    ins = dve.tensor_copy(v(start)[:, :, :, 0:1], v(gF)[:, :, :, 0:1])
                gstep(ins)
                flat = [a.rearrange("p h t -> p (h t)") for a in (gTmp, keep, start)]
                gstep(dve.tensor_tensor_scan(flat[0], flat[1], flat[2], 0.0, ALU.mult, ALU.add))
                dve.tensor_tensor(raw[:, ds(g * 2 + HQ, 2), :], gQ, gTmp, ALU.mult)
                dve.tensor_copy(decays[:, hg, 0:NCH], pr(gTmp)[:, :, :, CH - 1])
                dve.tensor_copy(decays[:, hg, NCH:NCH + NB], sa(gTmp)[:, :, :, NL - 1])
                dve.tensor_copy(raw[:, ds(g * 2 + HFG, 2), :], gKT)
                dve.tensor_copy(cat[:, ds(g * 2 + 6, 2), :], gO).then_inc(hg_done, 1)
                assert n_step == G_STEPS, n_step

            dve.wait_ge(hg_done, 4)
            n_st = 0

            def ststep(ins):
                nonlocal n_st
                n_st += 1
                ins.then_inc(st_step, 1)
                dve.wait_ge(st_step, n_st)

            def add_inter(h):
                dve.wait_ge(oi_filled, h + 1)
                o = cat[:, 6 + h, CH:T]
                dve.tensor_tensor(o, o, PS[:, 7, CH:T], ALU.add).then_inc(o_added, 1)

            for h in range(HG):
                if h:
                    add_inter(h - 1)
                for c in range(8):
                    dve.wait_ge(ds_filled, 10 * h + c + 1)
                    if c == 7 and h:
                        dve.wait_ge(stp_out, 16 * h)
                    for n in (2 * c, 2 * c + 1):
                        d = PS[:, 4 + c % 2, (n % 2) * P:(n % 2 + 1) * P]
                        if n == 0:
                            ins = dve.tensor_copy(states[:, 0, :], d)
                        else:
                            ins = dve.scalar_tensor_tensor(out=states[:, n, :], in0=states[:, n - 1, :], scalar=decays[:, h, n:n + 1],
                                                           in1=d, op0=ALU.mult, op1=ALU.add)
                        if n % 2 == 0:
                            ststep(ins)
                        else:
                            ins.then_inc(ds_used, 1)
                            dve.wait_ge(ds_used, 10 * h + c + 1)
                dve.wait_ge(os_filled, h + 1)
                for c in range(2):
                    sn = s_in[h % 2][:, 4 * c:4 * c + 4, :]
                    ststep(dve.tensor_tensor(sn, sn, decays[:, h, NCH + 4 * c:NCH + 4 * c + 4].rearrange("p (b a) -> p b a", a=1)
                                             .to_broadcast([P, 4, P]), ALU.mult))
                    dve.wait_ge(ds_filled, 10 * h + 9 + c)
                    dve.tensor_tensor(sn, sn, PS[:, 4 + c % 2, :].rearrange("p (b v) -> p b v", b=4), ALU.add).then_inc(ds_used, 1)
                dve.wait_ge(sig_done, h + 1)
                dve.tensor_tensor(raw[:, HGT + h, :], raw[:, HGT + h, :], sq[:, h % 2, :], ALU.mult).then_inc(gate_done, 1)
            add_inter(HG - 1)
            dve.memset(psum_p[:, :], 0.0).then_inc(lfs_done, 1)

            dve.wait_ge(gains_set, 5)
            for n, (src, w, g) in enumerate(NORMS):
                dve.wait_ge(hn_sqrt, n + 1)
                dve.reciprocal(rs[:, n % 2, 0:w], rs[:, n % 2, 0:w]).then_inc(hn_rcp, 1)
                dve.wait_ge(hn_rcp, n + 1)
                dve.scalar_tensor_tensor(out=src, in0=src, scalar=gq[:, g:g + 1], in1=rs[:, n % 2, 0:w],
                                         op0=ALU.mult, op1=ALU.mult).then_inc(hn_done, 1)
                if n >= NN - HG:
                    dve.wait_ge(hn_done, n + 1)
                    h = n - (NN - HG)
                    step(dve.tensor_tensor(cat[:, 6 + h, :], cat[:, 6 + h, :], raw[:, HGT + h, :], ALU.mult))

            dve.wait_ge(lf_act, 3)
            dve.scalar_tensor_tensor(out=lfT[:, :], in0=ffz[:, :], scalar=0.0, in1=ffw[:, :],
                                     op0=ALU.min, op1=ALU.subtract).then_inc(lf_done, 1)
            dve.wait_ge(lft_filled, 1)
            step(dve.tensor_copy(lftok[:, 0:2, :], PS[:, 4, 0:2 * HF].rearrange("p (t h) -> p t h", h=HF)))
            dve.tensor_copy(lftok[0:NS, 2, :], PS[0:NS, 4, 2 * HF:3 * HF]).then_inc(lft_drained, 1)
            dve.wait_ge(lft_drained, 1)
            dve.tensor_tensor(lfm[:, :, :], lftok[0:NS, 2:3, :].to_broadcast([NS, NB, HF]),
                              batch_of[:, :].rearrange("p (b a) -> p b a", a=1).to_broadcast([NS, NB, HF]),
                              ALU.mult).then_inc(lfm_done, 1)

            for s in range(NU + 2):
                if 1 <= s <= NU:
                    u = s - 1
                    dve.wait_ge(pa_exp, u + 1)
                    step(dve.reciprocal(psum_p[:, u % 2:u % 2 + 1], psum_p[:, u % 2:u % 2 + 1]))
                    dve.tensor_scalar(probs[:, u % 2, 0:width(u)], probs[:, u % 2, 0:width(u)], psum_p[:, u % 2:u % 2 + 1], None,
                                      ALU.mult).then_inc(pa_prob, 1)
                if s >= 2:
                    u = s - 2
                    dve.wait_ge(pa_t, u + 1)
                    if u >= 2:
                        dve.wait_ge(pa_pv, u - 1)
                    dve.tensor_copy(probsT[:, u % 2, 0:width(u) // P, :],
                                    PS[:, 2 + u % 2, 0:width(u)].rearrange("p (a q) -> p a q", q=P)).then_inc(pa_tc, 1)
                if s < NU:
                    dve.wait_ge(pa_scored, s + 1)
                    if s >= 2:
                        dve.wait_ge(pa_exp, s - 1)
                    dve.tensor_reduce(nmax[:, s % 2:s % 2 + 1], PS[:, s % 2, 0:width(s)], AX.X, ALU.max, negate=True).then_inc(pa_max, 1)

            dve.memset(q_rows[:, :], 0.0).then_inc(q_clear, 1)
            dve.memset(mq_rows[:, :], 0.0).then_inc(q_clear, 1)
            dve.wait_ge(q_clear, 2)

            def queries(b, first=False):
                if not first:
                    dve.wait_ge(d_scored, b)
                q = ds(b * NL + SEQ, NL)
                dve.tensor_copy(q_rows[:, :].rearrange("p (h c) -> p h c", c=28)[:, :, 0:NL], raw[:, FQ:FQ + HF, q])
                dve.tensor_copy(mq_rows[:, :].rearrange("p (h c) -> p h c", c=20)[:, :, 0:NL], raw[:, MQ:MQ + HM, q])
                dve.tensor_copy(causal_b.rearrange("p (a k) -> p a k", a=1), causal4[:, ds(b, 1), :])
                dve.tensor_copy(sel_b[:, :].rearrange("p (a h q) -> p a h q", a=1, q=NL), sel48[:, ds(b, 1), :, :]).then_inc(q_set, 1)

            def keys_out(b, u, gs):
                for g in gs:
                    bank = 2 * ((u + g) % 2) + 1
                    dve.wait_ge(kt_filled, b * 9 + (g + 1))
                    if g < NPG:
                        dve.tensor_copy(keysT[:, 4:6, g * P:(g + 1) * P],
                                        PS[:, bank, 0:2 * P].rearrange("p (h t) -> p h t", t=P)).then_inc(kt_dve, 1)
                    else:
                        dve.tensor_copy(mkeysT[:, 2:4, :], PS[:, bank, :].rearrange("p (h t) -> p h t", t=MEM)).then_inc(kt_dve, 1)

            def decode_max(b):
                dve.wait_ge(d_scored, b + 1)
                dve.tensor_reduce(nmax[0:24, 2:3], PS[0:24, 4:7, :].rearrange("p a b -> p (a b)")[:, 0:KEYS], AX.X, ALU.max, negate=True)
                dve.tensor_reduce(nmax[0:16, 3:4], PS[0:16, 6, 64:64 + MEM], AX.X, ALU.max, negate=True).then_inc(d_max, 1)

            def decode_norm(b):
                dve.wait_ge(d_exp, b + 1)
                dve.reciprocal(psum_p[0:24, 2:3], psum_p[0:24, 2:3])
                dve.reciprocal(psum_p[0:16, 3:4], psum_p[0:16, 3:4]).then_inc(d_rcp, 1)
                dve.wait_ge(d_rcp, b + 1)
                dve.tensor_scalar(dprob[0:24, :], dprob[0:24, :], psum_p[0:24, 2:3], None, ALU.mult)
                dve.tensor_scalar(mprob[0:16, :], mprob[0:16, :], psum_p[0:16, 3:4], None, ALU.mult).then_inc(d_prob, 1)

            def probs_out(b, first=False):
                dve.wait_ge(d_t, b + 1)
                if not first:
                    dve.wait_ge(d_pv, b)
                dve.tensor_copy(dprobT[:, 0:224], PS[:, 7, 0:224])
                dve.tensor_copy(npT, PS[0:NS, 7, 224:248]).then_inc(d_tc, 1)

            queries(0, True)
            keys_out(0, 0, range(9))
            decode_max(0)
            queries(1)
            keys_out(1, 1, range(2))
            decode_norm(0)
            keys_out(1, 1, range(2, 9))
            probs_out(0, True)
            with dve.Fori(0, 3) as i:
                for u in range(2):
                    decode_max(i * 2 + (u + 1))
                    queries(i * 2 + (u + 2))
                    keys_out(i * 2 + (u + 2), u, range(2))
                    decode_norm(i * 2 + (u + 1))
                    keys_out(i * 2 + (u + 2), u, range(2, 9))
                    probs_out(i * 2 + (u + 1))
            decode_max(NB - 1)
            decode_norm(NB - 1)
            probs_out(NB - 1)

            dve.wait_ge(x_again, 48)
            for n in range(KC):
                for t, (t0, w) in enumerate(TILES):
                    dve.wait_ge(at_filled, n + 1)
                    o = h_tok[0:w, t, n * P:(n + 1) * P]
                    dve.tensor_tensor(o, o, PS[0:w, 2 + n % 2, t * P:(t + 1) * P], ALU.add).then_inc(h_added, 1)
            dve.wait_ge(h_added, 3 * KC)
            for t, (t0, w) in enumerate(TILES):
                dve.wait_ge(h_sqrt, t + 1)
                step(dve.reciprocal(rstd[0:w, 5 + t:6 + t], rstd[0:w, 5 + t:6 + t]))
                dve.tensor_scalar(h_scaled[0:w, t, :], h_tok[0:w, t, :], rstd[0:w, 5 + t:6 + t], None, ALU.mult).then_inc(h_scl, 1)
                for f in range(HT_FILLS):
                    ft, c, m = HTF[f]
                    if ft == t:
                        dve.wait_ge(ht_filled, f + 1)
                        dve.tensor_tensor(xnT[:, c:c + m, t0:t0 + w], ht_out(f),
                                          G_FFN[:, c:c + m].rearrange("p (c a) -> p c a", a=1).to_broadcast([P, m, w]),
                                          ALU.mult).then_inc(ht_drained, 1)

            step(dve.memset(logits[:, :, :], 0.0))
            dve.memset(gates[:, :, :], 0.0)
            dve.wait_ge(lg_filled, 3)
            for t, (t0, w) in enumerate(TILES):
                ins = dve.tensor_copy(logits[0:w, t, :], PS[0:w, 4, t * 64:t * 64 + NG + NE])
            step(ins)
            gl = logits[:, :, 0:NG]
            el = logits[:, :, NG:NG + NE].rearrange("p t (g e) -> p t g e", g=NG)

            def bc(a, n):
                return a.to_broadcast([P, 3, n])

            first = rw[:, :, 40:48]
            for n in range(EPG):
                ins = dve.memset(first[:, :, n:n + 1], float(EPG - n))
            step(ins)

            def one_hot(out, x, m, tmp):
                n = x.shape[2]
                step(dve.tensor_reduce(m, x, AX.X, ALU.max))
                step(dve.tensor_tensor(out, x, bc(m, n), ALU.is_equal))
                step(dve.tensor_tensor(out, out, first[:, :, 0:n], ALU.mult))
                step(dve.tensor_reduce(tmp, out, AX.X, ALU.max))
                step(dve.tensor_tensor(out, out, bc(tmp, n), ALU.is_equal))

            gm, g1, e_in, m1, o1, m2, o2, tmp = (rw[:, :, a:b] for a, b in
                                                 ((48, 49), (4, 8), (8, 16), (49, 50), (16, 24), (50, 51), (24, 32), (51, 52)))
            ge, e2, dd, ga, gb, gsum = (rw[:, :, a:b] for a, b in ((0, 4), (32, 40), (60, 61), (61, 62), (62, 63), (52, 53)))
            one_hot(g1, gl, gm, tmp)
            dve.tensor_tensor(ge, gl, bc(gm, NG), ALU.subtract).then_inc(rt_sub, 1)
            picked = choice[:, :, 0, :].rearrange("p t (g e) -> p t g e", g=NG)
            step(dve.tensor_tensor(picked, el, g1.rearrange("p t (g a) -> p t g a", a=1).to_broadcast([P, 3, NG, EPG]), ALU.mult))
            step(dve.tensor_reduce(e_in, picked.rearrange("p t g e -> p t e g"), AX.X, ALU.add))
            one_hot(o1, e_in, m1, tmp)
            step(dve.scalar_tensor_tensor(out=e2, in0=o1, scalar=NEG, in1=e_in, op0=ALU.mult, op1=ALU.add))
            one_hot(o2, e2, m2, tmp)
            dve.tensor_tensor(dd, m2, m1, ALU.subtract).then_inc(rt_sub, 1)
            dve.wait_ge(rt_exp, 2)
            step(dve.tensor_reduce(gsum, ge, AX.X, ALU.add))
            step(dve.tensor_scalar(ga, dd, 1.0, None, ALU.add))
            step(dve.tensor_tensor(ga, ga, gsum, ALU.mult))
            step(dve.reciprocal(ga, ga))
            step(dve.tensor_tensor(gb, ga, dd, ALU.mult))
            for n, o in enumerate((o1, o2)):
                c = choice[:, :, n, :].rearrange("p t (g e) -> p t g e", g=NG)
                for g in range(NG):
                    ins = dve.tensor_tensor(c[:, :, g, :], o, bc(g1[:, :, g:g + 1], EPG), ALU.mult)
            step(ins)
            step(dve.tensor_tensor(c1g, choice[:, :, 0, :], bc(ga, NE), ALU.mult))
            step(dve.tensor_tensor(rw[:, :, 0:NE], choice[:, :, 1, :], bc(gb, NE), ALU.mult))
            for t, (t0, w) in enumerate(TILES):
                ins = dve.tensor_tensor(gates[0:w, t, :], c1g[0:w, t, :], rw[0:w, t, 0:NE], ALU.add)
            ins.then_inc(gates_set, 1)
            dve.wait_ge(gates_set, 1)
            dve.wait_ge(lg_filled, 3)
            dve.memset(yT, 0.0).then_inc(y_clear, 1)
            dve.wait_ge(y_clear, 1)
            for n, s in enumerate((gb_filled, silu_done, hs_done, md_filled, y_added)):
                dve.memset(rw[:, :, n:n + 1], 0.0).then_inc(s, 1)

            with dve.Fori(0, NE) as e:
                dve.wait_ge(gb_filled, e + 1)
                dve.tensor_copy(gcol[:, :, :], gates[:, :, ds(e, 1)].to_broadcast([P, 3, P])).then_inc(gcol_set, 1)
                dve.wait_ge(gb_copied, e + 1)
                for j in range(FB):
                    dve.wait_ge(mu_filled, e * 4 + (j + 1))
                    dve.wait_ge(silu_done, e * 4 + (j + 2))
                    dve.tensor_tensor(hS[:, j % 2, :], hS[:, j % 2, :], PS[:, 2 + j % 2, 0:T], ALU.mult).then_inc(hs_done, 1)
                    dve.wait_ge(hs_done, e * 4 + (j + 2))
                    dve.wait_ge(md_filled, e * 16 + 1)
                    dve.tensor_tensor(hT[:, j, :], hS[:, j % 2, :], gbc[:, :], ALU.mult).then_inc(hT_done, 1)
                for n in range(KC):
                    dve.wait_ge(md_filled, e * 16 + (n + 2))
                    dve.tensor_tensor(yT[:, n, :], yT[:, n, :], PS[:, 4 + n % 2, 0:T], ALU.add).then_inc(y_added, 1)
            for t, (t0, w) in enumerate(TILES):
                for c in range(4):
                    f = 4 * t + c
                    dve.wait_ge(yt_filled, f + 1)
                    o = h_tok[0:w, t, c * 512:(c + 1) * 512]
                    dve.tensor_tensor(o, o, PS[0:w, f % 2, :], ALU.add).then_inc(y_done, 1)

        @block.tensor
        def _(pe):
            pe.wait_ge(consts_set, N_CONSTS)
            pe.wait_ge(rows_in, 160)
            pe.transpose(PS[:, 7, 0:65], rows[:, :], ident[0:65, 0:65]).then_inc(cols_filled, 1)
            pe.wait_ge(cols_set, 1)
            for f, (n, c, m) in enumerate(FILLS):
                src, w, _ = NORM[n]
                pe.wait_ge(scaled, n + 1)
                if f >= 8:
                    pe.wait_ge(tT_drained, f - 7)
                for a in range(m):
                    last = pe.transpose(fill_out(f, w)[:, a, :], src[0:w, (c + a) * P:(c + a + 1) * P], ident[0:w, 0:w])
                last.then_inc(tT_filled, 1)

            def project(bank, w, rhs, wt, c, m=P, between=None):
                for k in range(KC):
                    last = pe.matmul(PS[0:m, bank, 0:w], wt[:, k, c:c + m], rhs[:, k, :], start=(k == 0), stop=(k == KC - 1))
                    if between is not None and k < KC - 1:
                        between(k)
                last.then_inc(blk_filled, 1)

            pe.wait_ge(tT_drained, 17)
            pe.wait_ge(lfpages_in, 16)
            pages_h = lfpages.rearrange("g (t h) -> g h t", h=HF)
            for h in range(HF):
                last = pe.transpose(PS[:, 6, h * 64:(h + 1) * 64], pages_h[:, h, :], ident[0:64, 0:64])
            last.then_inc(lfp_filled, 1)

            pe.wait_ge(lfp_drained, 1)
            for j in range(8):
                if j % 3 == 0:
                    pe.wait_ge(w_in_slot[(j // 3) % 2], 16 * (1 + j // 6))
                project(j, MEM, memT, wslot[(j // 3) % 2], (j % 3) * P)
            pe.wait_ge(blk_drained, 8)
            with pe.Fori(0, 3) as i:
                for half in (1, 0):
                    pe.wait_ge(w_in_slot[half], i * 16 + (48 - 16 * half))
                    for n in range(3):
                        pe.wait_ge(blk_drained, i * 6 + (ORDER.index(3 * half + n) + 3))
                        project(3 * half + n, T, xT, wslot[half], n * P)

            def intra(g, j):
                pe.wait_ge(qw_ready, g * CH + min(j + 1, CH))
                pe.wait_ge(intra_used, g * 17 + max(j, 1))
                rhs = gQW[j % 2].rearrange("p h t -> p (h t)")[:, 0:2 * NCH * (CH - j)] if j < CH else gS
                pe.matmul(PS[:, 6 + j % 2, 0:rhs.shape[1]], ones[:, :], rhs, start=True, stop=True).then_inc(intra_filled, 1)

            with pe.Fori(0, 3) as g:
                for half in (1, 0):
                    pe.wait_ge(w_in_slot[half], g * 16 + (48 + 48 - 16 * half))
                    for n in range(3):
                        b = ORDER.index(3 * half + n)
                        pe.wait_ge(blk_drained, g * 6 + (18 + b + 3))

                        def between(k, b=b):
                            at = {3: 0, 7: 1, 11: 2, 13: 3}.get(k)
                            if b and at is not None and (at < 3 or b >= 4):
                                intra(g, 3 * (b - 1) + max(b - 4, 0) + at)

                        project(3 * half + n, T, xT, wslot[half], n * P, between=between)

            def values_by_token(f):
                t, c, m = f // 2, (f % 2) * 4, 4 - 2 * (f % 2)
                t0, w = TILES[t]
                if f >= 2:
                    pe.wait_ge(vt_drained, f - 1)
                for a in range(m):
                    last = pe.transpose(PS[0:w, 6 + f % 2, a * P:(a + 1) * P], raw[:, HI + c + a, t0:t0 + w], ident[:, :])
                last.then_inc(vt_filled, 1)

            def keys_by_token(h):
                if h:
                    pe.wait_ge(kt2_drained, h)
                else:
                    pe.wait_ge(vt_drained, 6)
                for t, (t0, w) in enumerate(TILES):
                    last = pe.transpose(PS[0:w, 6, t * P:(t + 1) * P], raw[:, HFG + h, t0:t0 + w], ident[:, :])
                last.then_inc(kt2_filled, 1)

            def state_parts(h, c):
                q = 10 * h + c
                if q >= 2:
                    pe.wait_ge(ds_used, q - 1)
                if c == 0:
                    pe.wait_ge(kt2_drained, h + 1)
                if c < 8:
                    t, r = c // 4, 32 * (c % 4)
                    last = pe.matmul(PS[:, 4 + q % 2, 0:2 * P].rearrange("p (a v) -> p a v", a=2), ktil[r:r + 32, t, :],
                                     vpar[r:r + 32, :, t, h * P:(h + 1) * P], start=True, stop=True)
                else:
                    pe.wait_ge(sm_set, 2 * h + c - 7)
                    last = pe.matmul(PS[:, 4 + q % 2, :], ktil[0:NS, 2, :], vmask[c - 8].rearrange("p b v -> p (b v)"),
                                     start=True, stop=True)
                last.then_inc(ds_filled, 1)

            def inter_sample(h):
                pe.wait_ge(s_loaded[h % 2], 16 * (h // 2 + 1))
                if h:
                    pe.wait_ge(o_added, h)
                for b in range(NB):
                    c = SEQ + b * NL
                    last = pe.matmul(PS[:, 7, c:c + NL], s_in[h % 2][:, b, :], raw[:, HQ + h, c:c + NL], start=True, stop=True)
                last.then_inc(os_filled, 1)

            def inter_prompt(h):
                pe.wait_ge(ds_used, 10 * h + 8)
                for n in range(1, NCH):
                    last = pe.matmul(PS[:, 7, n * CH:(n + 1) * CH], states[:, n - 1, :], raw[:, HQ + h, n * CH:(n + 1) * CH],
                                     start=True, stop=True)
                last.then_inc(oi_filled, 1)

            def last_block(n):
                def between(k):
                    if n == 0 and 2 <= k < 14 and k % 2 == 0:
                        if k == 2:
                            pe.wait_ge(hg_done, 4)
                        values_by_token(k // 2 - 1)
                    h = n - 1
                    if 0 < h <= HG and k == 0:
                        inter_prompt(h - 1)
                    if 0 <= h < HG:
                        if k == 2:
                            keys_by_token(h)
                        if 4 <= k < 14:
                            state_parts(h, k - 4)
                        if k == 8:
                            inter_sample(h)
                if n < 4:
                    pe.wait_ge(blk_drained, 44)
                else:
                    pe.wait_ge(blk_drained, 44 + n - 3)
                if n in (0, 3):
                    pe.wait_ge(w_in_slot[1 - n // 3], 96 + 48 - 16 * (1 - n // 3))
                    slot = 1 - n // 3
                if n in (6, 8):
                    slot = (8 - n) // 2
                    pe.wait_ge(w_in_slot[slot], 144 + 16 * (1 - slot))
                slot, c = [(1, n), (0, n - 3), (1, n - 6), (0, n - 8)][(n >= 3) + (n >= 6) + (n >= 8)]
                project(n % 4, T, xT, wslot[slot], c * P, between=between)

            for n in range(10):
                last_block(n)
            pe.wait_ge(wff_in, 16)
            pe.wait_ge(blk_drained, 51)
            project(2, T, xT, w_ff, 0, HF)

            for n, (src, w, g) in enumerate(NORMS):
                pe.wait_ge(hn_sq, n + 1)
                if n >= 2:
                    pe.wait_ge(hn_sqrt, n - 1)
                pe.matmul(PS[:, n % 2, 0:w], ones[:, :], sq[:, n % 2, 0:w], start=True, stop=True).then_inc(hn_sum, 1)

            pe.wait_ge(lf_done, 1)
            for t, (t0, n) in enumerate(TILES):
                last = pe.transpose(PS[0:n, 4, t * HF:(t + 1) * HF], lfT[:, t0:t0 + n], ident[0:HF, 0:HF])
            last.then_inc(lft_filled, 1)
            pe.wait_ge(hn_done, NN)
            for n, (dst, m, srcs) in enumerate(TOKF):
                if n >= 2:
                    pe.wait_ge(tk_drained, n - 1)
                for a, s in enumerate(srcs):
                    last = pe.transpose(PS[0:m, 2 + n % 2, a * P:(a + 1) * P], s, ident[:, :])
                last.then_inc(tk_filled, 1)
            pe.wait_ge(lft_drained, 1)
            pe.matmul(PS[0:HF, 5, 0:P], lftok[:, 0, :], tri_le[:, :], start=True, stop=True)
            pe.matmul(PS[0:HF, 5, P:SEQ], lftok[:, 0, :], ones[:, :], start=True, stop=False)
            pe.matmul(PS[0:HF, 5, P:SEQ], lftok[:, 1, :], tri_le[:, :], start=False, stop=True).then_inc(c_filled, 1)
            pe.wait_ge(lfs_done, 1)
            pe.wait_ge(lfm_done, 1)
            pe.wait_ge(tk_drained, NTF)
            new = lfm[:, :, :].rearrange("p b h -> p (b h)")
            for g in range(NPG):
                o = PS[0:NB * HF, g // 4, (g % 4) * P:(g % 4 + 1) * P]
                pe.matmul(o, lfp[:, g, :, :].rearrange("p b h -> p (b h)"), tri_gt[:, :], start=True, stop=False)
                pe.matmul(o, lfs[:, g, :, :].rearrange("p b h -> p (b h)"), ones[:, :], start=False, stop=False)
                pe.matmul(o, new, ones[0:NS, :], start=False, stop=True)
            pe.matmul(PS[0:NB * HF, 2, 0:NS], new, tri_gt[0:NS, 0:NS], start=True, stop=True).then_inc(dec_filled, 1)

            pe.wait_ge(decay_set, 1)
            pe.wait_ge(negc_set, 1)
            for s in range(NU + 2):
                if s < NU:
                    fox, h, qb = UNITS[s]
                    if s >= 2:
                        pe.wait_ge(pa_exp, s - 1)
                    o = PS[:, s % 2, 0:width(s)]
                    q = raw[:, (FQ if fox else MQ) + h, qb * P:(qb + 1) * P]
                    k = raw[:, FK + h, 0:width(s)] if fox else mraw[:, h, :]
                    last = pe.matmul(o, q, k, start=True, stop=not fox)
                    if fox:
                        pe.matmul(o, head_row[:, h, :], negc[:, 0:width(s)], start=False, stop=False)
                        last = pe.matmul(PS[:, s % 2, qb * P:(qb + 1) * P], ident[:, :], causal[:, :], start=False, stop=True)
                    last.then_inc(pa_scored, 1)
                if 1 <= s <= NU:
                    u = s - 1
                    pe.wait_ge(pa_prob, u + 1)
                    if u >= 2:
                        pe.wait_ge(pa_tc, u - 1)
                    for a in range(width(u) // P):
                        last = pe.transpose(PS[:, 2 + u % 2, a * P:(a + 1) * P], probs[:, u % 2, a * P:(a + 1) * P], ident[:, :])
                    last.then_inc(pa_t, 1)
                if s >= 2:
                    u = s - 2
                    fox, h, qb = UNITS[u]
                    pe.wait_ge(pa_tc, u + 1)
                    if u >= 2:
                        pe.wait_ge(pa_out, u - 1)
                    na = width(u) // P
                    for a in range(na):
                        v = vtok[:, a, h * P:(h + 1) * P] if fox else mtok[:, a, MW + h * P:MW + (h + 1) * P]
                        last = pe.matmul(PS[:, 4 + u % 2, 0:P], v, probsT[:, u % 2, a, :], start=(a == 0), stop=(a == na - 1))
                    last.then_inc(pa_pv, 1)

            pe.wait_ge(pa_out, NU)

            def keys_in(b, u, first=False):
                for g in range(9):
                    bank = 2 * ((u + g) % 2)
                    if g < NPG:
                        pe.wait_ge(k_in[g % 4], b * 32 + (16 * (g // 4) + 16))
                    else:
                        pe.wait_ge(mk_loaded, b * 16 + 16)
                    if g >= 2 or not first:
                        pe.wait_ge(kt_act, b * 9 + (g - 1))
                        pe.wait_ge(kt_dve, b * 9 + (g - 1))
                    if g < NPG:
                        for h in range(HF):
                            last = pe.transpose(PS[:, bank + h // 4, (h % 4) * P:(h % 4 + 1) * P],
                                                kring[:, g % 4, h * P:(h + 1) * P], ident[:, :])
                    else:
                        for h in range(HM):
                            for a in range(2):
                                c = ((h % 2) * 2 + a) * P
                                last = pe.transpose(PS[:, bank + h // 2, c:c + P], mk_in[:, a, h * P:(h + 1) * P], ident[:, :])
                    last.then_inc(kt_filled, 1)

            def decode_scores(b, first=False):
                pe.wait_ge(kt_act, b * 9 + 9)
                pe.wait_ge(kt_dve, b * 9 + 9)
                pe.wait_ge(q_set, b + 1)
                if not first:
                    pe.wait_ge(d_exp, b)
                for c in range(3):
                    w = 512 if c < 2 else NS
                    o = PS[0:24, 4 + c, 0:w]
                    for h in range(HF):
                        k = keysT[:, h, c * 512:c * 512 + w] if c < 2 else raw[:, FK + h, SEQ:T]
                        pe.matmul(o, q_rows[:, h * 24:(h + 1) * 24], k, start=(h == 0), stop=False)
                    pe.matmul(o, sel_b[:, :], decay[:, c * 512:c * 512 + w], start=False, stop=(c < 2))
                pe.matmul(o, rep4[:, :, :].rearrange("p h q -> p (h q)"), causal_b,
                          start=False, stop=True)
                for h in range(HM):
                    last = pe.matmul(PS[0:16, 6, 64:64 + MEM], mq_rows[:, h * 16:(h + 1) * 16], mkeysT[:, h, :],
                                     start=(h == 0), stop=(h == HM - 1))
                last.then_inc(d_scored, 1)

            def decode_values(b, first=False):
                pe.wait_ge(d_prob, b + 1)
                if not first:
                    pe.wait_ge(d_out, b)
                pe.matmul(PS[:, 7, 0:24], dprob[0:24, 0:P], ident[0:24, 0:24], start=True, stop=True)
                for g in range(1, NPG):
                    pe.transpose(PS[:, 7, g * 24:(g + 1) * 24], dprob[0:24, g * P:(g + 1) * P], ident[0:24, 0:24])
                for a in range(2):
                    pe.transpose(PS[:, 7, 192 + a * 16:192 + (a + 1) * 16], mprob[0:16, a * P:(a + 1) * P], ident[0:16, 0:16])
                pe.transpose(PS[0:NS, 7, 224:248], dprob[0:24, PAST:KEYS], ident[0:24, 0:24]).then_inc(d_t, 1)
                pe.wait_ge(d_tc, b + 1)
                pe.wait_ge(v_loaded, b * 144 + 144)
                for h in range(HF):
                    o = PS[:, 7, 256 + h * NL:256 + (h + 1) * NL]
                    for g in range(NPG):
                        pe.matmul(o, vpages[:, g, h * P:(h + 1) * P], dpT[:, g, h * NL:(h + 1) * NL], start=(g == 0), stop=False)
                    pe.matmul(o, vtok[0:NS, 2, h * P:(h + 1) * P], npT[:, h * NL:(h + 1) * NL], start=False, stop=True)
                for h in range(HM):
                    for a in range(2):
                        last = pe.matmul(PS[:, 7, 280 + h * NL:280 + (h + 1) * NL], mv_in[:, a, h * P:(h + 1) * P],
                                         mpT[:, a, h * NL:(h + 1) * NL], start=(a == 0), stop=(a == 1))
                last.then_inc(d_pv, 1)

            keys_in(0, 0, True)
            decode_scores(0, True)
            keys_in(1, 1)
            decode_values(0, True)
            decode_scores(1)
            with pe.Fori(0, 3) as i:
                for u in range(2):
                    keys_in(i * 2 + (u + 2), u)
                    decode_values(i * 2 + (u + 1))
                    decode_scores(i * 2 + (u + 2))
            decode_values(NB - 1)

            def by_token(n):
                pe.wait_ge(wo_drained, n + 1)
                if n >= 2:
                    pe.wait_ge(h_added, 3 * (n - 1))
                for t, (t0, w) in enumerate(TILES):
                    last = pe.transpose(PS[0:w, 2 + n % 2, t * P:(t + 1) * P], attnT[:, n % 2, t0:t0 + w], ident[:, :])
                last.then_inc(at_filled, 1)

            pe.wait_ge(d_out, NB)
            for n in range(KC):
                pe.wait_ge(wo_in[(n // 2) % 3], 16 * (n // 6 + 1))
                if n >= 2:
                    pe.wait_ge(wo_drained, n - 1)
                for k in range(KC):
                    c = (n % 2) * P
                    last = pe.matmul(PS[:, n % 2, 0:T], wo_slot[(n // 2) % 3][:, k, c:c + P], cat[:, k, :], start=(k == 0), stop=(k == KC - 1))
                last.then_inc(wo_filled, 1)
                if n:
                    by_token(n - 1)
            by_token(KC - 1)
            for f, (t, c, m) in enumerate(HTF):
                pe.wait_ge(h_scl, t + 1)
                if f >= 2:
                    pe.wait_ge(ht_drained, f - 1)
                w = TILES[t][1]
                for a in range(m):
                    last = pe.transpose(ht_out(f)[:, a, :], h_scaled[0:w, t, (c + a) * P:(c + a + 1) * P], ident[0:w, 0:w])
                last.then_inc(ht_filled, 1)
            pe.wait_ge(ht_drained, HT_FILLS)
            pe.wait_ge(rt_in, 64)
            for t, (t0, w) in enumerate(TILES):
                o = PS[0:w, 4, t * 64:t * 64 + NG + NE]
                for k in range(KC):
                    pe.matmul(o, xnT[:, k, t0:t0 + w], w_rt[:, k, :], start=(k == 0), stop=False)
                pe.matmul(o, ones[0:1, 0:w], b_rt, start=False, stop=True).then_inc(lg_filled, 1)

            pe.wait_ge(y_clear, 1)
            with pe.Fori(0, NE) as e:
                pe.wait_ge(gcol_set, e + 1)
                for t, (t0, w) in enumerate(TILES):
                    last = pe.matmul(PS[:, 6, t0:t0 + w], gcol[0:w, t, :], ident[0:w, 0:w], start=True, stop=True)
                last.then_inc(gb_filled, 1)
                for j in range(FB):
                    for which, wt, sem_filled in ((0, wg_u, mg_filled), (1, wu_u, mu_filled)):
                        if j % 2 == 0:
                            pe.wait_ge(unit_in[j + which], e * 16 + 16)
                        if which == 0:
                            pe.wait_ge(silu_done, e * 4 + max(j, 1))
                        else:
                            pe.wait_ge(hs_done, e * 4 + max(j, 1))
                        for k in range(KC):
                            last = pe.matmul(PS[:, 2 * which + j % 2, 0:T], wt[j // 2][:, k, (j % 2) * P:(j % 2 + 1) * P], xnT[:, k, :],
                                             start=(k == 0), stop=(k == KC - 1))
                        last.then_inc(sem_filled, 1)
                pe.wait_ge(hT_done, e * 4 + 4)
                for n in range(KC):
                    if n % 8 == 0:
                        pe.wait_ge(unit_in[4 + n // 8], e * 16 + 16)
                    pe.wait_ge(y_added, e * 16 + max(n, 1))
                    for k in range(FB):
                        last = pe.matmul(PS[:, 4 + n % 2, 0:T], wd_u[n // 8][:, k, (n % 8) * P:(n % 8 + 1) * P], hT[:, k, :],
                                         start=(k == 0), stop=(k == FB - 1))
                    last.then_inc(md_filled, 1)
            pe.wait_ge(y_added, NE * 16 + 1)
            for t, (t0, w) in enumerate(TILES):
                for c in range(4):
                    f = 4 * t + c
                    if f >= 2:
                        pe.wait_ge(y_done, f - 1)
                    for a in range(4):
                        last = pe.transpose(PS[0:w, f % 2, a * P:(a + 1) * P], yT[:, 4 * c + a, t0:t0 + w], ident[:, :])
                    last.then_inc(yt_filled, 1)


N_CONSTS = 26
G_STEPS = 42


_INS = ['x_prompt', 'x_sample', 'cache_fox_k', 'cache_fox_v', 'cache_fox_logf', 'cache_mem_k', 'cache_mem_v',
        'state_hgrn', 'page_table', 'mem_prompt', 'g_attn_norm', 'w_in', 'b_fox_f', 'g_fox_q', 'g_fox_k', 'lb_logits',
        'g_hgrn_out', 'g_mem_norm', 'w_mem_kv', 'g_mem_q', 'g_mem_k', 'w_out', 'g_ffn_norm', 'w_router_group',
        'b_router_group', 'w_router_expert', 'b_router_expert', 'w_gate_e', 'w_up_e', 'w_down_e']
_OUTS = [(1, 256, 2048), (8, 4, 2048), (1, 1, 256, 6, 128), (1, 1, 256, 6, 128), (1, 1, 256, 6), (1, 1, 6, 128, 128),
         (1, 1, 256, 4, 128), (1, 1, 256, 4, 128), (1, 8, 4, 6, 128), (1, 8, 4, 6, 128), (1, 8, 4, 6), (1, 8, 6, 128, 128)]


def kernel(**inputs):
    import numpy as _np
    import concourse.bacc as _bacc
    from concourse import mybir as _mybir
    from concourse.bass_utils import run_bass_kernel_spmd as _run

    nc = _bacc.Bacc("TRN2", target_bir_lowering=False, num_devices=1)
    arrays, args = {}, []
    for name in _INS:
        a = _np.ascontiguousarray(inputs[name])
        arrays[f"in_{name}_dram"] = a
        args.append(nc.dram_tensor(f"in_{name}_dram", a.shape, _mybir.dt.from_np(a.dtype), kind="ExternalInput").ap())
    for i, shape in enumerate(_OUTS):
        args.append(nc.dram_tensor(f"out_{i}_dram", shape, _mybir.dt.float32, kind="ExternalOutput").ap())
    build(nc, *args)
    r = _run(nc, [arrays], core_ids=[0])
    return tuple(r.results[0][f"out_{i}_dram"] for i in range(len(_OUTS)))
```

```python
from contextlib import ExitStack

import concourse.bass as bass
from concourse import mybir

D = 2048
P = 128
KC = D // P
SEQ = 256
NB, NL = 8, 4
NS = NB * NL
T = SEQ + NS
TILES = [(0, P), (P, P), (SEQ, NS)]
MEM = 256
HF, HG, HM = 6, 6, 4
FW, MW = HF * P, HM * P
IN_W = 7 * FW + HF + MW
FF_COL = 3 * FW
NPG, PG = 8, 128
POOL = 80
PAST = NPG * PG
KEYS = PAST + NS
CH = 16
NCH = SEQ // CH
NE, NG, EPG = 32, 4, 8
FFW = 512
FB = FFW // P
EPS = 1e-6
SCALE = float(P) ** -0.5
NEG = -1.0e30
HQ, HFG, HI, HGT, FQ, FK, FV, MQ = 0, 6, 12, 18, 24, 30, 36, 42
NBLK = 46
NN = HF + HF + HM + HM + HG
SLOTS = 64
PAIRS = NE // 2
UNITS_PAIR = 12
UPP = 11


def build(nc, x_prompt, x_sample, cache_fox_k, cache_fox_v, cache_fox_logf, cache_mem_k, cache_mem_v,
          state_hgrn, page_table, mem_prompt, g_attn_norm, w_in, b_fox_f, g_fox_q, g_fox_k, lb_logits,
          g_hgrn_out, g_mem_norm, w_mem_kv, g_mem_q, g_mem_k, w_out, g_ffn_norm, w_router_group,
          b_router_group, w_router_expert, b_router_expert, w_gate_e, w_up_e, w_down_e,
          y_prompt, y_sample, fox_k_p, fox_v_p, fox_logf_p, hgrn_state_p, mem_k_p, mem_v_p,
          fox_k_s, fox_v_s, fox_logf_s, hgrn_state_s, dbg=None):
    f32, i32 = mybir.dt.float32, mybir.dt.int32
    ALU, ACT, AX = mybir.AluOpType, mybir.ActivationFunctionType, mybir.AxisListType
    ds = bass.ds

    x_tok_d = [x_prompt[0, 0:P, :], x_prompt[0, P:SEQ, :], x_sample.rearrange("b l d -> (b l) d")]
    mem_tok_d = [mem_prompt[0, 0:P, :], mem_prompt[0, P:MEM, :]]
    w_in_d = w_in[0].rearrange("(k p) n -> p k n", p=P)
    w_kv_d = w_mem_kv[0].rearrange("(k p) n -> p k n", p=P)
    w_out_d = w_out[0].rearrange("(k p) n -> p k n", p=P)
    w_gate_d = w_gate_e[0].rearrange("e (k p) n -> e p k n", p=P)
    w_up_d = w_up_e[0].rearrange("e (k p) n -> e p k n", p=P)
    w_down_d = w_down_e[0].rearrange("e (k p) n -> e p k n", p=P)
    w_rg_d = w_router_group[0].rearrange("(k p) n -> p k n", p=P)
    w_re_d = w_router_expert[0].rearrange("(k p) n -> p k n", p=P)
    y_tok_d = [y_prompt[0, 0:P, :], y_prompt[0, P:SEQ, :], y_sample.rearrange("b l d -> (b l) d")]
    logf_d = cache_fox_logf[0].rearrange("g t h -> g (t h)")
    k_pages = cache_fox_k[0].rearrange("g t h d -> g t (h d)")
    v_pages = cache_fox_v[0].rearrange("g t h d -> g t (h d)")

    ctx = ExitStack()
    with ctx:
        ctx.enter_context(nc.allow_non_contiguous_dma(reason="small vectors and column blocks"))

        def sb(name, shape, dt=f32):
            return ctx.enter_context(nc.sbuf_tensor(name, shape, dt))

        def sem(name):
            return ctx.enter_context(nc.semaphore(name))

        ident = sb("ident", [P, P])
        ones = sb("ones", [P, P])
        tri_le = sb("tri_le", [P, P])
        tri_gt = sb("tri_gt", [P, P])
        causal = sb("causal", [P, P])
        sel48 = sb("sel48", [NB * HF, NB, HF, NL])
        causal4 = sb("causal4", [NL, NB, NS])
        rep4 = sb("rep4", [NL, HF, NL])
        batch_of = sb("batch_of", [NS, NB])
        chunk_of = sb("chunk_of", [P, P // CH])
        rows = sb("rows", [65, P])
        cols = sb("cols", [P, 65])
        eps_t = sb("eps_t", [P, 1])
        one_t = sb("one_t", [P, 1])
        lbw = sb("lbw", [P, 6, HG])
        gq = sb("gq", [P, 5])
        ssq = sb("ssq", [P, 8])
        rstd = sb("rstd", [P, 8])
        b_f = sb("b_f", [HF, 1])
        G_ATT, G_MEM, G_FFN = cols[:, 0:KC], cols[:, KC:2 * KC], cols[:, 2 * KC:3 * KC]
        g_fq, g_fk, g_hn, g_mq, g_mk = (cols[:, 48 + n:49 + n] for n in range(5))
        lb0, lb1 = cols[:, 53:59], cols[:, 59:65]
        LB, LB1 = lbw[:, 4, :], lbw[:, 5, :]

        arena = sb("arena", [P, 45888])

        def view(off, *dims):
            n = 1
            for d in dims:
                n *= d
            a = arena[:, off:off + n]
            if len(dims) == 2:
                return a.rearrange("p (a b) -> p a b", b=dims[1])
            if len(dims) == 3:
                return a.rearrange("p (a b c) -> p a b c", b=dims[1], c=dims[2])
            return a

        RAW = 0
        CAT = RAW + NBLK * T
        MRAW = CAT + KC * T
        MTOK = MRAW + 8 * MEM
        TOK = MTOK + 2 * 1024
        WORK = TOK + 9 * FW
        raw = view(RAW, NBLK, T)
        x_tok = view(RAW, 3, D)
        mem_tok_in = view(RAW + 3 * D, 2, D)
        junk = view(CAT, D)
        cat = view(CAT, KC, T)
        mraw = view(MRAW, 8, MEM)
        mtok = view(MTOK, 2, 1024)
        memT = view(TOK, KC, MEM)
        ktok, vtok = (view(TOK + n * 3 * FW, 3, FW) for n in range(2))
        xT = view(WORK, KC, T)
        wslot = [view(WORK + KC * T + n * KC * 384, KC, 384) for n in range(2)]
        w_ff = view(WORK + KC * T + 2 * KC * 384, KC, HF)
        WEND = WORK + KC * T + 2 * KC * 384 + KC * HF

        def heads2(n):
            return view(TOK + n * 2 * T, 2, T)

        gQ, gF, gV, gO, gKT, gTmp = (heads2(n) for n in range(6))
        gW = [heads2(6), heads2(7)]
        gQW = [heads2(8), heads2(9)]
        gS = view(TOK + 10 * 2 * T, 160)
        decays = sb("decays", [P, HG, NCH + NB])
        vpar = view(TOK, 2, 2, FW)
        vsam = view(TOK + 4 * FW, FW)[0:NS]
        states = view(TOK + 5 * FW, NCH, P)
        vmask = [view(TOK + 5 * FW + NCH * P + n * 4 * P, 4, P)[0:NS] for n in range(2)]
        s_in = [view(MTOK + n * NB * P, NB, P) for n in range(2)]
        ktil = sb("ktil", [P, 3, P])
        parity = sb("parity", [P, 2])
        probs = view(WORK, 2, SEQ)
        probsT = view(WORK + 2 * SEQ, 2, 2, P)
        kpage = [view(TOK + (6 + g) * FW, FW) for g in range(7)] + [view(4096, FW)]
        vpages = view(WORK + 4 * FW, NPG, FW)
        keysT = view(WORK + 12 * FW, HF, PAST)
        dprob = view(WORK + 12 * FW + HF * PAST, KEYS)
        mk_in = view(MRAW, 2, MW)
        mv_in = view(MRAW + 2 * MW, 2, MW)
        mkeysT = view(MRAW + 4 * MW, HM, MEM)
        mprob = view(MRAW + 4 * MW + HM * MEM, MEM)
        dprobT = view(MRAW + 4 * MW + HM * MEM + MEM, 248)
        dpT = dprobT[:, 0:192].rearrange("p (g r) -> p g r", r=24)
        mpT = dprobT[:, 192:224].rearrange("p (g r) -> p g r", r=16)
        npT = dprobT[0:NS, 224:248]
        wo_slot = [view(o, KC, 256) for o in (RAW, WORK, WORK + 4096)]
        attnT = view(WORK + 9216, 2, T)
        h_tok = view(TOK, 3, D)
        UNIT = 4096
        LATE, LATE_END = 5 * UNIT, TOK
        HSC = TOK + 3 * D
        YT = HSC + 3 * D
        UNIT5 = YT + KC * T
        FREE = UNIT5 + UNIT
        unit = [view(o, UNIT) for o in (UNIT, 2 * UNIT, UNIT5, 0, 3 * UNIT, 4 * UNIT)]
        YB = (0, 1, 6, 7)
        h_scaled = view(HSC, 3, D)
        h_back = view(HSC, 3, D)
        xnT = view(YT, KC, T)
        yT = view(YT, KC, T)
        xgT = view(TOK, KC, 2 * SLOTS)
        yslot = view(TOK + 2 * D, D)
        hT = view(FREE, FB, 2 * SLOTS)
        hS = view(FREE + 2 * FB * SLOTS, FFW)
        pick_tok = view(FREE + 4 * FB * SLOTS, 3, 2, SLOTS)
        pick_gate = view(FREE + 4 * FB * SLOTS + 6 * SLOTS, 3, 2, SLOTS)
        w_rt = view(FREE, KC, NG + NE)
        gate_slot = view(FREE + 4 * FB * SLOTS + 12 * SLOTS, T)

        def late(*dims):
            nonlocal LATE
            n = 1
            for d in dims:
                n *= d
            LATE += n
            assert LATE <= LATE_END
            return view(LATE - n, *dims)

        logits = late(3, NG + NE)
        b_rt = late(NG + NE)[0:1]
        rw = late(3, 2 * NE)
        gates = late(3, NE)
        choice = late(3, 2, NE)
        c1g = late(3, NE)
        slot_of = late(3, NE)
        iota1 = late(SLOTS)
        over = late(3, NE)
        n_over = late(2)
        overflow = sb("overflow", [P, 1], i32)
        g_scaled = view(0, 3, D)
        g_xnT = view(TOK, KC, T)
        g_hT = view(TOK + KC * T, FB, T)
        gbc = view(TOK + KC * T + FB * T, T)
        gcol = view(FREE, 3, P)
        g_hS = view(FREE + 3 * P, 2, T)
        wg_u = [unit[n].rearrange("p (k n) -> p k n", k=KC) for n in (0, 2)]
        wu_u = [unit[n].rearrange("p (k n) -> p k n", k=KC) for n in (1, 3)]
        wd_u = [unit[n].rearrange("p (k n) -> p k n", k=FB) for n in (4, 5)]
        HTF = [(t, c, 4) for t in range(2) for c in range(0, KC, 4)] + [(2, 0, KC)]
        HT_FILLS = len(HTF)

        def ht_out(f):
            t, c, m = HTF[f]
            return PS[:, 4 * (f % 2), :].rearrange("p (c t) -> p c t", c=m)[:, :, 0:TILES[t][1]]

        q_rows = sb("q_rows", [P, HF * 28])
        mq_rows = sb("mq_rows", [P, HM * 20])
        sel_b = sb("sel_b", [NB * HF, HF * NL])
        causal_b = view(WORK + 12 * FW + HF * PAST + KEYS, NS)[0:NL]
        nmax = sb("nmax", [P, 4])
        psum_p = sb("psum_p", [P, 4])
        ptab_row = sb("ptab_row", [1, NB * NPG], i32)

        ffz = sb("ffz", [HF, T])
        ffw = sb("ffw", [HF, T])
        lfT = sb("lfT", [HF, T])
        lftok = sb("lftok", [P, 3, HF])
        negc = sb("negc", [HF, SEQ])
        ptab = sb("ptab", [NB * NPG, 1], i32)
        lfpages = view(MTOK, PG * HF)[0:NB * NPG]
        lfp = sb("lfp", [P, NPG, NB, HF])
        lfs = sb("lfs", [P, NPG, NB, HF])
        lfm = sb("lfm", [NS, NB, HF])
        decay = sb("decay", [NB * HF, KEYS])

        sq = sb("sq", [P, 2, T])
        hn_r = sb("hn_r", [NN, T])
        row_of = sb("row_of", [P, 2 * NN - 1])

        PS = ctx.enter_context(nc.psum_tensor("PS", [P, 8, 512], f32))

        consts_set = sem("consts_set")
        rows_in = sem("rows_in")
        cols_filled = sem("cols_filled")
        cols_set = sem("cols_set")
        gains_set = sem("gains_set")
        tok_in = [sem(f"tok_in{n}") for n in range(5)]
        ssq_clear = sem("ssq_clear")
        ssq_done = sem("ssq_done")
        sqrt_done = sem("sqrt_done")
        scaled = sem("scaled")
        tT_filled = sem("tT_filled")
        tT_drained = sem("tT_drained")
        w_in_slot = [sem(f"w_in_slot{n}") for n in range(2)]
        wff_in = sem("wff_in")
        blk_filled = sem("blk_filled")
        blk_drained = sem("blk_drained")
        hn_sq = sem("hn_sq")
        hn_sum = sem("hn_sum")
        hn_sqrt = sem("hn_sqrt")
        hn_rcp = sem("hn_rcp")
        hn_rows = sem("hn_rows")
        hn_done = sem("hn_done")
        tk_filled = sem("tk_filled")
        tk_drained = sem("tk_drained")
        lf_act = sem("lf_act")
        lf_done = sem("lf_done")
        lft_filled = sem("lft_filled")
        lft_drained = sem("lft_drained")
        c_filled = sem("c_filled")
        negc_set = sem("negc_set")
        ptab_in = sem("ptab_in")
        lfpages_in = sem("lfpages_in")
        lfp_filled = sem("lfp_filled")
        lfp_drained = sem("lfp_drained")
        lfs_done = sem("lfs_done")
        lfm_done = sem("lfm_done")
        dec_filled = sem("dec_filled")
        decay_set = sem("decay_set")
        out_done = sem("out_done")
        wo_in = [sem(f"wo_in{n}") for n in range(3)]
        x_again = sem("x_again")
        wo_filled = sem("wo_filled")
        wo_drained = sem("wo_drained")
        at_filled = sem("at_filled")
        h_added = sem("h_added")
        rt_in = sem("rt_in")
        h_ssq = sem("h_ssq")
        h_sqrt = sem("h_sqrt")
        h_scl = sem("h_scl")
        ht_filled = sem("ht_filled")
        ht_drained = sem("ht_drained")
        lg_filled = sem("lg_filled")
        rt_sub = sem("rt_sub")
        rt_exp = sem("rt_exp")
        gates_set = sem("gates_set")
        unit_in = [sem(f"unit_in{n}") for n in range(6)]
        y_clear = sem("y_clear")
        rank_filled = sem("rank_filled")
        slots_set = sem("slots_set")
        over_filled = sem("over_filled")
        overflow_set = sem("overflow_set")
        h_out = sem("h_out")
        h_again = sem("h_again")
        units_used = sem("units_used")
        picked_set = sem("picked_set")
        pg_set = sem("pg_set")
        xg_filled = sem("xg_filled")
        xg_drained = sem("xg_drained")
        pair_silu = sem("pair_silu")
        pair_hT = sem("pair_hT")
        pair_h = sem("pair_h")
        ph_filled = sem("ph_filled")
        g_filled = sem("g_filled")
        g_copied = sem("g_copied")
        yst_filled = sem("yst_filled")
        yst_act = sem("yst_act")
        yst_dve = sem("yst_dve")
        part_filled = sem("part_filled")
        part_added = sem("part_added")
        gcol_set = sem("gcol_set")
        mg_filled = sem("mg_filled")
        mu_filled = sem("mu_filled")
        hs_done = sem("hs_done")
        md_filled = sem("md_filled")
        yt_filled = sem("yt_filled")
        y_done = sem("y_done")
        lb_diff = sem("lb_diff")
        lb_exp = sem("lb_exp")
        lb_set = sem("lb_set")
        hg_prep = sem("hg_prep")
        hg_step = sem("hg_step")
        qw_ready = sem("qw_ready")
        intra_filled = sem("intra_filled")
        intra_used = sem("intra_used")
        hg_done = sem("hg_done")
        parity_set = sem("parity_set")
        vt_filled = sem("vt_filled")
        vt_drained = sem("vt_drained")
        kt2_filled = sem("kt2_filled")
        kt2_drained = sem("kt2_drained")
        s_loaded = [sem(f"s_loaded{n}") for n in range(2)]
        os_filled = sem("os_filled")
        ds_filled = sem("ds_filled")
        ds_used = sem("ds_used")
        sm_set = sem("sm_set")
        oi_filled = sem("oi_filled")
        o_added = sem("o_added")
        sig_done = sem("sig_done")
        gate_done = sem("gate_done")
        st_step = sem("st_step")
        stp_out = sem("stp_out")
        sts_out = [sem(f"sts_out{n}") for n in range(2)]
        pa_scored = sem("pa_scored")
        pa_max = sem("pa_max")
        pa_exp = sem("pa_exp")
        pa_prob = sem("pa_prob")
        pa_t = sem("pa_t")
        pa_tc = sem("pa_tc")
        pa_pv = sem("pa_pv")
        pa_out = sem("pa_out")
        ptrow_in = sem("ptrow_in")
        k_in = tok_in + [sem(f"k_in{n}") for n in range(5, NPG)]
        mk_loaded = sem("mk_loaded")
        v_loaded = sem("v_loaded")
        kt_filled = sem("kt_filled")
        kt_act = sem("kt_act")
        kt_dve = sem("kt_dve")
        q_clear = sem("q_clear")
        q_set = sem("q_set")
        d_scored = sem("d_scored")
        d_max = sem("d_max")
        d_exp = sem("d_exp")
        d_rcp = sem("d_rcp")
        d_prob = sem("d_prob")
        d_t = sem("d_t")
        d_tc = sem("d_tc")
        d_pv = sem("d_pv")
        d_out = sem("d_out")
        dve_step = sem("dve_step")

        NORM = [(mem_tok_in[:, 0], P, 3), (mem_tok_in[:, 1], P, 4),
                (x_tok[:, 0], P, 0), (x_tok[:, 1], P, 1), (x_tok[:, 2], NS, 2)]
        FILLS = [(n, c, 4) for n in range(4) for c in range(0, KC, 4)] + [(4, 0, KC)]

        def fill_out(f, w):
            n, c, m = FILLS[f]
            return PS[:, f % 8, :].rearrange("p (c t) -> p c t", c=m)[:, :, 0:w]

        NORMS = [(raw[:, FQ + h, :], T, 0) for h in range(HF)] + [(raw[:, FK + h, :], T, 1) for h in range(HF)] + \
                [(raw[:, MQ + h, :], T, 2) for h in range(HM)] + [(mraw[:, h, :], MEM, 3) for h in range(HM)]
        NORMS += [(cat[:, 6 + h, :], T, 4) for h in range(HG)]
        assert NN == len(NORMS)

        TOKF = []
        for dst, b0 in ((ktok, FK), (vtok, FV)):
            for t, (t0, n) in enumerate(TILES):
                for h0, m in ((0, 4), (4, 2)):
                    TOKF.append((dst[0:n, t, h0 * P:(h0 + m) * P], n,
                                 [raw[:, b0 + h, t0:t0 + n] for h in range(h0, h0 + m)]))
        for t in range(2):
            for h0 in (0, 4):
                TOKF.append((mtok[:, t, h0 * P:(h0 + 4) * P], P,
                             [mraw[:, h, t * P:(t + 1) * P] for h in range(h0, h0 + 4)]))
        NTF = len(TOKF)

        UNITS = [(True, h, qb) for h in range(HF) for qb in range(2)] + \
                [(False, h, qb) for h in range(HM) for qb in range(2)]
        NU = len(UNITS)

        def width(u):
            fox, h, qb = UNITS[u]
            return (qb + 1) * P if fox else MEM

        ORDER = [3, 4, 5, 0, 1, 2]
        LAST = [FV + h for h in range(HF)] + [MQ + h for h in range(HM)]

        block = ctx.enter_context(nc.Block())

        @block.sync
        def _(sp):
            for n, d in ((0, mem_tok_d[0]), (1, mem_tok_d[1])):
                sp.dma_start(NORM[n][0], d).then_inc(tok_in[n], 16)
            sp.dma_start(rows[0:16, :], g_attn_norm[0].rearrange("(k p) -> k p", p=P)).then_inc(rows_in, 16)
            sp.dma_start(rows[16:32, :], g_mem_norm[0].rearrange("(k p) -> k p", p=P)).then_inc(rows_in, 16)
            sp.dma_start(rows[32:48, :], g_ffn_norm[0].rearrange("(k p) -> k p", p=P)).then_inc(rows_in, 16)
            for n, g in enumerate((g_fox_q, g_fox_k, g_hgrn_out, g_mem_q, g_mem_k)):
                sp.dma_start(rows[48 + n:49 + n, :], g).then_inc(rows_in, 16)
            sp.dma_start(rows[53:65, :], lb_logits.rearrange("l (h p) -> (l h) p", p=P)).then_inc(rows_in, 16)
            sp.dma_start(wslot[0], w_kv_d[:, :, 0:384]).then_inc(w_in_slot[0], 16)
            for n in range(3):
                sp.dma_start(NORM[2 + n][0][0:NORM[2 + n][1]], x_tok_d[n]).then_inc(tok_in[2 + n], 16)
            sp.dma_start(wslot[1], w_kv_d[:, :, 384:768]).then_inc(w_in_slot[1], 16)
            sp.dma_start(b_f[:, :], b_fox_f.rearrange("a h -> h a")).then_inc(wff_in, 16)
            sp.dma_start(w_ff, w_in_d[:, :, FF_COL:FF_COL + HF]).then_inc(wff_in, 16)
            sp.wait_ge(blk_filled, 3)
            sp.dma_start(wslot[0][:, :, 0:256], w_kv_d[:, :, 768:1024]).then_inc(w_in_slot[0], 16)
            for i0, ni, col in ((0, 4, FF_COL + HF), (4, 3, 0)):
                with sp.Fori(0, ni) as i:
                    sp.wait_ge(blk_filled, i * 6 + (6 * i0 + 6))
                    sp.dma_start(wslot[1], w_in_d[:, :, ds(i * FW + col, 384)]).then_inc(w_in_slot[1], 16)
                    sp.wait_ge(blk_filled, i * 6 + (6 * i0 + 8))
                    sp.dma_start(wslot[0], w_in_d[:, :, ds(i * FW + (col + 384), 384)]).then_inc(w_in_slot[0], 16)
            mq0 = IN_W - MW
            sp.wait_ge(blk_filled, 47)
            sp.dma_start(wslot[1][:, :, 0:256], w_in_d[:, :, mq0:mq0 + 256]).then_inc(w_in_slot[1], 16)
            sp.wait_ge(blk_filled, 50)
            sp.dma_start(wslot[0][:, :, 0:256], w_in_d[:, :, mq0 + 256:mq0 + 512]).then_inc(w_in_slot[0], 16)

            no = 0
            sp.wait_ge(tk_drained, NTF)
            for dst_p, dst_s, src in ((fox_k_p, fox_k_s, ktok), (fox_v_p, fox_v_s, vtok)):
                sp.dma_start(dst_p[0, 0].rearrange("(a t) h d -> t a (h d)", t=P), src[:, 0:2, :]).then_inc(out_done, 16)
                sp.dma_start(dst_s[0].rearrange("b l h d -> (b l) (h d)"), src[0:NS, 2, :]).then_inc(out_done, 16)
                no += 2
            for dst, c in ((mem_k_p, 0), (mem_v_p, 512)):
                sp.dma_start(dst[0, 0].rearrange("(a t) h d -> t a (h d)", t=P), mtok[:, :, c:c + 512]).then_inc(out_done, 16)
                no += 1
            sp.wait_ge(lft_drained, 1)
            sp.dma_start(fox_logf_p[0, 0].rearrange("(a t) h -> t a h", t=P), lftok[:, 0:2, :]).then_inc(out_done, 16)
            sp.dma_start(fox_logf_s[0].rearrange("b l h -> (b l) h"), lftok[0:NS, 2, :]).then_inc(out_done, 16)
            no += 2
            sp.dma_start(ptab_row[:, :], page_table.rearrange("(a b) g -> a (b g)", a=1)).then_inc(ptrow_in, 16)
            sp.wait_ge(ptrow_in, 16)

            def load_key_page(b, g, first=False):
                page = sp.value_load(ptab_row[0:1, ds(b * NPG + g, 1)], min_val=0, max_val=POOL - 1)
                if not first:
                    sp.wait_ge(kt_filled, b * 9 + (g - 8))
                sp.dma_start(kpage[g], k_pages[ds(page, 1)].rearrange("g t n -> t (g n)")).then_inc(k_in[g], 16)

            def load_mem_keys(b, first=False):
                if not first:
                    sp.wait_ge(kt_filled, b * 9)
                sp.dma_start(mk_in, cache_mem_k[0][ds(b, 1)].rearrange("b (a t) h d -> t (b a) (h d)", t=P)).then_inc(mk_loaded, 16)

            for g in (0, 1, 2, 5, 6, 7):
                load_key_page(0, g, True)
            sp.wait_ge(pa_out, NU)
            for g in (3, 4):
                load_key_page(0, g, True)
            load_mem_keys(0, True)
            with sp.Fori(0, NB - 1) as i:
                for g in range(NPG):
                    load_key_page(i + 1, g)
                load_mem_keys(i + 1)

            sp.wait_ge(hn_done, NN)
            sp.dma_start(wo_slot[0], w_out_d[:, :, 0:256]).then_inc(wo_in[0], 16)
            sp.wait_ge(d_pv, NB)
            for n in (1, 2):
                sp.dma_start(wo_slot[n], w_out_d[:, :, n * 256:(n + 1) * 256]).then_inc(wo_in[n], 16)
            sp.wait_ge(out_done, 16 * no)
            for t, (t0, n) in enumerate(TILES):
                sp.dma_start(h_tok[0:n, t, :], x_tok_d[t]).then_inc(x_again, 16)
            sp.dma_start(b_rt[:, 0:NG], b_router_group).then_inc(rt_in, 16)
            sp.dma_start(b_rt[:, NG:NG + NE], b_router_expert).then_inc(rt_in, 16)
            for n in range(3, 8):
                sp.wait_ge(wo_filled, 2 * (n - 2))
                sp.dma_start(wo_slot[n % 3], w_out_d[:, :, n * 256:(n + 1) * 256]).then_inc(wo_in[n % 3], 16)
            sp.dma_start(w_rt[:, :, 0:NG], w_rg_d).then_inc(rt_in, 16)
            sp.dma_start(w_rt[:, :, NG:NG + NE], w_re_d).then_inc(rt_in, 16)

            def load_unit(p, u, slot):
                x, half, which = u % 2, (u // 2) % 2, u // 4
                k = (KC, KC, FB)[which] // 2
                src = (w_gate_d, w_up_d, w_down_d)[which][ds(p * 2 + x, 1), :, half * k:(half + 1) * k, :]
                sp.dma_start(unit[slot].rearrange("p (k n) -> p k n", k=k), src.rearrange("e p k n -> p (e k) n")).then_inc(unit_in[slot], 16)

            def ring_loads(p):
                for u in range(UNITS_PAIR):
                    if u < 5:
                        sp.wait_ge(units_used, p * UPP - (4 - u))
                    elif u == 5:
                        sp.wait_ge(yst_filled, p * 4)
                    else:
                        sp.wait_ge(units_used, p * UPP + (u - 5))
                    load_unit(p, u, u % 6)

            for u in range(3):
                load_unit(0, u, u)
            sp.wait_ge(wo_filled, 14)
            load_unit(0, 3, 3)
            sp.wait_ge(h_added, 3 * KC)
            for u in (4, 5):
                load_unit(0, u, u)
            for t, (t0, n) in enumerate(TILES):
                sp.dma_start(y_tok_d[t], h_tok[0:n, t, :]).then_inc(h_out, 16)
            for u in range(6, UNITS_PAIR):
                sp.wait_ge(units_used, u - 5)
                load_unit(0, u, u % 6)
            with sp.Fori(0, PAIRS - 1) as i:
                ring_loads(i + 1)
            sp.wait_ge(h_out, 48)
            for t, (t0, n) in enumerate(TILES):
                sp.dma_start(h_back[0:n, t, :], y_tok_d[t]).then_inc(h_again, 16)

            def expert_loads(e, first=False):
                for c in range(2):
                    cols = slice(c * 256, (c + 1) * 256)
                    if not first:
                        sp.wait_ge(mg_filled, e * 4 + (2 * c - 2))
                    sp.dma_start(wg_u[c], w_gate_d[ds(e, 1), :, :, cols].rearrange("e p k n -> p (e k) n")).then_inc(unit_in[2 * c], 16)
                    if not first:
                        sp.wait_ge(mu_filled, e * 4 + (2 * c - 2))
                    sp.dma_start(wu_u[c], w_up_d[ds(e, 1), :, :, cols].rearrange("e p k n -> p (e k) n")).then_inc(unit_in[2 * c + 1], 16)
                for c in range(2):
                    cols = slice(c * 1024, (c + 1) * 1024)
                    if not first:
                        sp.wait_ge(md_filled, e * 16 + (8 * c - 7))
                    sp.dma_start(wd_u[c], w_down_d[ds(e, 1), :, :, cols].rearrange("e p k n -> p (e k) n")).then_inc(unit_in[4 + c], 16)

            sp.wait_ge(overflow_set, 1)
            n_past = sp.value_load(overflow[0:1, 0:1], min_val=0, max_val=2 * T)
            with sp.If(n_past > 0):
                sp.wait_ge(ht_filled, 2 * HT_FILLS)
                expert_loads(0, True)
                with sp.Fori(0, NE - 1) as e:
                    expert_loads(e + 1)
            for t, (t0, n) in enumerate(TILES):
                sp.wait_ge(y_done, 4 * t + 4)
                sp.dma_start(y_tok_d[t], h_back[0:n, t, :]).then_inc(h_out, 16)
            sp.wait_ge(h_out, 96)

        @block.gpsimd
        def _(pool):
            n_set = 0

            def fill(ap, v):
                nonlocal n_set
                pool.memset(ap, v).then_inc(consts_set, 1)
                n_set += 1

            def pick(ap, op, value, base, pattern, cm):
                nonlocal n_set
                pool.wait_ge(consts_set, n_set)
                pool.affine_select(out=ap, in_=ap, compare_op=op, fill=value, base=base, pattern=pattern,
                                   channel_multiplier=cm).then_inc(consts_set, 1)
                n_set += 1

            fill(ident[:, :], 0.0)
            fill(ones[:, :], 1.0)
            pick(ident[:, :], ALU.not_equal, 1.0, 0, [[-1, P]], 1)
            fill(eps_t[:, :], EPS)
            fill(one_t[:, :], 1.0)
            fill(tri_le[:, :], 1.0)
            fill(tri_gt[:, :], 1.0)
            fill(causal[:, :], 0.0)
            fill(sel48[:, :, :, :], 0.0)
            fill(causal4[:, :, :], 0.0)
            fill(rep4[:, :, :], 0.0)
            fill(batch_of[:, :], 1.0)
            fill(chunk_of[:, :], 1.0)
            fill(row_of[:, :], 0.0)
            pick(tri_le[:, :], ALU.is_ge, 0.0, 0, [[1, P]], -1)
            pick(tri_gt[:, :], ALU.is_gt, 0.0, 0, [[-1, P]], 1)
            pick(causal[:, :], ALU.is_ge, NEG, 0, [[-1, P]], 1)
            pick(sel48[:, :, :, :], ALU.not_equal, 1.0, 0, [[-HF, NB], [-1, HF], [0, NL]], 1)
            pick(causal4[:, :, :], ALU.is_ge, NEG, 0, [[-NL, NB], [1, NS]], 0)
            pick(causal4[:, :, :], ALU.is_ge, NEG, 0, [[NL, NB], [-1, NS]], 1)
            pick(rep4[:, :, :], ALU.not_equal, 1.0, 0, [[0, HF], [-1, NL]], 1)
            pick(batch_of[:, :], ALU.is_ge, 0.0, 0, [[-NL, NB]], 1)
            pick(batch_of[:, :], ALU.is_ge, 0.0, NL - 1, [[NL, NB]], -1)
            pick(chunk_of[:, :], ALU.is_ge, 0.0, 0, [[-CH, P // CH]], 1)
            pick(chunk_of[:, :], ALU.is_ge, 0.0, CH - 1, [[CH, P // CH]], -1)
            pick(row_of[:, :], ALU.not_equal, 1.0, 1 - NN, [[1, 2 * NN - 1]], 0)
            assert n_set == N_CONSTS, n_set
            pool.dma_start(ptab[:, :], page_table.rearrange("b (g a) -> (b g) a", a=1)).then_inc(ptab_in, 16)
            pool.wait_ge(ptab_in, 16)
            pool.indirect_dma_start(out=lfpages, out_offset=None, in_=logf_d,
                                    in_offset=bass.IndirectOffsetOnAxis(ap=ptab[:, 0:1], axis=0)).then_inc(lfpages_in, 16)
            pool.wait_ge(lfp_filled, 1)
            for h in range(2):
                pool.dma_start(s_in[h], state_hgrn[0, :, h].rearrange("b k v -> k b v")).then_inc(s_loaded[h], 16)
            def states_out(h):
                pool.wait_ge(ds_used, 10 * h + 8)
                pool.dma_start(hgrn_state_p[0, 0, h], states[:, NCH - 1, :]).then_inc(stp_out, 16)
                pool.wait_ge(ds_used, 10 * h + 10)
                pool.dma_start(hgrn_state_s[0, :, h].rearrange("b k v -> k b v"), s_in[h % 2]).then_inc(sts_out[h % 2], 16)
                if h + 2 < HG:
                    pool.wait_ge(sts_out[h % 2], 16 * (h // 2 + 1))
                    pool.dma_start(s_in[h % 2], state_hgrn[0, :, h + 2].rearrange("b k v -> k b v")).then_inc(s_loaded[h % 2], 16)

            pool.wait_ge(vt_drained, 6)
            for h in range(HG):
                for c in range(2):
                    if h:
                        pool.wait_ge(ds_filled, 10 * (h - 1) + 9 + c)
                    pool.tensor_tensor(vmask[c], vsam[:, h * P:(h + 1) * P].rearrange("p (a v) -> p a v", a=1).to_broadcast([NS, 4, P]),
                                       batch_of[:, 4 * c:4 * c + 4].rearrange("p (b a) -> p b a", a=1).to_broadcast([NS, 4, P]),
                                       ALU.mult).then_inc(sm_set, 1)
                if h:
                    states_out(h - 1)
            states_out(HG - 1)
            pool.wait_ge(stp_out, 16 * HG)
            for n in range(2):
                pool.wait_ge(sts_out[n], 16 * HG // 2)

            pool.wait_ge(ptrow_in, 16)
            pool.wait_ge(blk_filled, 55)

            def load_values(b, first=False):
                for g in range(NPG):
                    page = pool.value_load(ptab_row[0:1, ds(b * NPG + g, 1)], min_val=0, max_val=POOL - 1)
                    if not first:
                        pool.wait_ge(d_pv, b)
                    pool.dma_start(vpages[:, g, :], v_pages[ds(page, 1)].rearrange("g t n -> t (g n)")).then_inc(v_loaded, 16)
                if first:
                    pool.wait_ge(pa_out, NU)
                else:
                    pool.wait_ge(d_pv, b)
                pool.dma_start(mv_in, cache_mem_v[0][ds(b, 1)].rearrange("b (a t) h d -> t (b a) (h d)", t=P)).then_inc(v_loaded, 16)

            load_values(0, True)
            with pool.Fori(0, NB - 1) as i:
                load_values(i + 1)

        @block.scalar
        def _(act):
            act.wait_ge(consts_set, N_CONSTS)
            act.wait_ge(ssq_clear, 1)
            for group in ((0, 1), (2, 3, 4)):
                for n in group:
                    src, m, c = NORM[n]
                    act.wait_ge(tok_in[n], 16)
                    if n:
                        act.wait_ge(ssq_done, n)
                    act.activation(junk[0:m, :], src[0:m], ACT.Square, accum_out=ssq[0:m, c:c + 1]).then_inc(ssq_done, 1)
                for n in group:
                    src, m, c = NORM[n]
                    act.wait_ge(ssq_done, n + 1)
                    act.activation(rstd[0:m, c:c + 1], ssq[0:m, c:c + 1], ACT.Sqrt, bias=eps_t[0:m, :], scale=1.0 / D).then_inc(sqrt_done, 1)
            act.wait_ge(lb_diff, 1)
            act.activation(lbw[:, 2:4, :], lbw[:, 0:2, :], ACT.Exp).then_inc(lb_exp, 1)
            for j in range(8):
                act.wait_ge(blk_filled, j + 1)
                act.activation(mraw[:, j, :], PS[:, j, 0:MEM], ACT.Copy).then_inc(blk_drained, 1)
            with act.Fori(0, 3) as i:
                for n, j in enumerate(ORDER):
                    act.wait_ge(blk_filled, i * 6 + (8 + n + 1))
                    act.activation(raw[:, ds(i * 6 + n, 1), :], PS[:, j:j + 1, 0:T], ACT.Copy).then_inc(blk_drained, 1)
            act.wait_ge(blk_drained, 26)
            with act.Fori(0, 3) as g:
                act.wait_ge(hg_done, g + 1)
                zq, zf = raw[:, ds(g * 2 + HQ, 2), :], raw[:, ds(g * 2 + HFG, 2), :]
                act.activation(gQ, zq, ACT.Sigmoid)
                act.activation(gF, zf, ACT.Sigmoid)
                act.activation(gW[0], zf, ACT.Sigmoid, scale=-1.0)
                act.activation(gV, raw[:, ds(g * 2 + HI, 2), :], ACT.Copy).then_inc(hg_prep, 1)
                for n, j in enumerate(ORDER):
                    act.wait_ge(blk_filled, g * 6 + (26 + n + 1))
                    act.activation(raw[:, ds(g * 6 + (HGT + n), 1), :], PS[:, j:j + 1, 0:T], ACT.Copy).then_inc(blk_drained, 1)

            def block_out(n):
                act.wait_ge(blk_filled, 44 + n + 1)
                act.activation(raw[:, LAST[n], :], PS[:, n % 4, 0:T], ACT.Copy).then_inc(blk_drained, 1)

            act.wait_ge(parity_set, 1)
            act.wait_ge(hg_done, 4)
            for f in range(6):
                t, c, m = f // 2, (f % 2) * 4, 4 - 2 * (f % 2)
                act.wait_ge(vt_filled, f + 1)
                src = PS[:, 6 + f % 2, 0:m * P]
                if t < 2:
                    act.activation(vpar[:, 0, t, c * P:(c + m) * P], src, ACT.Copy, scale=parity[:, 0:1])
                    act.activation(vpar[:, 1, t, c * P:(c + m) * P], src, ACT.Copy, scale=parity[:, 1:2]).then_inc(vt_drained, 1)
                else:
                    act.activation(vsam[:, c * P:(c + m) * P], src[0:NS], ACT.Copy).then_inc(vt_drained, 1)
            block_out(0)
            for h in range(HG):
                act.wait_ge(kt2_filled, h + 1)
                if h:
                    act.wait_ge(ds_filled, 10 * h)
                act.activation(ktil[:, 0:2, :], PS[:, 6, 0:2 * P].rearrange("p (a k) -> p a k", a=2), ACT.Copy)
                act.activation(ktil[0:NS, 2, :], PS[0:NS, 6, 2 * P:3 * P], ACT.Copy).then_inc(kt2_drained, 1)
                if h >= 2:
                    act.wait_ge(gate_done, h - 1)
                act.activation(sq[:, h % 2, :], raw[:, HGT + h, :], ACT.Sigmoid).then_inc(sig_done, 1)
                block_out(h + 1)
            for n in range(7, 10):
                block_out(n)
            act.wait_ge(blk_filled, 55)
            act.wait_ge(wff_in, 32)
            act.activation(ffz[:, :], PS[0:HF, 2, 0:T], ACT.Identity, bias=b_f[:, :]).then_inc(blk_drained, 1)

            act.wait_ge(blk_drained, 55)
            act.wait_ge(gate_done, HG)
            act.wait_ge(o_added, HG)
            for n, (src, w, g) in enumerate(NORMS):
                if n >= 2:
                    act.wait_ge(hn_sum, n - 1)
                act.activation(sq[:, n % 2, 0:w], src, ACT.Square).then_inc(hn_sq, 1)
            act.wait_ge(hn_sum, NN)
            act.activation(hn_r[:, :], PS[0:NN, 0, 0:T], ACT.Sqrt, bias=eps_t[0:NN, :], scale=1.0 / P).then_inc(hn_sqrt, 1)

            act.activation(ffw[:, :], ffz[:, :], ACT.Abs).then_inc(lf_act, 1)
            act.wait_ge(lf_act, 1)
            act.activation(ffw[:, :], ffw[:, :], ACT.Exp, scale=-1.0).then_inc(lf_act, 1)
            act.wait_ge(lf_act, 2)
            act.activation(ffw[:, :], ffw[:, :], ACT.Ln, bias=one_t[0:HF, :]).then_inc(lf_act, 1)

            act.wait_ge(stp_out, 16 * HG)
            for n in range(2):
                act.wait_ge(sts_out[n], 16 * HG // 2)
            for n, (dst, m, srcs) in enumerate(TOKF):
                act.wait_ge(tk_filled, n + 1)
                act.activation(dst, PS[0:m, 2 + n % 2, 0:len(srcs) * P], ACT.Copy).then_inc(tk_drained, 1)
            act.wait_ge(c_filled, 1)
            act.activation(negc[:, :], PS[0:HF, 5, 0:SEQ], ACT.Copy, scale=-1.0).then_inc(negc_set, 1)
            act.wait_ge(dec_filled, 1)
            act.activation(decay[:, :], PS[0:NB * HF, 0:3, :].rearrange("p a b -> p (a b)")[:, 0:KEYS], ACT.Copy).then_inc(decay_set, 1)

            for s in range(NU + 2):
                if s < NU:
                    act.wait_ge(pa_max, s + 1)
                    if s >= 2:
                        act.wait_ge(pa_t, s - 1)
                    act.activation(probs[:, s % 2, 0:width(s)], PS[:, s % 2, 0:width(s)], ACT.Exp, bias=nmax[:, s % 2:s % 2 + 1],
                                   accum_out=psum_p[:, s % 2:s % 2 + 1]).then_inc(pa_exp, 1)
                if s >= 2:
                    fox, h, qb = UNITS[s - 2]
                    act.wait_ge(pa_pv, s - 1)
                    act.activation(cat[:, h if fox else 12 + h, qb * P:(qb + 1) * P], PS[:, 4 + s % 2, 0:P], ACT.Copy).then_inc(pa_out, 1)

            def keys_out(b, u, first=False):
                for g in range(9):
                    bank = 2 * ((u + g) % 2)
                    if g == 0 and not first:
                        act.wait_ge(d_scored, b)
                    act.wait_ge(kt_filled, b * 9 + (g + 1))
                    src = PS[:, bank, :].rearrange("p (h t) -> p h t", t=P)
                    if g < NPG:
                        act.activation(keysT[:, 0:4, g * P:(g + 1) * P], src, ACT.Copy).then_inc(kt_act, 1)
                    else:
                        act.activation(mkeysT[:, 0:2, :], PS[:, bank, :].rearrange("p (h t) -> p h t", t=MEM), ACT.Copy).then_inc(kt_act, 1)

            def decode_exp(b, first=False):
                act.wait_ge(d_max, b + 1)
                if not first:
                    act.wait_ge(d_t, b)
                act.activation(dprob[0:24, :], PS[0:24, 4:7, :].rearrange("p a b -> p (a b)")[:, 0:KEYS], ACT.Exp, bias=nmax[0:24, 2:3],
                               accum_out=psum_p[0:24, 2:3])
                act.activation(mprob[0:16, :], PS[0:16, 6, 64:64 + MEM], ACT.Exp, bias=nmax[0:16, 3:4],
                               accum_out=psum_p[0:16, 3:4]).then_inc(d_exp, 1)

            def decode_out(b):
                act.wait_ge(d_pv, b + 1)
                act.activation(cat[:, 0:HF, ds(b * NL + SEQ, NL)], PS[:, 7, 256:280].rearrange("p (h q) -> p h q", q=NL), ACT.Copy)
                act.activation(cat[:, 12:16, ds(b * NL + SEQ, NL)], PS[:, 7, 280:296].rearrange("p (h q) -> p h q", q=NL), ACT.Copy).then_inc(d_out, 1)

            keys_out(0, 0, True)
            decode_exp(0, True)
            keys_out(1, 1)
            decode_out(0)
            with act.Fori(0, 3) as i:
                for u in range(2):
                    decode_exp(i * 2 + (u + 1))
                    keys_out(i * 2 + (u + 2), u)
                    decode_out(i * 2 + (u + 1))
            decode_exp(NB - 1)
            decode_out(NB - 1)

            for n in range(KC):
                act.wait_ge(wo_filled, n + 1)
                if n >= 2:
                    act.wait_ge(at_filled, n - 1)
                act.activation(attnT[:, n % 2, :], PS[:, n % 2, 0:T], ACT.Copy).then_inc(wo_drained, 1)
            act.wait_ge(h_added, 3 * KC)
            for t, (t0, n) in enumerate(TILES):
                if t:
                    act.wait_ge(h_ssq, t)
                act.activation(h_scaled[0:n, t, :], h_tok[0:n, t, :], ACT.Square, accum_out=ssq[0:n, 5 + t:6 + t]).then_inc(h_ssq, 1)
            act.wait_ge(h_ssq, 3)
            for t, (t0, n) in enumerate(TILES):
                act.activation(rstd[0:n, 5 + t:6 + t], ssq[0:n, 5 + t:6 + t], ACT.Sqrt, bias=eps_t[0:n, :], scale=1.0 / D).then_inc(h_sqrt, 1)
            for n, (o, i) in enumerate(((rw[:, :, 0:NG], rw[:, :, 0:NG]), (rw[:, :, 60:61], rw[:, :, 60:61]))):
                act.wait_ge(rt_sub, n + 1)
                act.activation(o, i, ACT.Exp).then_inc(rt_exp, 1)
            def pair_act(p):
                act.wait_ge(units_used, p * UPP + 4)
                act.activation(hS[:, :], PS[:, 0, :], ACT.Silu).then_inc(pair_silu, 1)
                act.wait_ge(ph_filled, p + 1)
                act.activation(hT.rearrange("p k s -> p (k s)"), PS[:, 6, :], ACT.Copy).then_inc(pair_hT, 1)
                act.wait_ge(g_filled, p + 1)
                act.activation(gate_slot[:, :], PS[:, 7, 0:T], ACT.Copy).then_inc(g_copied, 1)
                for n in (0, 2):
                    act.wait_ge(yst_filled, p * 4 + (n + 1))
                    act.activation(yslot[:, n * 512:(n + 1) * 512], PS[:, YB[n], :], ACT.Copy).then_inc(yst_act, 1)

            act.wait_ge(h_out, 48)
            with act.Fori(0, PAIRS) as p:
                pair_act(p)

            act.wait_ge(overflow_set, 1)
            n_past = act.value_load(overflow[0:1, 0:1], min_val=0, max_val=2 * T)
            with act.If(n_past > 0):
                with act.Fori(0, NE) as e:
                    act.wait_ge(g_filled, e + (PAIRS + 1))
                    act.activation(gbc[:, :], PS[:, 6, 0:T], ACT.Copy).then_inc(g_copied, 1)
                    for j in range(FB):
                        act.wait_ge(mg_filled, e * 4 + (j + 1))
                        act.wait_ge(hs_done, e * 4 + (j + 1))
                        act.activation(g_hS[:, j % 2, :], PS[:, j % 2, 0:T], ACT.Silu).then_inc(pair_silu, 1)

        @block.vector
        def _(dve):
            steps = [0]

            def step(ins):
                steps[0] += 1
                ins.then_inc(dve_step, 1)
                dve.wait_ge(dve_step, steps[0])

            dve.memset(ssq[:, :], 1.0).then_inc(ssq_clear, 1)
            dve.wait_ge(cols_filled, 1)
            dve.tensor_copy(cols[:, :], PS[:, 7, 0:65]).then_inc(cols_set, 1)
            dve.wait_ge(cols_set, 1)
            dve.tensor_scalar(gq[:, 0:1], g_fq, SCALE, None, ALU.mult).then_inc(gains_set, 1)
            dve.tensor_scalar(gq[:, 2:3], g_mq, SCALE, None, ALU.mult).then_inc(gains_set, 1)
            dve.tensor_copy(gq[:, 1:2], g_fk).then_inc(gains_set, 1)
            dve.tensor_copy(gq[:, 3:4], g_mk).then_inc(gains_set, 1)

            dve.tensor_copy(gq[:, 4:5], g_hn).then_inc(gains_set, 1)
            step(dve.tensor_tensor(lbw[:, 2, :], lb0, lb1, ALU.max))
            dve.tensor_tensor(lbw[:, 0, :], lb0, lbw[:, 2, :], ALU.subtract)
            dve.tensor_tensor(lbw[:, 1, :], lb1, lbw[:, 2, :], ALU.subtract).then_inc(lb_diff, 1)

            def drain(f):
                n, c, m = FILLS[f]
                w = NORM[n][1]
                dst, g = (memT, G_MEM) if n < 2 else (xT, G_ATT)
                t0 = (n if n < 2 else n - 2) * P
                dve.wait_ge(tT_filled, f + 1)
                dve.tensor_tensor(dst[:, c:c + m, t0:t0 + w], fill_out(f, w),
                                  g[:, c:c + m].rearrange("p (c a) -> p c a", a=1).to_broadcast([P, m, w]),
                                  ALU.mult).then_inc(tT_drained, 1)

            for n, (src, m, c) in enumerate(NORM):
                dve.wait_ge(sqrt_done, n + 1)
                step(dve.reciprocal(rstd[0:m, c:c + 1], rstd[0:m, c:c + 1]))
                dve.tensor_scalar(src[0:m], src[0:m], rstd[0:m, c:c + 1], None, ALU.mult).then_inc(scaled, 1)
                if n:
                    for f in range(4 * n - 4, 4 * n):
                        drain(f)
            drain(16)

            dve.wait_ge(lfp_filled, 1)
            dve.tensor_copy(lfp[:, :, :, :].rearrange("p g b h -> p h b g"),
                            PS[:, 6, 0:HF * 64].rearrange("p (h b g) -> p h b g", h=HF, b=NB)).then_inc(lfp_drained, 1)
            dve.wait_ge(lfp_drained, 1)
            step(dve.memset(lfs[:, NPG - 1, :, :], 0.0))
            for g in range(NPG - 2, -1, -1):
                step(dve.tensor_tensor(lfs[:, g, :, :], lfs[:, g + 1, :, :], lfp[:, g + 1, :, :], ALU.add))
            dve.wait_ge(lb_exp, 1)
            step(dve.tensor_tensor(lbw[:, 0, :], lbw[:, 2, :], lbw[:, 3, :], ALU.add))
            step(dve.reciprocal(lbw[:, 1, :], lbw[:, 0, :]))
            dve.tensor_tensor(LB, lbw[:, 2, :], lbw[:, 1, :], ALU.mult).then_inc(lb_set, 1)
            dve.tensor_tensor(LB1, lbw[:, 3, :], lbw[:, 1, :], ALU.mult).then_inc(lb_set, 1)
            for n in range(2):
                dve.tensor_reduce(parity[:, n:n + 1], chunk_of[:, :].rearrange("p (a b) -> p b a", b=2)[:, n, :], AX.X, ALU.add)
            dve.memset(nmax[:, :], 0.0).then_inc(parity_set, 1)
            dve.memset(psum_p[:, 0:1], 0.0).then_inc(hg_done, 1)
            dve.memset(psum_p[:, 1:2], 0.0).then_inc(intra_used, 1)
            dve.wait_ge(lb_set, 2)

            def pr(a):
                return a[:, :, 0:SEQ].rearrange("p h (n t) -> p h n t", t=CH)

            def sa(a):
                return a[:, :, SEQ:T].rearrange("p h (n t) -> p h n t", t=NL)

            def packed(buf, j):
                return buf.rearrange("p h t -> p (h t)")[:, 0:2 * NCH * (CH - j)].rearrange("p (h n t) -> p h n t", h=2, n=NCH)

            S_OFF = [0, 64, 112, 144]

            def spacked(a, j):
                return a[:, S_OFF[j]:S_OFF[j] + 16 * (NL - j)].rearrange("p (h n t) -> p h n t", h=2, n=NB)

            with dve.Fori(0, 3) as g:
                n_step = 0

                def gstep(ins):
                    nonlocal n_step
                    n_step += 1
                    ins.then_inc(hg_step, 1)
                    dve.wait_ge(hg_step, g * G_STEPS + n_step)

                hg = ds(g * 2, 2)
                lb1b = lbw[:, 5, hg].rearrange("p (h a) -> p h a", a=1).to_broadcast([P, 2, T])
                lbb = lbw[:, 4, hg].rearrange("p (h a) -> p h a", a=1).to_broadcast([P, 2, T])
                dve.wait_ge(hg_prep, g + 1)
                dve.scalar_tensor_tensor(out=gQ, in0=raw[:, ds(g * 2 + HQ, 2), :], scalar=SCALE, in1=gQ, op0=ALU.mult, op1=ALU.mult)
                dve.tensor_tensor(gW[0], gW[0], lb1b, ALU.mult)
                gstep(dve.tensor_tensor(gF, gF, lb1b, ALU.mult))
                gstep(dve.tensor_tensor(gF, gF, lbb, ALU.add))

                def add_distance(j):
                    dve.wait_ge(intra_filled, g * 17 + (j + 1))
                    o = gO if j == 0 else gTmp
                    dve.tensor_tensor(pr(o)[:, :, :, j:CH], packed(PS[:, 6 + j % 2, :].rearrange("p (h t) -> p h t", h=2), j),
                                      pr(gV)[:, :, :, 0:CH - j], ALU.mult).then_inc(intra_used, 1)
                    dve.wait_ge(intra_used, g * 17 + (j + 2))
                    if j:
                        gstep(dve.tensor_tensor(pr(gO)[:, :, :, j:CH], pr(gO)[:, :, :, j:CH], pr(gTmp)[:, :, :, j:CH], ALU.add))

                for j in range(CH):
                    w, w0 = gW[j % 2], gW[(j + 1) % 2]
                    if j:
                        if j < NL:
                            dve.tensor_tensor(sa(w)[:, :, :, j:NL], sa(gF)[:, :, :, j:NL], sa(w0)[:, :, :, j - 1:NL - 1], ALU.mult)
                        gstep(dve.tensor_tensor(pr(w)[:, :, :, j:CH], pr(gF)[:, :, :, j:CH], pr(w0)[:, :, :, j - 1:CH - 1], ALU.mult))
                    dve.tensor_copy(pr(gKT)[:, :, :, CH - 1 - j:CH - j], pr(w)[:, :, :, CH - 1:CH])
                    if j < NL:
                        dve.tensor_copy(sa(gKT)[:, :, :, NL - 1 - j:NL - j], sa(w)[:, :, :, NL - 1:NL])
                        dve.tensor_tensor(spacked(gS, j), sa(gQ)[:, :, :, j:NL], sa(w)[:, :, :, j:NL], ALU.mult)
                    if j >= 2:
                        dve.wait_ge(intra_filled, g * 17 + (j - 1))
                    dve.tensor_tensor(packed(gQW[j % 2], j), pr(gQ)[:, :, :, j:CH], pr(w)[:, :, :, j:CH], ALU.mult).then_inc(qw_ready, 1)
                    if j:
                        add_distance(j - 1)
                add_distance(CH - 1)
                dve.wait_ge(intra_filled, g * 17 + 17)
                for j in range(NL):
                    o = gO if j == 0 else gTmp
                    ins = dve.tensor_tensor(sa(o)[:, :, :, j:NL], spacked(PS[:, 6, :], j), sa(gV)[:, :, :, 0:NL - j], ALU.mult)
                    if j == NL - 1:
                        ins.then_inc(intra_used, 1)
                        dve.wait_ge(intra_used, g * 17 + 18)
                    else:
                        gstep(ins)
                    if j:
                        gstep(dve.tensor_tensor(sa(gO)[:, :, :, j:NL], sa(gO)[:, :, :, j:NL], sa(gTmp)[:, :, :, j:NL], ALU.add))
                keep, start = gW
                gstep(dve.tensor_copy(keep, gF))
                gstep(dve.memset(start, 0.0))
                for v in (pr, sa):
                    dve.memset(v(keep)[:, :, :, 0:1], 0.0)
                    ins = dve.tensor_copy(v(start)[:, :, :, 0:1], v(gF)[:, :, :, 0:1])
                gstep(ins)
                flat = [a.rearrange("p h t -> p (h t)") for a in (gTmp, keep, start)]
                gstep(dve.tensor_tensor_scan(flat[0], flat[1], flat[2], 0.0, ALU.mult, ALU.add))
                dve.tensor_tensor(raw[:, ds(g * 2 + HQ, 2), :], gQ, gTmp, ALU.mult)
                dve.tensor_copy(decays[:, hg, 0:NCH], pr(gTmp)[:, :, :, CH - 1])
                dve.tensor_copy(decays[:, hg, NCH:NCH + NB], sa(gTmp)[:, :, :, NL - 1])
                dve.tensor_copy(raw[:, ds(g * 2 + HFG, 2), :], gKT)
                dve.tensor_copy(cat[:, ds(g * 2 + 6, 2), :], gO).then_inc(hg_done, 1)
                assert n_step == G_STEPS, n_step

            dve.wait_ge(hg_done, 4)
            n_st = 0

            def ststep(ins):
                nonlocal n_st
                n_st += 1
                ins.then_inc(st_step, 1)
                dve.wait_ge(st_step, n_st)

            def add_inter(h):
                dve.wait_ge(oi_filled, h + 1)
                o = cat[:, 6 + h, CH:T]
                dve.tensor_tensor(o, o, PS[:, 7, CH:T], ALU.add).then_inc(o_added, 1)

            for h in range(HG):
                if h:
                    add_inter(h - 1)
                for c in range(8):
                    dve.wait_ge(ds_filled, 10 * h + c + 1)
                    if c == 7 and h:
                        dve.wait_ge(stp_out, 16 * h)
                    for n in (2 * c, 2 * c + 1):
                        d = PS[:, 4 + c % 2, (n % 2) * P:(n % 2 + 1) * P]
                        if n == 0:
                            ins = dve.tensor_copy(states[:, 0, :], d)
                        else:
                            ins = dve.scalar_tensor_tensor(out=states[:, n, :], in0=states[:, n - 1, :], scalar=decays[:, h, n:n + 1],
                                                           in1=d, op0=ALU.mult, op1=ALU.add)
                        if n % 2 == 0:
                            ststep(ins)
                        else:
                            ins.then_inc(ds_used, 1)
                            dve.wait_ge(ds_used, 10 * h + c + 1)
                dve.wait_ge(os_filled, h + 1)
                for c in range(2):
                    sn = s_in[h % 2][:, 4 * c:4 * c + 4, :]
                    ststep(dve.tensor_tensor(sn, sn, decays[:, h, NCH + 4 * c:NCH + 4 * c + 4].rearrange("p (b a) -> p b a", a=1)
                                             .to_broadcast([P, 4, P]), ALU.mult))
                    dve.wait_ge(ds_filled, 10 * h + 9 + c)
                    dve.tensor_tensor(sn, sn, PS[:, 4 + c % 2, :].rearrange("p (b v) -> p b v", b=4), ALU.add).then_inc(ds_used, 1)
                dve.wait_ge(sig_done, h + 1)
                dve.tensor_tensor(raw[:, HGT + h, :], raw[:, HGT + h, :], sq[:, h % 2, :], ALU.mult).then_inc(gate_done, 1)
            add_inter(HG - 1)
            dve.memset(psum_p[:, :], 0.0).then_inc(lfs_done, 1)

            dve.wait_ge(gains_set, 5)
            dve.wait_ge(hn_sqrt, 1)
            dve.reciprocal(hn_r[:, :], hn_r[:, :]).then_inc(hn_rcp, 1)
            for n, (src, w, g) in enumerate(NORMS):
                dve.wait_ge(hn_rows, n + 1)
                dve.scalar_tensor_tensor(out=src, in0=src, scalar=gq[:, g:g + 1], in1=PS[:, 1 + n % 3, 0:w],
                                         op0=ALU.mult, op1=ALU.mult).then_inc(hn_done, 1)
                if n >= NN - HG:
                    dve.wait_ge(hn_done, n + 1)
                    h = n - (NN - HG)
                    step(dve.tensor_tensor(cat[:, 6 + h, :], cat[:, 6 + h, :], raw[:, HGT + h, :], ALU.mult))

            dve.wait_ge(lf_act, 3)
            dve.scalar_tensor_tensor(out=lfT[:, :], in0=ffz[:, :], scalar=0.0, in1=ffw[:, :],
                                     op0=ALU.min, op1=ALU.subtract).then_inc(lf_done, 1)
            dve.wait_ge(lft_filled, 1)
            step(dve.tensor_copy(lftok[:, 0:2, :], PS[:, 4, 0:2 * HF].rearrange("p (t h) -> p t h", h=HF)))
            dve.tensor_copy(lftok[0:NS, 2, :], PS[0:NS, 4, 2 * HF:3 * HF]).then_inc(lft_drained, 1)
            dve.wait_ge(lft_drained, 1)
            dve.tensor_tensor(lfm[:, :, :], lftok[0:NS, 2:3, :].to_broadcast([NS, NB, HF]),
                              batch_of[:, :].rearrange("p (b a) -> p b a", a=1).to_broadcast([NS, NB, HF]),
                              ALU.mult).then_inc(lfm_done, 1)

            for s in range(NU + 2):
                if 1 <= s <= NU:
                    u = s - 1
                    dve.wait_ge(pa_exp, u + 1)
                    step(dve.reciprocal(psum_p[:, u % 2:u % 2 + 1], psum_p[:, u % 2:u % 2 + 1]))
                    dve.tensor_scalar(probs[:, u % 2, 0:width(u)], probs[:, u % 2, 0:width(u)], psum_p[:, u % 2:u % 2 + 1], None,
                                      ALU.mult).then_inc(pa_prob, 1)
                if s >= 2:
                    u = s - 2
                    dve.wait_ge(pa_t, u + 1)
                    if u >= 2:
                        dve.wait_ge(pa_pv, u - 1)
                    dve.tensor_copy(probsT[:, u % 2, 0:width(u) // P, :],
                                    PS[:, 2 + u % 2, 0:width(u)].rearrange("p (a q) -> p a q", q=P)).then_inc(pa_tc, 1)
                if s < NU:
                    dve.wait_ge(pa_scored, s + 1)
                    if s >= 2:
                        dve.wait_ge(pa_exp, s - 1)
                    dve.tensor_reduce(nmax[:, s % 2:s % 2 + 1], PS[:, s % 2, 0:width(s)], AX.X, ALU.max, negate=True).then_inc(pa_max, 1)

            dve.memset(q_rows[:, :], 0.0).then_inc(q_clear, 1)
            dve.memset(mq_rows[:, :], 0.0).then_inc(q_clear, 1)
            dve.wait_ge(q_clear, 2)

            def queries(b, first=False):
                if not first:
                    dve.wait_ge(d_scored, b)
                q = ds(b * NL + SEQ, NL)
                dve.tensor_copy(q_rows[:, :].rearrange("p (h c) -> p h c", c=28)[:, :, 0:NL], raw[:, FQ:FQ + HF, q])
                dve.tensor_copy(mq_rows[:, :].rearrange("p (h c) -> p h c", c=20)[:, :, 0:NL], raw[:, MQ:MQ + HM, q])
                dve.tensor_copy(causal_b.rearrange("p (a k) -> p a k", a=1), causal4[:, ds(b, 1), :])
                dve.tensor_copy(sel_b[:, :].rearrange("p (a h q) -> p a h q", a=1, q=NL), sel48[:, ds(b, 1), :, :]).then_inc(q_set, 1)

            def keys_out(b, u, gs):
                for g in gs:
                    bank = 2 * ((u + g) % 2) + 1
                    dve.wait_ge(kt_filled, b * 9 + (g + 1))
                    if g < NPG:
                        dve.tensor_copy(keysT[:, 4:6, g * P:(g + 1) * P],
                                        PS[:, bank, 0:2 * P].rearrange("p (h t) -> p h t", t=P)).then_inc(kt_dve, 1)
                    else:
                        dve.tensor_copy(mkeysT[:, 2:4, :], PS[:, bank, :].rearrange("p (h t) -> p h t", t=MEM)).then_inc(kt_dve, 1)

            def decode_max(b):
                dve.wait_ge(d_scored, b + 1)
                dve.tensor_reduce(nmax[0:24, 2:3], PS[0:24, 4:7, :].rearrange("p a b -> p (a b)")[:, 0:KEYS], AX.X, ALU.max, negate=True)
                dve.tensor_reduce(nmax[0:16, 3:4], PS[0:16, 6, 64:64 + MEM], AX.X, ALU.max, negate=True).then_inc(d_max, 1)

            def decode_norm(b):
                dve.wait_ge(d_exp, b + 1)
                dve.reciprocal(psum_p[0:24, 2:3], psum_p[0:24, 2:3])
                dve.reciprocal(psum_p[0:16, 3:4], psum_p[0:16, 3:4]).then_inc(d_rcp, 1)
                dve.wait_ge(d_rcp, b + 1)
                dve.tensor_scalar(dprob[0:24, :], dprob[0:24, :], psum_p[0:24, 2:3], None, ALU.mult)
                dve.tensor_scalar(mprob[0:16, :], mprob[0:16, :], psum_p[0:16, 3:4], None, ALU.mult).then_inc(d_prob, 1)

            def probs_out(b, first=False):
                dve.wait_ge(d_t, b + 1)
                if not first:
                    dve.wait_ge(d_pv, b)
                dve.tensor_copy(dprobT[:, 0:224], PS[:, 7, 0:224])
                dve.tensor_copy(npT, PS[0:NS, 7, 224:248]).then_inc(d_tc, 1)

            queries(0, True)
            keys_out(0, 0, range(9))
            decode_max(0)
            queries(1)
            keys_out(1, 1, range(2))
            decode_norm(0)
            keys_out(1, 1, range(2, 9))
            probs_out(0, True)
            with dve.Fori(0, 3) as i:
                for u in range(2):
                    decode_max(i * 2 + (u + 1))
                    queries(i * 2 + (u + 2))
                    keys_out(i * 2 + (u + 2), u, range(2))
                    decode_norm(i * 2 + (u + 1))
                    keys_out(i * 2 + (u + 2), u, range(2, 9))
                    probs_out(i * 2 + (u + 1))
            decode_max(NB - 1)
            decode_norm(NB - 1)
            probs_out(NB - 1)

            dve.wait_ge(x_again, 48)
            for n in range(KC):
                for t, (t0, w) in enumerate(TILES):
                    dve.wait_ge(at_filled, n + 1)
                    o = h_tok[0:w, t, n * P:(n + 1) * P]
                    dve.tensor_tensor(o, o, PS[0:w, 2 + n % 2, t * P:(t + 1) * P], ALU.add).then_inc(h_added, 1)
            dve.wait_ge(h_added, 3 * KC)
            for t, (t0, w) in enumerate(TILES):
                dve.wait_ge(h_sqrt, t + 1)
                step(dve.reciprocal(rstd[0:w, 5 + t:6 + t], rstd[0:w, 5 + t:6 + t]))
                dve.tensor_scalar(h_scaled[0:w, t, :], h_tok[0:w, t, :], rstd[0:w, 5 + t:6 + t], None, ALU.mult).then_inc(h_scl, 1)
                for f in range(HT_FILLS):
                    ft, c, m = HTF[f]
                    if ft == t:
                        dve.wait_ge(ht_filled, f + 1)
                        dve.tensor_tensor(xnT[:, c:c + m, t0:t0 + w], ht_out(f),
                                          G_FFN[:, c:c + m].rearrange("p (c a) -> p c a", a=1).to_broadcast([P, m, w]),
                                          ALU.mult).then_inc(ht_drained, 1)

            step(dve.memset(logits[:, :, :], 0.0))
            dve.memset(gates[:, :, :], 0.0)
            dve.wait_ge(lg_filled, 3)
            for t, (t0, w) in enumerate(TILES):
                ins = dve.tensor_copy(logits[0:w, t, :], PS[0:w, 4, t * 64:t * 64 + NG + NE])
            step(ins)
            gl = logits[:, :, 0:NG]
            el = logits[:, :, NG:NG + NE].rearrange("p t (g e) -> p t g e", g=NG)

            def bc(a, n):
                return a.to_broadcast([P, 3, n])

            first = rw[:, :, 40:48]
            for n in range(EPG):
                ins = dve.memset(first[:, :, n:n + 1], float(EPG - n))
            step(ins)

            def one_hot(out, x, m, tmp):
                n = x.shape[2]
                step(dve.tensor_reduce(m, x, AX.X, ALU.max))
                step(dve.tensor_tensor(out, x, bc(m, n), ALU.is_equal))
                step(dve.tensor_tensor(out, out, first[:, :, 0:n], ALU.mult))
                step(dve.tensor_reduce(tmp, out, AX.X, ALU.max))
                step(dve.tensor_tensor(out, out, bc(tmp, n), ALU.is_equal))

            gm, g1, e_in, m1, o1, m2, o2, tmp = (rw[:, :, a:b] for a, b in
                                                 ((48, 49), (4, 8), (8, 16), (49, 50), (16, 24), (50, 51), (24, 32), (51, 52)))
            ge, e2, dd, ga, gb, gsum = (rw[:, :, a:b] for a, b in ((0, 4), (32, 40), (60, 61), (61, 62), (62, 63), (52, 53)))
            one_hot(g1, gl, gm, tmp)
            dve.tensor_tensor(ge, gl, bc(gm, NG), ALU.subtract).then_inc(rt_sub, 1)
            picked = choice[:, :, 0, :].rearrange("p t (g e) -> p t g e", g=NG)
            step(dve.tensor_tensor(picked, el, g1.rearrange("p t (g a) -> p t g a", a=1).to_broadcast([P, 3, NG, EPG]), ALU.mult))
            step(dve.tensor_reduce(e_in, picked.rearrange("p t g e -> p t e g"), AX.X, ALU.add))
            one_hot(o1, e_in, m1, tmp)
            step(dve.scalar_tensor_tensor(out=e2, in0=o1, scalar=NEG, in1=e_in, op0=ALU.mult, op1=ALU.add))
            one_hot(o2, e2, m2, tmp)
            dve.tensor_tensor(dd, m2, m1, ALU.subtract).then_inc(rt_sub, 1)
            dve.wait_ge(rt_exp, 2)
            step(dve.tensor_reduce(gsum, ge, AX.X, ALU.add))
            step(dve.tensor_scalar(ga, dd, 1.0, None, ALU.add))
            step(dve.tensor_tensor(ga, ga, gsum, ALU.mult))
            step(dve.reciprocal(ga, ga))
            step(dve.tensor_tensor(gb, ga, dd, ALU.mult))
            for n, o in enumerate((o1, o2)):
                c = choice[:, :, n, :].rearrange("p t (g e) -> p t g e", g=NG)
                for g in range(NG):
                    ins = dve.tensor_tensor(c[:, :, g, :], o, bc(g1[:, :, g:g + 1], EPG), ALU.mult)
            step(ins)
            step(dve.tensor_tensor(c1g, choice[:, :, 0, :], bc(ga, NE), ALU.mult))
            step(dve.tensor_tensor(rw[:, :, 0:NE], choice[:, :, 1, :], bc(gb, NE), ALU.mult))
            for t, (t0, w) in enumerate(TILES):
                ins = dve.tensor_tensor(gates[0:w, t, :], c1g[0:w, t, :], rw[0:w, t, 0:NE], ALU.add)
            ins.then_inc(gates_set, 1)
            dve.wait_ge(gates_set, 1)
            chosen = rw[:, :, NE:2 * NE]
            dve.tensor_tensor(chosen, choice[:, :, 0, :], choice[:, :, 1, :], ALU.add).then_inc(y_clear, 1)
            dve.memset(yT, 0.0).then_inc(y_clear, 1)
            dve.memset(over[:, :, :], 0.0)
            step(dve.memset(slot_of[:, :, :], 0.0))
            dve.wait_ge(y_clear, 2)
            dve.wait_ge(rank_filled, 1)
            dve.tensor_copy(iota1, PS[:, 5, 128:128 + SLOTS])
            for t, (t0, w) in enumerate(TILES):
                ins = dve.tensor_tensor(slot_of[0:w, t, :], chosen[0:w, t, :], PS[0:w, 5, t * NE:(t + 1) * NE], ALU.mult)
            ins.then_inc(slots_set, 1)
            dve.wait_ge(slots_set, 1)

            def pick_pair(p):
                for t in range(3):
                    ins = dve.tensor_tensor(pick_tok[:, t, :, :], iota1.rearrange("p (a s) -> p a s", a=1).to_broadcast([P, 2, SLOTS]),
                                            slot_of[:, t, ds(p * 2, 2)].rearrange("p (x a) -> p x a", a=1).to_broadcast([P, 2, SLOTS]),
                                            ALU.is_equal)
                ins.then_inc(picked_set, 1)

            def gathered_out(p):
                for c in range(4):
                    dve.wait_ge(xg_filled, p * 4 + (c + 1))
                    dve.tensor_tensor(xgT[:, 4 * c:4 * c + 4, :], PS[:, 2 + c, :].rearrange("p (c s) -> p c s", s=2 * SLOTS),
                                      G_FFN[:, 4 * c:4 * c + 4].rearrange("p (c a) -> p c a", a=1).to_broadcast([P, 4, 2 * SLOTS]),
                                      ALU.mult).then_inc(xg_drained, 1)

            def pair_dve(p, first=False, last=False):
                if not first:
                    dve.wait_ge(g_filled, p)
                dve.wait_ge(picked_set, p + 1)
                for t in range(3):
                    ins = dve.tensor_tensor(pick_gate[:, t, :, :], pick_tok[:, t, :, :],
                                            gates[:, t, ds(p * 2, 2)].rearrange("p (x a) -> p x a", a=1).to_broadcast([P, 2, SLOTS]), ALU.mult)
                ins.then_inc(pg_set, 1)
                if not last:
                    dve.wait_ge(pg_set, p + 1)
                    pick_pair(p + 1)
                dve.wait_ge(pair_silu, p + 1)
                dve.wait_ge(units_used, p * UPP + 8)
                dve.tensor_tensor(hS[:, :], hS[:, :], PS[:, 1, :], ALU.mult).then_inc(pair_h, 1)
                if not last:
                    gathered_out(p + 1)
                for n in (1, 3):
                    dve.wait_ge(yst_filled, p * 4 + (n + 1))
                    dve.tensor_copy(yslot[:, n * 512:(n + 1) * 512], PS[:, YB[n], :]).then_inc(yst_dve, 1)
                for n in range(KC):
                    dve.wait_ge(part_filled, p * KC + (n + 1))
                    dve.tensor_tensor(yT[:, n, :], yT[:, n, :], PS[:, 2 + n % 4, 0:T], ALU.add).then_inc(part_added, 1)

            pick_pair(0)
            step(dve.tensor_scalar(over, slot_of, float(SLOTS), None, ALU.is_gt))
            step(dve.tensor_reduce(n_over[:, 0:1], over.rearrange("p t e -> p (t e)"), AX.X, ALU.add))
            dve.tensor_tensor(over, over, gates, ALU.mult).then_inc(slots_set, 1)
            dve.wait_ge(over_filled, 1)
            dve.tensor_copy(overflow[:, :], PS[:, 6, 0:1]).then_inc(overflow_set, 1)
            dve.wait_ge(h_out, 48)
            gathered_out(0)
            pair_dve(0, first=True)
            with dve.Fori(0, PAIRS - 2) as i:
                pair_dve(i + 1)
            pair_dve(PAIRS - 1, last=True)

            dve.wait_ge(h_again, 48)
            dve.wait_ge(overflow_set, 1)
            n_past = dve.value_load(overflow[0:1, 0:1], min_val=0, max_val=2 * T)
            with dve.If(n_past > 0):
                dve.wait_ge(part_added, PAIRS * KC)
                for t, (t0, w) in enumerate(TILES):
                    dve.tensor_scalar(g_scaled[0:w, t, :], h_back[0:w, t, :], rstd[0:w, 5 + t:6 + t], None, ALU.mult).then_inc(h_scl, 1)
                for f in range(HT_FILLS):
                    t, c, m = HTF[f]
                    t0, w = TILES[t]
                    dve.wait_ge(ht_filled, HT_FILLS + f + 1)
                    dve.tensor_tensor(g_xnT[:, c:c + m, t0:t0 + w], ht_out(f),
                                      G_FFN[:, c:c + m].rearrange("p (c a) -> p c a", a=1).to_broadcast([P, m, w]),
                                      ALU.mult).then_inc(ht_drained, 1)
                for n, s in enumerate((hs_done, md_filled)):
                    dve.memset(rw[:, :, n:n + 1], 0.0).then_inc(s, 1)
                with dve.Fori(0, NE) as e:
                    dve.wait_ge(g_filled, e + PAIRS)
                    dve.tensor_copy(gcol[:, :, :], over[:, :, ds(e, 1)].to_broadcast([P, 3, P])).then_inc(gcol_set, 1)
                    dve.wait_ge(g_copied, e + (PAIRS + 1))
                    for j in range(FB):
                        dve.wait_ge(mu_filled, e * 4 + (j + 1))
                        dve.wait_ge(pair_silu, e * 4 + (PAIRS + j + 1))
                        dve.tensor_tensor(g_hS[:, j % 2, :], g_hS[:, j % 2, :], PS[:, 2 + j % 2, 0:T], ALU.mult).then_inc(hs_done, 1)
                        dve.wait_ge(hs_done, e * 4 + (j + 2))
                        dve.wait_ge(md_filled, e * 16 + 1)
                        dve.tensor_tensor(g_hT[:, j, :], g_hS[:, j % 2, :], gbc[:, :], ALU.mult).then_inc(pair_hT, 1)
                    for n in range(KC):
                        dve.wait_ge(md_filled, e * 16 + (n + 2))
                        dve.tensor_tensor(yT[:, n, :], yT[:, n, :], PS[:, 4 + n % 2, 0:T], ALU.add).then_inc(part_added, 1)
            for t, (t0, w) in enumerate(TILES):
                for c in range(4):
                    f = 4 * t + c
                    dve.wait_ge(yt_filled, f + 1)
                    o = h_back[0:w, t, c * 512:(c + 1) * 512]
                    dve.tensor_tensor(o, o, PS[0:w, f % 2, :], ALU.add).then_inc(y_done, 1)

        @block.tensor
        def _(pe):
            pe.wait_ge(consts_set, N_CONSTS)
            pe.wait_ge(rows_in, 144)
            pe.transpose(PS[:, 7, 0:65], rows[:, :], ident[0:65, 0:65]).then_inc(cols_filled, 1)
            pe.wait_ge(cols_set, 1)
            for f, (n, c, m) in enumerate(FILLS):
                src, w, _ = NORM[n]
                pe.wait_ge(scaled, n + 1)
                if f >= 8:
                    pe.wait_ge(tT_drained, f - 7)
                for a in range(m):
                    last = pe.transpose(fill_out(f, w)[:, a, :], src[0:w, (c + a) * P:(c + a + 1) * P], ident[0:w, 0:w])
                last.then_inc(tT_filled, 1)

            def project(bank, w, rhs, wt, c, m=P, between=None):
                for k in range(KC):
                    last = pe.matmul(PS[0:m, bank, 0:w], wt[:, k, c:c + m], rhs[:, k, :], start=(k == 0), stop=(k == KC - 1))
                    if between is not None and k < KC - 1:
                        between(k)
                last.then_inc(blk_filled, 1)

            pe.wait_ge(tT_drained, 17)
            pe.wait_ge(lfpages_in, 16)
            pages_h = lfpages.rearrange("g (t h) -> g h t", h=HF)
            for h in range(HF):
                last = pe.transpose(PS[:, 6, h * 64:(h + 1) * 64], pages_h[:, h, :], ident[0:64, 0:64])
            last.then_inc(lfp_filled, 1)

            pe.wait_ge(lfp_drained, 1)
            for j in range(8):
                if j % 3 == 0:
                    pe.wait_ge(w_in_slot[(j // 3) % 2], 16 * (1 + j // 6))
                project(j, MEM, memT, wslot[(j // 3) % 2], (j % 3) * P)
            pe.wait_ge(blk_drained, 8)
            with pe.Fori(0, 3) as i:
                for half in (1, 0):
                    pe.wait_ge(w_in_slot[half], i * 16 + (48 - 16 * half))
                    for n in range(3):
                        pe.wait_ge(blk_drained, i * 6 + (ORDER.index(3 * half + n) + 3))
                        project(3 * half + n, T, xT, wslot[half], n * P)

            def intra(g, j):
                pe.wait_ge(qw_ready, g * CH + min(j + 1, CH))
                pe.wait_ge(intra_used, g * 17 + max(j, 1))
                rhs = gQW[j % 2].rearrange("p h t -> p (h t)")[:, 0:2 * NCH * (CH - j)] if j < CH else gS
                pe.matmul(PS[:, 6 + j % 2, 0:rhs.shape[1]], ones[:, :], rhs, start=True, stop=True).then_inc(intra_filled, 1)

            with pe.Fori(0, 3) as g:
                for half in (1, 0):
                    pe.wait_ge(w_in_slot[half], g * 16 + (48 + 48 - 16 * half))
                    for n in range(3):
                        b = ORDER.index(3 * half + n)
                        pe.wait_ge(blk_drained, g * 6 + (18 + b + 3))

                        def between(k, b=b):
                            at = {3: 0, 7: 1, 11: 2, 13: 3}.get(k)
                            if b and at is not None and (at < 3 or b >= 4):
                                intra(g, 3 * (b - 1) + max(b - 4, 0) + at)

                        project(3 * half + n, T, xT, wslot[half], n * P, between=between)

            def values_by_token(f):
                t, c, m = f // 2, (f % 2) * 4, 4 - 2 * (f % 2)
                t0, w = TILES[t]
                if f >= 2:
                    pe.wait_ge(vt_drained, f - 1)
                for a in range(m):
                    last = pe.transpose(PS[0:w, 6 + f % 2, a * P:(a + 1) * P], raw[:, HI + c + a, t0:t0 + w], ident[:, :])
                last.then_inc(vt_filled, 1)

            def keys_by_token(h):
                if h:
                    pe.wait_ge(kt2_drained, h)
                else:
                    pe.wait_ge(vt_drained, 6)
                for t, (t0, w) in enumerate(TILES):
                    last = pe.transpose(PS[0:w, 6, t * P:(t + 1) * P], raw[:, HFG + h, t0:t0 + w], ident[:, :])
                last.then_inc(kt2_filled, 1)

            def state_parts(h, c):
                q = 10 * h + c
                if q >= 2:
                    pe.wait_ge(ds_used, q - 1)
                if c == 0:
                    pe.wait_ge(kt2_drained, h + 1)
                if c < 8:
                    t, r = c // 4, 32 * (c % 4)
                    last = pe.matmul(PS[:, 4 + q % 2, 0:2 * P].rearrange("p (a v) -> p a v", a=2), ktil[r:r + 32, t, :],
                                     vpar[r:r + 32, :, t, h * P:(h + 1) * P], start=True, stop=True)
                else:
                    pe.wait_ge(sm_set, 2 * h + c - 7)
                    last = pe.matmul(PS[:, 4 + q % 2, :], ktil[0:NS, 2, :], vmask[c - 8].rearrange("p b v -> p (b v)"),
                                     start=True, stop=True)
                last.then_inc(ds_filled, 1)

            def inter_sample(h):
                pe.wait_ge(s_loaded[h % 2], 16 * (h // 2 + 1))
                if h:
                    pe.wait_ge(o_added, h)
                for b in range(NB):
                    c = SEQ + b * NL
                    last = pe.matmul(PS[:, 7, c:c + NL], s_in[h % 2][:, b, :], raw[:, HQ + h, c:c + NL], start=True, stop=True)
                last.then_inc(os_filled, 1)

            def inter_prompt(h):
                pe.wait_ge(ds_used, 10 * h + 8)
                for n in range(1, NCH):
                    last = pe.matmul(PS[:, 7, n * CH:(n + 1) * CH], states[:, n - 1, :], raw[:, HQ + h, n * CH:(n + 1) * CH],
                                     start=True, stop=True)
                last.then_inc(oi_filled, 1)

            def last_block(n):
                def between(k):
                    if n == 0 and 2 <= k < 14 and k % 2 == 0:
                        if k == 2:
                            pe.wait_ge(hg_done, 4)
                        values_by_token(k // 2 - 1)
                    h = n - 1
                    if 0 < h <= HG and k == 0:
                        inter_prompt(h - 1)
                    if 0 <= h < HG:
                        if k == 2:
                            keys_by_token(h)
                        if 4 <= k < 14:
                            state_parts(h, k - 4)
                        if k == 8:
                            inter_sample(h)
                if n < 4:
                    pe.wait_ge(blk_drained, 44)
                else:
                    pe.wait_ge(blk_drained, 44 + n - 3)
                if n in (0, 3):
                    pe.wait_ge(w_in_slot[1 - n // 3], 96 + 48 - 16 * (1 - n // 3))
                    slot = 1 - n // 3
                if n in (6, 8):
                    slot = (8 - n) // 2
                    pe.wait_ge(w_in_slot[slot], 144 + 16 * (1 - slot))
                slot, c = [(1, n), (0, n - 3), (1, n - 6), (0, n - 8)][(n >= 3) + (n >= 6) + (n >= 8)]
                project(n % 4, T, xT, wslot[slot], c * P, between=between)

            for n in range(10):
                last_block(n)
            pe.wait_ge(wff_in, 32)
            pe.wait_ge(blk_drained, 51)
            project(2, T, xT, w_ff, 0, HF)

            for n, (src, w, g) in enumerate(NORMS):
                pe.wait_ge(hn_sq, n + 1)
                pe.matmul(PS[0:NN, 0, 0:w], row_of[:, NN - 1 - n:2 * NN - 1 - n], sq[:, n % 2, 0:w], start=(n == 0), stop=(n == NN - 1)).then_inc(hn_sum, 1)
            pe.wait_ge(hn_rcp, 1)
            for n, (src, w, g) in enumerate(NORMS):
                if n >= 3:
                    pe.wait_ge(hn_done, n - 2)
                pe.matmul(PS[:, 1 + n % 3, 0:w], ident[0:NN, n:n + 1].to_broadcast([NN, P]), hn_r[:, 0:w], start=True, stop=True).then_inc(hn_rows, 1)

            pe.wait_ge(lf_done, 1)
            for t, (t0, n) in enumerate(TILES):
                last = pe.transpose(PS[0:n, 4, t * HF:(t + 1) * HF], lfT[:, t0:t0 + n], ident[0:HF, 0:HF])
            last.then_inc(lft_filled, 1)
            pe.wait_ge(hn_done, NN)
            for n, (dst, m, srcs) in enumerate(TOKF):
                if n >= 2:
                    pe.wait_ge(tk_drained, n - 1)
                for a, s in enumerate(srcs):
                    last = pe.transpose(PS[0:m, 2 + n % 2, a * P:(a + 1) * P], s, ident[:, :])
                last.then_inc(tk_filled, 1)
            pe.wait_ge(lft_drained, 1)
            pe.matmul(PS[0:HF, 5, 0:P], lftok[:, 0, :], tri_le[:, :], start=True, stop=True)
            pe.matmul(PS[0:HF, 5, P:SEQ], lftok[:, 0, :], ones[:, :], start=True, stop=False)
            pe.matmul(PS[0:HF, 5, P:SEQ], lftok[:, 1, :], tri_le[:, :], start=False, stop=True).then_inc(c_filled, 1)
            pe.wait_ge(lfs_done, 1)
            pe.wait_ge(lfm_done, 1)
            pe.wait_ge(tk_drained, NTF)
            new = lfm[:, :, :].rearrange("p b h -> p (b h)")
            for g in range(NPG):
                o = PS[0:NB * HF, g // 4, (g % 4) * P:(g % 4 + 1) * P]
                pe.matmul(o, lfp[:, g, :, :].rearrange("p b h -> p (b h)"), tri_gt[:, :], start=True, stop=False)
                pe.matmul(o, lfs[:, g, :, :].rearrange("p b h -> p (b h)"), ones[:, :], start=False, stop=False)
                pe.matmul(o, new, ones[0:NS, :], start=False, stop=True)
            pe.matmul(PS[0:NB * HF, 2, 0:NS], new, tri_gt[0:NS, 0:NS], start=True, stop=True).then_inc(dec_filled, 1)

            pe.wait_ge(decay_set, 1)
            pe.wait_ge(negc_set, 1)
            for s in range(NU + 2):
                if s < NU:
                    fox, h, qb = UNITS[s]
                    if s >= 2:
                        pe.wait_ge(pa_exp, s - 1)
                    o = PS[:, s % 2, 0:width(s)]
                    q = raw[:, (FQ if fox else MQ) + h, qb * P:(qb + 1) * P]
                    k = raw[:, FK + h, 0:width(s)] if fox else mraw[:, h, :]
                    last = pe.matmul(o, q, k, start=True, stop=not fox)
                    if fox:
                        pe.matmul(o, ident[0:HF, h:h + 1].to_broadcast([HF, P]), negc[:, 0:width(s)], start=False, stop=False)
                        last = pe.matmul(PS[:, s % 2, qb * P:(qb + 1) * P], ident[:, :], causal[:, :], start=False, stop=True)
                    last.then_inc(pa_scored, 1)
                if 1 <= s <= NU:
                    u = s - 1
                    pe.wait_ge(pa_prob, u + 1)
                    if u >= 2:
                        pe.wait_ge(pa_tc, u - 1)
                    for a in range(width(u) // P):
                        last = pe.transpose(PS[:, 2 + u % 2, a * P:(a + 1) * P], probs[:, u % 2, a * P:(a + 1) * P], ident[:, :])
                    last.then_inc(pa_t, 1)
                if s >= 2:
                    u = s - 2
                    fox, h, qb = UNITS[u]
                    pe.wait_ge(pa_tc, u + 1)
                    if u >= 2:
                        pe.wait_ge(pa_out, u - 1)
                    na = width(u) // P
                    for a in range(na):
                        v = vtok[:, a, h * P:(h + 1) * P] if fox else mtok[:, a, MW + h * P:MW + (h + 1) * P]
                        last = pe.matmul(PS[:, 4 + u % 2, 0:P], v, probsT[:, u % 2, a, :], start=(a == 0), stop=(a == na - 1))
                    last.then_inc(pa_pv, 1)

            pe.wait_ge(pa_out, NU)

            def keys_in(b, u, first=False):
                for g in range(9):
                    bank = 2 * ((u + g) % 2)
                    if g < NPG:
                        pe.wait_ge(k_in[g], b * 16 + (32 if g < 5 else 16))
                    else:
                        pe.wait_ge(mk_loaded, b * 16 + 16)
                    if g >= 2 or not first:
                        pe.wait_ge(kt_act, b * 9 + (g - 1))
                        pe.wait_ge(kt_dve, b * 9 + (g - 1))
                    if g < NPG:
                        for h in range(HF):
                            last = pe.transpose(PS[:, bank + h // 4, (h % 4) * P:(h % 4 + 1) * P],
                                                kpage[g][:, h * P:(h + 1) * P], ident[:, :])
                    else:
                        for h in range(HM):
                            for a in range(2):
                                c = ((h % 2) * 2 + a) * P
                                last = pe.transpose(PS[:, bank + h // 2, c:c + P], mk_in[:, a, h * P:(h + 1) * P], ident[:, :])
                    last.then_inc(kt_filled, 1)

            def decode_scores(b, first=False):
                pe.wait_ge(kt_act, b * 9 + 9)
                pe.wait_ge(kt_dve, b * 9 + 9)
                pe.wait_ge(q_set, b + 1)
                if not first:
                    pe.wait_ge(d_exp, b)
                for c in range(3):
                    w = 512 if c < 2 else NS
                    o = PS[0:24, 4 + c, 0:w]
                    for h in range(HF):
                        k = keysT[:, h, c * 512:c * 512 + w] if c < 2 else raw[:, FK + h, SEQ:T]
                        pe.matmul(o, q_rows[:, h * 24:(h + 1) * 24], k, start=(h == 0), stop=False)
                    pe.matmul(o, sel_b[:, :], decay[:, c * 512:c * 512 + w], start=False, stop=(c < 2))
                pe.matmul(o, rep4[:, :, :].rearrange("p h q -> p (h q)"), causal_b,
                          start=False, stop=True)
                for h in range(HM):
                    last = pe.matmul(PS[0:16, 6, 64:64 + MEM], mq_rows[:, h * 16:(h + 1) * 16], mkeysT[:, h, :],
                                     start=(h == 0), stop=(h == HM - 1))
                last.then_inc(d_scored, 1)

            def decode_values(b, first=False):
                pe.wait_ge(d_prob, b + 1)
                if not first:
                    pe.wait_ge(d_out, b)
                pe.matmul(PS[:, 7, 0:24], dprob[0:24, 0:P], ident[0:24, 0:24], start=True, stop=True)
                for g in range(1, NPG):
                    pe.transpose(PS[:, 7, g * 24:(g + 1) * 24], dprob[0:24, g * P:(g + 1) * P], ident[0:24, 0:24])
                for a in range(2):
                    pe.transpose(PS[:, 7, 192 + a * 16:192 + (a + 1) * 16], mprob[0:16, a * P:(a + 1) * P], ident[0:16, 0:16])
                pe.transpose(PS[0:NS, 7, 224:248], dprob[0:24, PAST:KEYS], ident[0:24, 0:24]).then_inc(d_t, 1)
                pe.wait_ge(d_tc, b + 1)
                pe.wait_ge(v_loaded, b * 144 + 144)
                for h in range(HF):
                    o = PS[:, 7, 256 + h * NL:256 + (h + 1) * NL]
                    for g in range(NPG):
                        pe.matmul(o, vpages[:, g, h * P:(h + 1) * P], dpT[:, g, h * NL:(h + 1) * NL], start=(g == 0), stop=False)
                    pe.matmul(o, vtok[0:NS, 2, h * P:(h + 1) * P], npT[:, h * NL:(h + 1) * NL], start=False, stop=True)
                for h in range(HM):
                    for a in range(2):
                        last = pe.matmul(PS[:, 7, 280 + h * NL:280 + (h + 1) * NL], mv_in[:, a, h * P:(h + 1) * P],
                                         mpT[:, a, h * NL:(h + 1) * NL], start=(a == 0), stop=(a == 1))
                last.then_inc(d_pv, 1)

            keys_in(0, 0, True)
            decode_scores(0, True)
            keys_in(1, 1)
            decode_values(0, True)
            decode_scores(1)
            with pe.Fori(0, 3) as i:
                for u in range(2):
                    keys_in(i * 2 + (u + 2), u)
                    decode_values(i * 2 + (u + 1))
                    decode_scores(i * 2 + (u + 2))
            decode_values(NB - 1)

            def by_token(n):
                pe.wait_ge(wo_drained, n + 1)
                if n >= 2:
                    pe.wait_ge(h_added, 3 * (n - 1))
                for t, (t0, w) in enumerate(TILES):
                    last = pe.transpose(PS[0:w, 2 + n % 2, t * P:(t + 1) * P], attnT[:, n % 2, t0:t0 + w], ident[:, :])
                last.then_inc(at_filled, 1)

            pe.wait_ge(d_out, NB)
            for n in range(KC):
                pe.wait_ge(wo_in[(n // 2) % 3], 16 * (n // 6 + 1))
                if n >= 2:
                    pe.wait_ge(wo_drained, n - 1)
                for k in range(KC):
                    c = (n % 2) * P
                    last = pe.matmul(PS[:, n % 2, 0:T], wo_slot[(n // 2) % 3][:, k, c:c + P], cat[:, k, :], start=(k == 0), stop=(k == KC - 1))
                last.then_inc(wo_filled, 1)
                if n:
                    by_token(n - 1)
            by_token(KC - 1)
            for f, (t, c, m) in enumerate(HTF):
                pe.wait_ge(h_scl, t + 1)
                if f >= 2:
                    pe.wait_ge(ht_drained, f - 1)
                w = TILES[t][1]
                for a in range(m):
                    last = pe.transpose(ht_out(f)[:, a, :], h_scaled[0:w, t, (c + a) * P:(c + a + 1) * P], ident[0:w, 0:w])
                last.then_inc(ht_filled, 1)
            pe.wait_ge(ht_drained, HT_FILLS)
            pe.wait_ge(rt_in, 64)
            for t, (t0, w) in enumerate(TILES):
                o = PS[0:w, 4, t * 64:t * 64 + NG + NE]
                for k in range(KC):
                    pe.matmul(o, xnT[:, k, t0:t0 + w], w_rt[:, k, :], start=(k == 0), stop=False)
                pe.matmul(o, ones[0:1, 0:w], b_rt, start=False, stop=True).then_inc(lg_filled, 1)

            pe.wait_ge(y_clear, 1)
            chosen = rw[:, :, NE:2 * NE]
            pe.matmul(PS[:, 5, 128:128 + SLOTS], ones[:, :], tri_le[:, 0:SLOTS], start=True, stop=True)
            for t, (t0, w) in enumerate(TILES):
                o = PS[0:w, 5, t * NE:(t + 1) * NE]
                for a in range(t):
                    pe.matmul(o, ones[:, 0:w], chosen[:, a, :], start=(a == 0), stop=False)
                last = pe.matmul(o, tri_le[0:w, 0:w], chosen[0:w, t, :], start=(t == 0), stop=True)
            last.then_inc(rank_filled, 1)

            def gather(p, chunks):
                for c in chunks:
                    o = PS[:, 2 + c // 4, (c % 4) * P:(c % 4 + 1) * P]
                    for t, (t0, w) in enumerate(TILES):
                        last = pe.matmul(o, h_scaled[0:w, t, c * P:(c + 1) * P], pick_tok[0:w, t, :, :].rearrange("p x s -> p (x s)"),
                                         start=(t == 0), stop=(t == 2))
                    if c % 4 == 3:
                        last.then_inc(xg_filled, 1)

            def pair_pe(p, first=False, last_pair=False):
                pe.wait_ge(xg_drained, p * 4 + 4)
                for which in range(2):
                    for half in range(2):
                        for x in range(2):
                            u = 4 * which + 2 * half + x
                            pe.wait_ge(unit_in[u % 6], p * 32 + (16 * (u // 6) + 16))
                        for k in range(KC // 2):
                            for x in range(2):
                                u = 4 * which + 2 * half + x
                                kk = half * KC // 2 + k
                                wt = unit[u % 6].rearrange("p (k n) -> p k n", n=FFW)
                                last = pe.matmul(PS[x * SLOTS:(x + 1) * SLOTS, which, :], xgT[:, kk, x * SLOTS:(x + 1) * SLOTS], wt[:, k, :],
                                                 start=(kk == 0), stop=(kk == KC - 1))
                                if k == KC // 2 - 1:
                                    last.then_inc(units_used, 1)
                if not last_pair:
                    pe.wait_ge(picked_set, p + 2)
                    if not first:
                        pe.wait_ge(part_added, p * KC)
                    gather(p + 1, range(8))
                pe.wait_ge(pg_set, p + 1)
                for t, (t0, w) in enumerate(TILES):
                    last = pe.matmul(PS[:, 7, t0:t0 + w], pick_gate[0:w, t, :, :].rearrange("p x s -> p (x s)"), ident[0:w, 0:w],
                                     start=True, stop=True)
                last.then_inc(g_filled, 1)
                pe.wait_ge(pair_h, p + 1)
                for k in range(FB):
                    last = pe.transpose(PS[:, 6, k * P:(k + 1) * P], hS[:, k * P:(k + 1) * P], ident[:, :])
                last.then_inc(ph_filled, 1)
                if not last_pair:
                    gather(p + 1, range(8, KC))
                pe.wait_ge(pair_hT, p + 1)
                pe.wait_ge(g_copied, p + 1)
                for half in range(2):
                    for x in range(2):
                        u = 8 + 2 * half + x
                        pe.wait_ge(unit_in[u % 6], p * 32 + 32)
                    for k in range(FB // 2):
                        kk = half * FB // 2 + k
                        for n in range(4):
                            for x in range(2):
                                wt = unit[(8 + 2 * half + x) % 6].rearrange("p (k n) -> p k n", n=D)
                                last = pe.matmul(PS[x * SLOTS:(x + 1) * SLOTS, YB[n], :], hT[:, kk, x * SLOTS:(x + 1) * SLOTS],
                                                 wt[:, k, n * 512:(n + 1) * 512], start=(kk == 0), stop=(kk == FB - 1))
                                if kk == FB - 1 and x == 1:
                                    last.then_inc(yst_filled, 1)
                                elif k == FB // 2 - 1 and n == 3:
                                    last.then_inc(units_used, 1)
                if not last_pair:
                    pe.wait_ge(xg_drained, p * 4 + 8)
                for n in range(KC):
                    if n % 4 == 0:
                        if (n // 4) % 2 == 0:
                            pe.wait_ge(yst_act, p * 2 + (n // 8 + 1))
                        else:
                            pe.wait_ge(yst_dve, p * 2 + (n // 8 + 1))
                    if n >= 4:
                        pe.wait_ge(part_added, p * KC + (n - 3))
                    last = pe.matmul(PS[:, 2 + n % 4, 0:T], yslot[:, n * P:(n + 1) * P], gate_slot[:, :], start=True, stop=True)
                    last.then_inc(part_filled, 1)

            pe.wait_ge(picked_set, 1)
            gather(0, range(KC))
            pe.wait_ge(slots_set, 2)
            pe.matmul(PS[:, 6, 0:2], ones[:, :], n_over, start=True, stop=True).then_inc(over_filled, 1)
            pe.wait_ge(overflow_set, 1)
            pair_pe(0, True)
            with pe.Fori(0, PAIRS - 2) as i:
                pair_pe(i + 1)
            pair_pe(PAIRS - 1, last_pair=True)

            pe.wait_ge(part_added, PAIRS * KC)
            n_past = pe.value_load(overflow[0:1, 0:1], min_val=0, max_val=2 * T)
            with pe.If(n_past > 0):
                for f, (t, c, m) in enumerate(HTF):
                    pe.wait_ge(h_scl, 3 + t + 1)
                    if f >= 2:
                        pe.wait_ge(ht_drained, HT_FILLS + f - 1)
                    w = TILES[t][1]
                    for a in range(m):
                        last = pe.transpose(ht_out(f)[:, a, :], g_scaled[0:w, t, (c + a) * P:(c + a + 1) * P], ident[0:w, 0:w])
                    last.then_inc(ht_filled, 1)
                pe.wait_ge(ht_drained, 2 * HT_FILLS)
                with pe.Fori(0, NE) as e:
                    pe.wait_ge(gcol_set, e + 1)
                    for t, (t0, w) in enumerate(TILES):
                        last = pe.matmul(PS[:, 6, t0:t0 + w], gcol[0:w, t, :], ident[0:w, 0:w], start=True, stop=True)
                    last.then_inc(g_filled, 1)
                    for j in range(FB):
                        for which, wt, sem_filled in ((0, wg_u, mg_filled), (1, wu_u, mu_filled)):
                            if j % 2 == 0:
                                pe.wait_ge(unit_in[j + which], e * 16 + (32 * PAIRS + 16))
                            if which == 0:
                                pe.wait_ge(pair_silu, e * 4 + (PAIRS + max(j - 1, 0)))
                            else:
                                pe.wait_ge(hs_done, e * 4 + max(j, 1))
                            for k in range(KC):
                                last = pe.matmul(PS[:, 2 * which + j % 2, 0:T], wt[j // 2][:, k, (j % 2) * P:(j % 2 + 1) * P],
                                                 g_xnT[:, k, :], start=(k == 0), stop=(k == KC - 1))
                            last.then_inc(sem_filled, 1)
                    pe.wait_ge(pair_hT, e * 4 + (PAIRS + 4))
                    for n in range(KC):
                        if n % 8 == 0:
                            pe.wait_ge(unit_in[4 + n // 8], e * 16 + (32 * PAIRS + 16))
                        pe.wait_ge(part_added, e * 16 + (PAIRS * KC + max(n - 1, 0)))
                        for k in range(FB):
                            last = pe.matmul(PS[:, 4 + n % 2, 0:T], wd_u[n // 8][:, k, (n % 8) * P:(n % 8 + 1) * P], g_hT[:, k, :],
                                             start=(k == 0), stop=(k == FB - 1))
                        last.then_inc(md_filled, 1)
                pe.wait_ge(part_added, (PAIRS + NE) * KC)
            for t, (t0, w) in enumerate(TILES):
                for c in range(4):
                    f = 4 * t + c
                    if f >= 2:
                        pe.wait_ge(y_done, f - 1)
                    for a in range(4):
                        last = pe.transpose(PS[0:w, f % 2, a * P:(a + 1) * P], yT[:, 4 * c + a, t0:t0 + w], ident[:, :])
                    last.then_inc(yt_filled, 1)


N_CONSTS = 26
G_STEPS = 42


_INS = ['x_prompt', 'x_sample', 'cache_fox_k', 'cache_fox_v', 'cache_fox_logf', 'cache_mem_k', 'cache_mem_v',
        'state_hgrn', 'page_table', 'mem_prompt', 'g_attn_norm', 'w_in', 'b_fox_f', 'g_fox_q', 'g_fox_k', 'lb_logits',
        'g_hgrn_out', 'g_mem_norm', 'w_mem_kv', 'g_mem_q', 'g_mem_k', 'w_out', 'g_ffn_norm', 'w_router_group',
        'b_router_group', 'w_router_expert', 'b_router_expert', 'w_gate_e', 'w_up_e', 'w_down_e']
_OUTS = [(1, 256, 2048), (8, 4, 2048), (1, 1, 256, 6, 128), (1, 1, 256, 6, 128), (1, 1, 256, 6), (1, 1, 6, 128, 128),
         (1, 1, 256, 4, 128), (1, 1, 256, 4, 128), (1, 8, 4, 6, 128), (1, 8, 4, 6, 128), (1, 8, 4, 6), (1, 8, 6, 128, 128)]


def kernel(**inputs):
    import numpy as _np
    import concourse.bacc as _bacc
    from concourse import mybir as _mybir
    from concourse.bass_utils import run_bass_kernel_spmd as _run

    nc = _bacc.Bacc("TRN2", target_bir_lowering=False, num_devices=1)
    arrays, args = {}, []
    for name in _INS:
        a = _np.ascontiguousarray(inputs[name])
        arrays[f"in_{name}_dram"] = a
        args.append(nc.dram_tensor(f"in_{name}_dram", a.shape, _mybir.dt.from_np(a.dtype), kind="ExternalInput").ap())
    for i, shape in enumerate(_OUTS):
        args.append(nc.dram_tensor(f"out_{i}_dram", shape, _mybir.dt.float32, kind="ExternalOutput").ap())
    build(nc, *args)
    r = _run(nc, [arrays], core_ids=[0])
    return tuple(r.results[0][f"out_{i}_dram"] for i in range(len(_OUTS)))
```

```python
from contextlib import ExitStack

import concourse.bass as bass
from concourse import mybir

D = 2048
P = 128
KC = D // P
SEQ = 256
NB, NL = 8, 4
NS = NB * NL
T = SEQ + NS
TILES = [(0, P), (P, P), (SEQ, NS)]
MEM = 256
HF, HG, HM = 6, 6, 4
FW, MW = HF * P, HM * P
IN_W = 7 * FW + HF + MW
FF_COL = 3 * FW
NPG, PG = 8, 128
POOL = 80
PAST = NPG * PG
KEYS = PAST + NS
CH = 16
NCH = SEQ // CH
NE, NG, EPG = 32, 4, 8
FFW = 512
FB = FFW // P
EPS = 1e-6
SCALE = float(P) ** -0.5
NEG = -1.0e30
HQ, HFG, HI, HGT, FQ, FK, FV, MQ = 0, 6, 12, 18, 24, 30, 36, 42
NBLK = 46
NN = HF + HF + HM + HM + HG
SLOTS = 64
PAIRS = NE // 2
UNITS_PAIR = 12
UPP = 11


def build(nc, x_prompt, x_sample, cache_fox_k, cache_fox_v, cache_fox_logf, cache_mem_k, cache_mem_v,
          state_hgrn, page_table, mem_prompt, g_attn_norm, w_in, b_fox_f, g_fox_q, g_fox_k, lb_logits,
          g_hgrn_out, g_mem_norm, w_mem_kv, g_mem_q, g_mem_k, w_out, g_ffn_norm, w_router_group,
          b_router_group, w_router_expert, b_router_expert, w_gate_e, w_up_e, w_down_e,
          y_prompt, y_sample, fox_k_p, fox_v_p, fox_logf_p, hgrn_state_p, mem_k_p, mem_v_p,
          fox_k_s, fox_v_s, fox_logf_s, hgrn_state_s, dbg=None):
    f32, i32 = mybir.dt.float32, mybir.dt.int32
    ALU, ACT, AX = mybir.AluOpType, mybir.ActivationFunctionType, mybir.AxisListType
    ds = bass.ds

    x_tok_d = [x_prompt[0, 0:P, :], x_prompt[0, P:SEQ, :], x_sample.rearrange("b l d -> (b l) d")]
    mem_tok_d = [mem_prompt[0, 0:P, :], mem_prompt[0, P:MEM, :]]
    w_in_d = w_in[0].rearrange("(k p) n -> p k n", p=P)
    w_kv_d = w_mem_kv[0].rearrange("(k p) n -> p k n", p=P)
    w_out_d = w_out[0].rearrange("(k p) n -> p k n", p=P)
    w_gate_d = w_gate_e[0].rearrange("e (k p) n -> e p k n", p=P)
    w_up_d = w_up_e[0].rearrange("e (k p) n -> e p k n", p=P)
    w_down_d = w_down_e[0].rearrange("e (k p) n -> e p k n", p=P)
    w_rg_d = w_router_group[0].rearrange("(k p) n -> p k n", p=P)
    w_re_d = w_router_expert[0].rearrange("(k p) n -> p k n", p=P)
    y_tok_d = [y_prompt[0, 0:P, :], y_prompt[0, P:SEQ, :], y_sample.rearrange("b l d -> (b l) d")]
    logf_d = cache_fox_logf[0].rearrange("g t h -> g (t h)")
    k_pages = cache_fox_k[0].rearrange("g t h d -> g t (h d)")
    v_pages = cache_fox_v[0].rearrange("g t h d -> g t (h d)")

    ctx = ExitStack()
    with ctx:
        ctx.enter_context(nc.allow_non_contiguous_dma(reason="small vectors and column blocks"))

        def sb(name, shape, dt=f32):
            return ctx.enter_context(nc.sbuf_tensor(name, shape, dt))

        def sem(name):
            return ctx.enter_context(nc.semaphore(name))

        ident = sb("ident", [P, P])
        ones = sb("ones", [P, P])
        tri_le = sb("tri_le", [P, P])
        tri_gt = sb("tri_gt", [P, P])
        causal = sb("causal", [P, P])
        sel48 = sb("sel48", [NB * HF, NB, HF, NL])
        causal4 = sb("causal4", [NL, NB, NS])
        rep4 = sb("rep4", [NL, 8, NL])
        batch_of = sb("batch_of", [NS, NB])
        chunk_of = sb("chunk_of", [P, P // CH])
        rows = sb("rows", [65, P])
        cols = sb("cols", [P, 65])
        eps_t = sb("eps_t", [P, 1])
        one_t = sb("one_t", [P, 1])
        lbw = sb("lbw", [P, 6, HG])
        gq = sb("gq", [P, 5])
        ssq = sb("ssq", [P, 8])
        rstd = sb("rstd", [P, 8])
        b_f = sb("b_f", [HF, 1])
        G_ATT, G_MEM, G_FFN = cols[:, 0:KC], cols[:, KC:2 * KC], cols[:, 2 * KC:3 * KC]
        g_fq, g_fk, g_hn, g_mq, g_mk = (cols[:, 48 + n:49 + n] for n in range(5))
        lb0, lb1 = cols[:, 53:59], cols[:, 59:65]
        LB, LB1 = lbw[:, 4, :], lbw[:, 5, :]

        arena = sb("arena", [P, 45888])

        def view(off, *dims):
            n = 1
            for d in dims:
                n *= d
            a = arena[:, off:off + n]
            if len(dims) == 2:
                return a.rearrange("p (a b) -> p a b", b=dims[1])
            if len(dims) == 3:
                return a.rearrange("p (a b c) -> p a b c", b=dims[1], c=dims[2])
            return a

        RAW = 0
        CAT = RAW + NBLK * T
        MRAW = CAT + KC * T
        MTOK = MRAW + 8 * MEM
        TOK = MTOK + 2 * 1024
        WORK = TOK + 9 * FW
        raw = view(RAW, NBLK, T)
        x_tok = view(RAW, 3, D)
        mem_tok_in = view(RAW + 3 * D, 2, D)
        junk = view(CAT, D)
        cat = view(CAT, KC, T)
        mraw = view(MRAW, 8, MEM)
        mtok = view(MTOK, 2, 1024)
        memT = view(TOK, KC, MEM)
        ktok, vtok = (view(TOK + n * 3 * FW, 3, FW) for n in range(2))
        xT = view(WORK, KC, T)
        wslot = [view(WORK + KC * T + n * KC * 384, KC, 384) for n in range(2)]
        w_ff = view(WORK + KC * T + 2 * KC * 384, KC, HF)
        WEND = WORK + KC * T + 2 * KC * 384 + KC * HF

        def heads2(n):
            return view(TOK + n * 2 * T, 2, T)

        gQ, gF, gV, gO, gKT, gTmp = (heads2(n) for n in range(6))
        gW = [heads2(6), heads2(7)]
        gQW = [heads2(8), heads2(9)]
        gS = view(TOK + 10 * 2 * T, 160)
        decays = sb("decays", [P, HG, NCH + NB])
        vpar = view(TOK, 2, 2, FW)
        vsam = view(TOK + 4 * FW, FW)[0:NS]
        states = view(TOK + 5 * FW, NCH, P)
        vmask = [view(TOK + 5 * FW + NCH * P + n * 4 * P, 4, P)[0:NS] for n in range(2)]
        s_in = [view(MTOK + n * NB * P, NB, P) for n in range(2)]
        ktil = sb("ktil", [P, 3, P])
        parity = sb("parity", [P, 2])
        probs = view(WORK, 2, SEQ)
        probsT = view(WORK + 2 * SEQ, 2, 2, P)
        kpage = [view(TOK + (6 + g) * FW, FW) for g in range(7)] + [view(4096, FW)]
        vpages = view(WORK + 4 * FW, NPG, FW)
        keysT = view(WORK + 12 * FW, HF, PAST)
        dprob = view(WORK + 12 * FW + HF * PAST, KEYS)
        mk_in = view(MRAW, 2, MW)
        mv_in = view(MRAW + 2 * MW, 2, MW)
        mkeysT = view(MRAW + 4 * MW, HM, MEM)
        mprob = view(MRAW + 4 * MW + HM * MEM, MEM)
        dprobT = view(4864, NPG + 3, P)
        dout = view(4864 + (NPG + 3) * P, 3, P)
        wo_slot = [view(o, KC, 256) for o in (RAW, WORK, WORK + 4096)]
        attnT = view(WORK + 9216, 2, T)
        h_tok = view(TOK, 3, D)
        UNIT = 4096
        LATE, LATE_END = 5 * UNIT, TOK
        HSC = TOK + 3 * D
        YT = HSC + 3 * D
        UNIT5 = YT + KC * T
        FREE = UNIT5 + UNIT
        unit = [view(o, UNIT) for o in (UNIT, 2 * UNIT, UNIT5, 0, 3 * UNIT, 4 * UNIT)]
        YB = (0, 1, 6, 7)
        h_scaled = view(HSC, 3, D)
        h_back = view(HSC, 3, D)
        yT = view(YT, KC, T)
        xgT = view(TOK, KC, 2 * SLOTS)
        yslot = view(TOK + 2 * D, D)
        hT = view(FREE, FB, 2 * SLOTS)
        hS = view(FREE + 2 * FB * SLOTS, FFW)
        pick_tok = view(FREE + 4 * FB * SLOTS, 3, 2, SLOTS)
        pick_gate = view(FREE + 4 * FB * SLOTS + 6 * SLOTS, 3, 2, SLOTS)
        w_rt = view(FREE, KC, NG + NE)
        xgain = view(FREE + KC * (NG + NE), 2, T)
        gate_slot = view(FREE + 4 * FB * SLOTS + 12 * SLOTS, T)

        def late(*dims):
            nonlocal LATE
            n = 1
            for d in dims:
                n *= d
            LATE += n
            assert LATE <= LATE_END
            return view(LATE - n, *dims)

        logits = late(3, NG + NE)
        b_rt = late(NG + NE)[0:1]
        rw = late(3, 2 * NE)
        gates = late(3, NE)
        choice = late(3, 2, NE)
        c1g = late(3, NE)
        slot_of = late(3, NE)
        iota1 = late(SLOTS)
        over = late(3, NE)
        n_over = late(2)
        lgT = xgain[0:NG + NE, 0, :]
        ssq_part = late(3, KC)
        sq_out = late(P)
        b_all = late(NG + NE)
        overflow = sb("overflow", [P, 1], i32)
        g_scaled = view(0, 3, D)
        g_xnT = view(TOK, KC, T)
        g_hT = view(TOK + KC * T, FB, T)
        gbc = view(TOK + KC * T + FB * T, T)
        gcol = view(FREE, 3, P)
        g_hS = view(FREE + 3 * P, 2, T)
        wg_u = [unit[n].rearrange("p (k n) -> p k n", k=KC) for n in (0, 2)]
        wu_u = [unit[n].rearrange("p (k n) -> p k n", k=KC) for n in (1, 3)]
        wd_u = [unit[n].rearrange("p (k n) -> p k n", k=FB) for n in (4, 5)]
        HTF = [(t, c, 4) for t in range(2) for c in range(0, KC, 4)] + [(2, 0, KC)]
        HT_FILLS = len(HTF)

        def ht_out(f):
            t, c, m = HTF[f]
            return PS[:, 4 * (f % 2), :].rearrange("p (c t) -> p c t", c=m)[:, :, 0:TILES[t][1]]

        q_rows = sb("q_rows", [P, HF + HM, 32])
        sel_b = sb("sel_b", [NB * HF, 4, 32])
        causal_b = view(WORK + 12 * FW + HF * PAST + KEYS, NS)[0:NL]
        nmax = sb("nmax", [P, 4])
        psum_p = sb("psum_p", [P, 4])
        ptab_row = sb("ptab_row", [1, NB * NPG], i32)

        ffz = sb("ffz", [HF, T])
        ffw = sb("ffw", [HF, T])
        lfT = sb("lfT", [HF, T])
        lftok = sb("lftok", [P, 3, HF])
        negc = sb("negc", [HF, SEQ])
        ptab = sb("ptab", [NB * NPG, 1], i32)
        lfpages = view(MTOK, PG * HF)[0:NB * NPG]
        lfp = sb("lfp", [P, NPG, NB, HF])
        lfs = sb("lfs", [P, NPG, NB, HF])
        lfm = sb("lfm", [NS, NB, HF])
        decay = sb("decay", [NB * HF, KEYS])

        sq = sb("sq", [P, 2, T])
        hn_r = sb("hn_r", [NN, T])
        row_of = sb("row_of", [P, 2 * NN - 1])

        PS = ctx.enter_context(nc.psum_tensor("PS", [P, 8, 512], f32))

        consts_set = sem("consts_set")
        rows_in = sem("rows_in")
        cols_filled = sem("cols_filled")
        cols_set = sem("cols_set")
        gains_set = sem("gains_set")
        tok_in = [sem(f"tok_in{n}") for n in range(5)]
        ssq_clear = sem("ssq_clear")
        ssq_done = sem("ssq_done")
        sqrt_done = sem("sqrt_done")
        scaled = sem("scaled")
        tT_filled = sem("tT_filled")
        tT_drained = sem("tT_drained")
        w_in_slot = [sem(f"w_in_slot{n}") for n in range(2)]
        wff_in = sem("wff_in")
        blk_filled = sem("blk_filled")
        blk_drained = sem("blk_drained")
        hn_sq = sem("hn_sq")
        hn_sum = sem("hn_sum")
        hn_sqrt = sem("hn_sqrt")
        hn_rcp = sem("hn_rcp")
        hn_rows = sem("hn_rows")
        hn_done = sem("hn_done")
        tk_filled = sem("tk_filled")
        tk_drained = sem("tk_drained")
        lf_act = sem("lf_act")
        lf_done = sem("lf_done")
        lft_filled = sem("lft_filled")
        lft_drained = sem("lft_drained")
        c_filled = sem("c_filled")
        negc_set = sem("negc_set")
        ptab_in = sem("ptab_in")
        lfpages_in = sem("lfpages_in")
        lfp_filled = sem("lfp_filled")
        lfp_drained = sem("lfp_drained")
        lfs_done = sem("lfs_done")
        lfm_done = sem("lfm_done")
        dec_filled = sem("dec_filled")
        decay_set = sem("decay_set")
        out_done = sem("out_done")
        wo_in = [sem(f"wo_in{n}") for n in range(3)]
        x_again = sem("x_again")
        wo_filled = sem("wo_filled")
        wo_drained = sem("wo_drained")
        at_filled = sem("at_filled")
        h_added = sem("h_added")
        rt_in = sem("rt_in")
        h_ssq = sem("h_ssq")
        h_rstd = sem("h_rstd")
        h_scl = sem("h_scl")
        ht_filled = sem("ht_filled")
        ht_drained = sem("ht_drained")
        lg_filled = sem("lg_filled")
        bias_filled = sem("bias_filled")
        lgT_set = bias_filled
        rt_sub = sem("rt_sub")
        rt_exp = sem("rt_exp")
        gates_set = sem("gates_set")
        unit_in = [sem(f"unit_in{n}") for n in range(6)]
        moe_prep = sem("moe_prep")
        rank_filled = sem("rank_filled")
        slots_set = sem("slots_set")
        over_filled = sem("over_filled")
        overflow_set = sem("overflow_set")
        h_out = sem("h_out")
        h_again = sem("h_again")
        units_used = sem("units_used")
        picked_set = sem("picked_set")
        pg_set = sem("pg_set")
        xg_filled = sem("xg_filled")
        xg_drained = sem("xg_drained")
        pair_silu = sem("pair_silu")
        pair_hT = sem("pair_hT")
        pair_h = sem("pair_h")
        ph_filled = sem("ph_filled")
        g_filled = sem("g_filled")
        g_copied = sem("g_copied")
        yst_filled = sem("yst_filled")
        yst_act = sem("yst_act")
        yst_dve = sem("yst_dve")
        part_filled = sem("part_filled")
        part_added = sem("part_added")
        gcol_set = sem("gcol_set")
        mg_filled = sem("mg_filled")
        mu_filled = sem("mu_filled")
        hs_done = sem("hs_done")
        md_filled = sem("md_filled")
        yt_filled = sem("yt_filled")
        y_done = sem("y_done")
        lb_diff = sem("lb_diff")
        lb_exp = sem("lb_exp")
        lb_set = sem("lb_set")
        hg_prep = sem("hg_prep")
        hg_step = sem("hg_step")
        qw_ready = sem("qw_ready")
        intra_filled = sem("intra_filled")
        intra_used = sem("intra_used")
        hg_done = sem("hg_done")
        parity_set = sem("parity_set")
        vt_filled = sem("vt_filled")
        vt_drained = sem("vt_drained")
        kt2_filled = sem("kt2_filled")
        kt2_drained = sem("kt2_drained")
        s_loaded = [sem(f"s_loaded{n}") for n in range(2)]
        os_filled = sem("os_filled")
        ds_filled = sem("ds_filled")
        ds_used = sem("ds_used")
        sm_set = sem("sm_set")
        oi_filled = sem("oi_filled")
        o_added = sem("o_added")
        sig_done = sem("sig_done")
        gate_done = sem("gate_done")
        st_step = sem("st_step")
        stp_out = sem("stp_out")
        sts_out = [sem(f"sts_out{n}") for n in range(2)]
        pa_scored = sem("pa_scored")
        pa_max = sem("pa_max")
        pa_exp = sem("pa_exp")
        pa_prob = sem("pa_prob")
        pa_t = sem("pa_t")
        pa_tc = sem("pa_tc")
        pa_pv = sem("pa_pv")
        pa_out = sem("pa_out")
        ptrow_in = sem("ptrow_in")
        k_in = tok_in + [sem(f"k_in{n}") for n in range(5, NPG)]
        mk_loaded = sem("mk_loaded")
        v_loaded = sem("v_loaded")
        kt_filled = sem("kt_filled")
        kt_act = sem("kt_act")
        kt_dve = sem("kt_dve")
        q_clear = sem("q_clear")
        q_set = sem("q_set")
        d_scored = sem("d_scored")
        d_max = sem("d_max")
        d_exp = sem("d_exp")
        d_rcp = sem("d_rcp")
        d_oc = sem("d_oc")
        d_ot = sem("d_ot")
        d_t = sem("d_t")
        d_tc = sem("d_tc")
        d_pv = sem("d_pv")
        d_out = sem("d_out")
        dve_step = sem("dve_step")

        NORM = [(mem_tok_in[:, 0], P, 3), (mem_tok_in[:, 1], P, 4),
                (x_tok[:, 0], P, 0), (x_tok[:, 1], P, 1), (x_tok[:, 2], NS, 2)]
        FILLS = [(n, c, 4) for n in range(4) for c in range(0, KC, 4)] + [(4, 0, KC)]

        def fill_out(f, w):
            n, c, m = FILLS[f]
            return PS[:, f % 8, :].rearrange("p (c t) -> p c t", c=m)[:, :, 0:w]

        NORMS = [(raw[:, FQ + h, :], T, 0) for h in range(HF)] + [(raw[:, FK + h, :], T, 1) for h in range(HF)] + \
                [(raw[:, MQ + h, :], T, 2) for h in range(HM)] + [(mraw[:, h, :], MEM, 3) for h in range(HM)]
        NORMS += [(cat[:, 6 + h, :], T, 4) for h in range(HG)]
        assert NN == len(NORMS)

        def by_token_fills(dst, b0):
            return [(dst[0:n, t, h0 * P:(h0 + m) * P], n, [raw[:, b0 + h, t0:t0 + n] for h in range(h0, h0 + m)])
                    for t, (t0, n) in enumerate(TILES) for h0, m in ((0, 4), (4, 2))]

        def memory_fills(h0):
            return [(mtok[:, t, h0 * P:(h0 + 4) * P], P, [mraw[:, h, t * P:(t + 1) * P] for h in range(h0, h0 + 4)]) for t in range(2)]

        TOKF = by_token_fills(vtok, FV) + memory_fills(4)
        NVF = len(TOKF)
        TOKF += by_token_fills(ktok, FK) + memory_fills(0)
        NTF = len(TOKF)

        UNITS = [(True, h, qb) for h in range(HF) for qb in range(2)] + \
                [(False, h, qb) for h in range(HM) for qb in range(2)]
        NU = len(UNITS)

        def width(u):
            fox, h, qb = UNITS[u]
            return (qb + 1) * P if fox else MEM

        ORDER = [3, 4, 5, 0, 1, 2]
        LAST = [FV + h for h in range(HF)] + [MQ + h for h in range(HM)]

        block = ctx.enter_context(nc.Block())

        @block.sync
        def _(sp):
            for n, d in ((0, mem_tok_d[0]), (1, mem_tok_d[1])):
                sp.dma_start(NORM[n][0], d).then_inc(tok_in[n], 16)
            sp.dma_start(rows[0:16, :], g_attn_norm[0].rearrange("(k p) -> k p", p=P)).then_inc(rows_in, 16)
            sp.dma_start(rows[16:32, :], g_mem_norm[0].rearrange("(k p) -> k p", p=P)).then_inc(rows_in, 16)
            sp.dma_start(rows[32:48, :], g_ffn_norm[0].rearrange("(k p) -> k p", p=P)).then_inc(rows_in, 16)
            for n, g in enumerate((g_fox_q, g_fox_k, g_hgrn_out, g_mem_q, g_mem_k)):
                sp.dma_start(rows[48 + n:49 + n, :], g).then_inc(rows_in, 16)
            sp.dma_start(rows[53:65, :], lb_logits.rearrange("l (h p) -> (l h) p", p=P)).then_inc(rows_in, 16)
            sp.dma_start(wslot[0], w_kv_d[:, :, 0:384]).then_inc(w_in_slot[0], 16)
            for n in range(3):
                sp.dma_start(NORM[2 + n][0][0:NORM[2 + n][1]], x_tok_d[n]).then_inc(tok_in[2 + n], 16)
            sp.dma_start(wslot[1], w_kv_d[:, :, 384:768]).then_inc(w_in_slot[1], 16)
            sp.dma_start(b_f[:, :], b_fox_f.rearrange("a h -> h a")).then_inc(wff_in, 16)
            sp.dma_start(w_ff, w_in_d[:, :, FF_COL:FF_COL + HF]).then_inc(wff_in, 16)
            sp.wait_ge(blk_filled, 3)
            sp.dma_start(wslot[0][:, :, 0:256], w_kv_d[:, :, 768:1024]).then_inc(w_in_slot[0], 16)
            for i0, ni, col in ((0, 4, FF_COL + HF), (4, 3, 0)):
                with sp.Fori(0, ni) as i:
                    sp.wait_ge(blk_filled, i * 6 + (6 * i0 + 6))
                    sp.dma_start(wslot[1], w_in_d[:, :, ds(i * FW + col, 384)]).then_inc(w_in_slot[1], 16)
                    sp.wait_ge(blk_filled, i * 6 + (6 * i0 + 8))
                    sp.dma_start(wslot[0], w_in_d[:, :, ds(i * FW + (col + 384), 384)]).then_inc(w_in_slot[0], 16)
            mq0 = IN_W - MW
            sp.wait_ge(blk_filled, 47)
            sp.dma_start(wslot[1][:, :, 0:256], w_in_d[:, :, mq0:mq0 + 256]).then_inc(w_in_slot[1], 16)
            sp.wait_ge(blk_filled, 50)
            sp.dma_start(wslot[0][:, :, 0:256], w_in_d[:, :, mq0 + 256:mq0 + 512]).then_inc(w_in_slot[0], 16)

            no = 0
            sp.wait_ge(tk_drained, NTF)
            for dst_p, dst_s, src in ((fox_k_p, fox_k_s, ktok), (fox_v_p, fox_v_s, vtok)):
                sp.dma_start(dst_p[0, 0].rearrange("(a t) h d -> t a (h d)", t=P), src[:, 0:2, :]).then_inc(out_done, 16)
                sp.dma_start(dst_s[0].rearrange("b l h d -> (b l) (h d)"), src[0:NS, 2, :]).then_inc(out_done, 16)
                no += 2
            for dst, c in ((mem_k_p, 0), (mem_v_p, 512)):
                sp.dma_start(dst[0, 0].rearrange("(a t) h d -> t a (h d)", t=P), mtok[:, :, c:c + 512]).then_inc(out_done, 16)
                no += 1
            sp.wait_ge(lft_drained, 1)
            sp.dma_start(fox_logf_p[0, 0].rearrange("(a t) h -> t a h", t=P), lftok[:, 0:2, :]).then_inc(out_done, 16)
            sp.dma_start(fox_logf_s[0].rearrange("b l h -> (b l) h"), lftok[0:NS, 2, :]).then_inc(out_done, 16)
            no += 2
            sp.dma_start(ptab_row[:, :], page_table.rearrange("(a b) g -> a (b g)", a=1)).then_inc(ptrow_in, 16)
            sp.wait_ge(ptrow_in, 16)

            def load_key_page(b, g, first=False):
                page = sp.value_load(ptab_row[0:1, ds(b * NPG + g, 1)], min_val=0, max_val=POOL - 1)
                if not first:
                    sp.wait_ge(kt_filled, b * 9 + (g - 8))
                sp.dma_start(kpage[g], k_pages[ds(page, 1)].rearrange("g t n -> t (g n)")).then_inc(k_in[g], 16)

            def load_mem_keys(b, first=False):
                if not first:
                    sp.wait_ge(kt_filled, b * 9)
                sp.dma_start(mk_in, cache_mem_k[0][ds(b, 1)].rearrange("b (a t) h d -> t (b a) (h d)", t=P)).then_inc(mk_loaded, 16)

            for g in (0, 1, 2, 5, 6, 7):
                load_key_page(0, g, True)
            sp.wait_ge(pa_out, NU)
            for g in (3, 4):
                load_key_page(0, g, True)
            load_mem_keys(0, True)
            with sp.Fori(0, NB - 1) as i:
                for g in range(NPG):
                    load_key_page(i + 1, g)
                load_mem_keys(i + 1)

            sp.wait_ge(hn_done, NN)
            sp.dma_start(wo_slot[0], w_out_d[:, :, 0:256]).then_inc(wo_in[0], 16)
            sp.wait_ge(d_pv, NB)
            sp.wait_ge(d_ot, NB)
            for n in (1, 2):
                sp.dma_start(wo_slot[n], w_out_d[:, :, n * 256:(n + 1) * 256]).then_inc(wo_in[n], 16)
            sp.wait_ge(out_done, 16 * no)
            for t, (t0, n) in enumerate(TILES):
                sp.dma_start(h_tok[0:n, t, :], x_tok_d[t]).then_inc(x_again, 16)
            sp.dma_start(b_rt[:, 0:NG], b_router_group).then_inc(rt_in, 16)
            sp.dma_start(b_rt[:, NG:NG + NE], b_router_expert).then_inc(rt_in, 16)
            sp.dma_start(w_rt[:, :, 0:NG], w_rg_d).then_inc(rt_in, 16)
            sp.dma_start(w_rt[:, :, NG:NG + NE], w_re_d).then_inc(rt_in, 16)
            for n in range(3, 8):
                sp.wait_ge(wo_filled, 2 * (n - 2))
                sp.dma_start(wo_slot[n % 3], w_out_d[:, :, n * 256:(n + 1) * 256]).then_inc(wo_in[n % 3], 16)

            def load_unit(p, u, slot):
                x, half, which = u % 2, (u // 2) % 2, u // 4
                k = (KC, KC, FB)[which] // 2
                src = (w_gate_d, w_up_d, w_down_d)[which][ds(p * 2 + x, 1), :, half * k:(half + 1) * k, :]
                sp.dma_start(unit[slot].rearrange("p (k n) -> p k n", k=k), src.rearrange("e p k n -> p (e k) n")).then_inc(unit_in[slot], 16)

            def ring_loads(p):
                for u in range(UNITS_PAIR):
                    if u < 5:
                        sp.wait_ge(units_used, p * UPP - (4 - u))
                    elif u == 5:
                        sp.wait_ge(yst_filled, p * 4)
                    else:
                        sp.wait_ge(units_used, p * UPP + (u - 5))
                    load_unit(p, u, u % 6)

            for u in range(3):
                load_unit(0, u, u)
            sp.wait_ge(wo_filled, 14)
            load_unit(0, 3, 3)
            sp.wait_ge(h_added, 3 * KC)
            for u in (4, 5):
                load_unit(0, u, u)
            for t, (t0, n) in enumerate(TILES):
                sp.dma_start(y_tok_d[t], h_tok[0:n, t, :]).then_inc(h_out, 16)
            for u in range(6, UNITS_PAIR):
                sp.wait_ge(units_used, u - 5)
                load_unit(0, u, u % 6)
            with sp.Fori(0, PAIRS - 1) as i:
                ring_loads(i + 1)
            sp.wait_ge(h_out, 48)
            for t, (t0, n) in enumerate(TILES):
                sp.dma_start(h_back[0:n, t, :], y_tok_d[t]).then_inc(h_again, 16)

            def expert_loads(e, first=False):
                for c in range(2):
                    cols = slice(c * 256, (c + 1) * 256)
                    if not first:
                        sp.wait_ge(mg_filled, e * 4 + (2 * c - 2))
                    sp.dma_start(wg_u[c], w_gate_d[ds(e, 1), :, :, cols].rearrange("e p k n -> p (e k) n")).then_inc(unit_in[2 * c], 16)
                    if not first:
                        sp.wait_ge(mu_filled, e * 4 + (2 * c - 2))
                    sp.dma_start(wu_u[c], w_up_d[ds(e, 1), :, :, cols].rearrange("e p k n -> p (e k) n")).then_inc(unit_in[2 * c + 1], 16)
                for c in range(2):
                    cols = slice(c * 1024, (c + 1) * 1024)
                    if not first:
                        sp.wait_ge(md_filled, e * 16 + (8 * c - 7))
                    sp.dma_start(wd_u[c], w_down_d[ds(e, 1), :, :, cols].rearrange("e p k n -> p (e k) n")).then_inc(unit_in[4 + c], 16)

            sp.wait_ge(overflow_set, 1)
            n_past = sp.value_load(overflow[0:1, 0:1], min_val=0, max_val=2 * T)
            with sp.If(n_past > 0):
                sp.wait_ge(ht_filled, KC + HT_FILLS)
                expert_loads(0, True)
                with sp.Fori(0, NE - 1) as e:
                    expert_loads(e + 1)
            for t, (t0, n) in enumerate(TILES):
                sp.wait_ge(y_done, 4 * t + 4)
                sp.dma_start(y_tok_d[t], h_back[0:n, t, :]).then_inc(h_out, 16)
            sp.wait_ge(h_out, 96)

        @block.gpsimd
        def _(pool):
            n_set = 0

            def fill(ap, v):
                nonlocal n_set
                pool.memset(ap, v).then_inc(consts_set, 1)
                n_set += 1

            def pick(ap, op, value, base, pattern, cm):
                nonlocal n_set
                pool.wait_ge(consts_set, n_set)
                pool.affine_select(out=ap, in_=ap, compare_op=op, fill=value, base=base, pattern=pattern,
                                   channel_multiplier=cm).then_inc(consts_set, 1)
                n_set += 1

            fill(ident[:, :], 0.0)
            fill(ones[:, :], 1.0)
            pick(ident[:, :], ALU.not_equal, 1.0, 0, [[-1, P]], 1)
            fill(eps_t[:, :], EPS)
            fill(one_t[:, :], 1.0)
            fill(tri_le[:, :], 1.0)
            fill(tri_gt[:, :], 1.0)
            fill(causal[:, :], 0.0)
            fill(sel48[:, :, :, :], 0.0)
            fill(causal4[:, :, :], 0.0)
            fill(rep4[:, :, :], 0.0)
            fill(batch_of[:, :], 1.0)
            fill(chunk_of[:, :], 1.0)
            fill(row_of[:, :], 0.0)
            pick(tri_le[:, :], ALU.is_ge, 0.0, 0, [[1, P]], -1)
            pick(tri_gt[:, :], ALU.is_gt, 0.0, 0, [[-1, P]], 1)
            pick(causal[:, :], ALU.is_ge, NEG, 0, [[-1, P]], 1)
            pick(sel48[:, :, :, :], ALU.not_equal, 1.0, 0, [[-HF, NB], [-1, HF], [0, NL]], 1)
            pick(causal4[:, :, :], ALU.is_ge, NEG, 0, [[-NL, NB], [1, NS]], 0)
            pick(causal4[:, :, :], ALU.is_ge, NEG, 0, [[NL, NB], [-1, NS]], 1)
            pick(rep4[:, :, :], ALU.not_equal, 1.0, 0, [[0, 8], [-1, NL]], 1)
            pick(batch_of[:, :], ALU.is_ge, 0.0, 0, [[-NL, NB]], 1)
            pick(batch_of[:, :], ALU.is_ge, 0.0, NL - 1, [[NL, NB]], -1)
            pick(chunk_of[:, :], ALU.is_ge, 0.0, 0, [[-CH, P // CH]], 1)
            pick(chunk_of[:, :], ALU.is_ge, 0.0, CH - 1, [[CH, P // CH]], -1)
            pick(row_of[:, :], ALU.not_equal, 1.0, 1 - NN, [[1, 2 * NN - 1]], 0)
            assert n_set == N_CONSTS, n_set
            pool.dma_start(ptab[:, :], page_table.rearrange("b (g a) -> (b g) a", a=1)).then_inc(ptab_in, 16)
            pool.wait_ge(ptab_in, 16)
            pool.indirect_dma_start(out=lfpages, out_offset=None, in_=logf_d,
                                    in_offset=bass.IndirectOffsetOnAxis(ap=ptab[:, 0:1], axis=0)).then_inc(lfpages_in, 16)
            pool.wait_ge(lfp_filled, 1)
            for h in range(2):
                pool.dma_start(s_in[h], state_hgrn[0, :, h].rearrange("b k v -> k b v")).then_inc(s_loaded[h], 16)
            def states_out(h):
                pool.wait_ge(ds_used, 10 * h + 8)
                pool.dma_start(hgrn_state_p[0, 0, h], states[:, NCH - 1, :]).then_inc(stp_out, 16)
                pool.wait_ge(ds_used, 10 * h + 10)
                pool.dma_start(hgrn_state_s[0, :, h].rearrange("b k v -> k b v"), s_in[h % 2]).then_inc(sts_out[h % 2], 16)
                if h + 2 < HG:
                    pool.wait_ge(sts_out[h % 2], 16 * (h // 2 + 1))
                    pool.dma_start(s_in[h % 2], state_hgrn[0, :, h + 2].rearrange("b k v -> k b v")).then_inc(s_loaded[h % 2], 16)

            pool.wait_ge(vt_drained, 6)
            for h in range(HG):
                for c in range(2):
                    if h:
                        pool.wait_ge(ds_filled, 10 * (h - 1) + 9 + c)
                    pool.tensor_tensor(vmask[c], vsam[:, h * P:(h + 1) * P].rearrange("p (a v) -> p a v", a=1).to_broadcast([NS, 4, P]),
                                       batch_of[:, 4 * c:4 * c + 4].rearrange("p (b a) -> p b a", a=1).to_broadcast([NS, 4, P]),
                                       ALU.mult).then_inc(sm_set, 1)
                if h:
                    states_out(h - 1)
            states_out(HG - 1)
            pool.wait_ge(stp_out, 16 * HG)
            for n in range(2):
                pool.wait_ge(sts_out[n], 16 * HG // 2)

            pool.wait_ge(ptrow_in, 16)
            pool.wait_ge(blk_filled, 55)

            def load_values(b, first=False):
                for g in range(NPG):
                    page = pool.value_load(ptab_row[0:1, ds(b * NPG + g, 1)], min_val=0, max_val=POOL - 1)
                    if not first:
                        pool.wait_ge(d_pv, b)
                    pool.dma_start(vpages[:, g, :], v_pages[ds(page, 1)].rearrange("g t n -> t (g n)")).then_inc(v_loaded, 16)
                if first:
                    pool.wait_ge(pa_out, NU)
                else:
                    pool.wait_ge(d_pv, b)
                pool.dma_start(mv_in, cache_mem_v[0][ds(b, 1)].rearrange("b (a t) h d -> t (b a) (h d)", t=P)).then_inc(v_loaded, 16)

            load_values(0, True)
            with pool.Fori(0, NB - 1) as i:
                load_values(i + 1)
            pool.wait_ge(wo_drained, KC)
            pool.memset(h_scaled[:, 2, :], 0.0).then_inc(consts_set, 1)

        @block.scalar
        def _(act):
            act.wait_ge(consts_set, N_CONSTS)
            act.wait_ge(ssq_clear, 1)
            for group in ((0, 1), (2, 3, 4)):
                for n in group:
                    src, m, c = NORM[n]
                    act.wait_ge(tok_in[n], 16)
                    if n:
                        act.wait_ge(ssq_done, n)
                    act.activation(junk[0:m, :], src[0:m], ACT.Square, accum_out=ssq[0:m, c:c + 1]).then_inc(ssq_done, 1)
                for n in group:
                    src, m, c = NORM[n]
                    act.wait_ge(ssq_done, n + 1)
                    act.activation(rstd[0:m, c:c + 1], ssq[0:m, c:c + 1], ACT.Sqrt, bias=eps_t[0:m, :], scale=1.0 / D).then_inc(sqrt_done, 1)
            act.wait_ge(lb_diff, 1)
            act.activation(lbw[:, 2:4, :], lbw[:, 0:2, :], ACT.Exp).then_inc(lb_exp, 1)
            for j in range(8):
                act.wait_ge(blk_filled, j + 1)
                act.activation(mraw[:, j, :], PS[:, j, 0:MEM], ACT.Copy).then_inc(blk_drained, 1)
            with act.Fori(0, 3) as i:
                for n, j in enumerate(ORDER):
                    act.wait_ge(blk_filled, i * 6 + (8 + n + 1))
                    act.activation(raw[:, ds(i * 6 + n, 1), :], PS[:, j:j + 1, 0:T], ACT.Copy).then_inc(blk_drained, 1)
            act.wait_ge(blk_drained, 26)
            with act.Fori(0, 3) as g:
                act.wait_ge(hg_done, g + 1)
                zq, zf = raw[:, ds(g * 2 + HQ, 2), :], raw[:, ds(g * 2 + HFG, 2), :]
                act.activation(gQ, zq, ACT.Sigmoid)
                act.activation(gF, zf, ACT.Sigmoid)
                act.activation(gW[0], zf, ACT.Sigmoid, scale=-1.0)
                act.activation(gV, raw[:, ds(g * 2 + HI, 2), :], ACT.Copy).then_inc(hg_prep, 1)
                for n, j in enumerate(ORDER):
                    act.wait_ge(blk_filled, g * 6 + (26 + n + 1))
                    act.activation(raw[:, ds(g * 6 + (HGT + n), 1), :], PS[:, j:j + 1, 0:T], ACT.Copy).then_inc(blk_drained, 1)

            def block_out(n):
                act.wait_ge(blk_filled, 44 + n + 1)
                act.activation(raw[:, LAST[n], :], PS[:, n % 4, 0:T], ACT.Copy).then_inc(blk_drained, 1)

            act.wait_ge(parity_set, 1)
            act.wait_ge(hg_done, 4)
            for f in range(6):
                t, c, m = f // 2, (f % 2) * 4, 4 - 2 * (f % 2)
                act.wait_ge(vt_filled, f + 1)
                src = PS[:, 6 + f % 2, 0:m * P]
                if t < 2:
                    act.activation(vpar[:, 0, t, c * P:(c + m) * P], src, ACT.Copy, scale=parity[:, 0:1])
                    act.activation(vpar[:, 1, t, c * P:(c + m) * P], src, ACT.Copy, scale=parity[:, 1:2]).then_inc(vt_drained, 1)
                else:
                    act.activation(vsam[:, c * P:(c + m) * P], src[0:NS], ACT.Copy).then_inc(vt_drained, 1)
            block_out(0)
            for h in range(HG):
                act.wait_ge(kt2_filled, h + 1)
                if h:
                    act.wait_ge(ds_filled, 10 * h)
                act.activation(ktil[:, 0:2, :], PS[:, 6, 0:2 * P].rearrange("p (a k) -> p a k", a=2), ACT.Copy)
                act.activation(ktil[0:NS, 2, :], PS[0:NS, 6, 2 * P:3 * P], ACT.Copy).then_inc(kt2_drained, 1)
                if h >= 2:
                    act.wait_ge(gate_done, h - 1)
                act.activation(sq[:, h % 2, :], raw[:, HGT + h, :], ACT.Sigmoid).then_inc(sig_done, 1)
                block_out(h + 1)
            for n in range(7, 10):
                block_out(n)
            act.wait_ge(blk_filled, 55)
            act.wait_ge(wff_in, 32)
            act.activation(ffz[:, :], PS[0:HF, 2, 0:T], ACT.Identity, bias=b_f[:, :]).then_inc(blk_drained, 1)

            act.wait_ge(blk_drained, 55)
            act.wait_ge(gate_done, HG)
            for n, (src, w, g) in enumerate(NORMS):
                if n == NN - HG:
                    act.wait_ge(o_added, HG)
                if n >= 2:
                    act.wait_ge(hn_sum, n - 1)
                act.activation(sq[:, n % 2, 0:w], src, ACT.Square).then_inc(hn_sq, 1)
            act.wait_ge(hn_sum, NN)
            act.activation(hn_r[:, :], PS[0:NN, 0, 0:T], ACT.Sqrt, bias=eps_t[0:NN, :], scale=1.0 / P).then_inc(hn_sqrt, 1)

            def tokens_out(n):
                dst, m, srcs = TOKF[n]
                act.wait_ge(tk_filled, n + 1)
                act.activation(dst, PS[0:m, 6 + n % 2, 0:len(srcs) * P], ACT.Copy).then_inc(tk_drained, 1)

            act.wait_ge(stp_out, 16 * HG)
            for n in range(2):
                act.wait_ge(sts_out[n], 16 * HG // 2)
            for n in range(NVF):
                tokens_out(n)

            act.activation(ffw[:, :], ffz[:, :], ACT.Abs).then_inc(lf_act, 1)
            act.wait_ge(lf_act, 1)
            act.activation(ffw[:, :], ffw[:, :], ACT.Exp, scale=-1.0).then_inc(lf_act, 1)
            act.wait_ge(lf_act, 2)
            act.activation(ffw[:, :], ffw[:, :], ACT.Ln, bias=one_t[0:HF, :]).then_inc(lf_act, 1)

            for n in range(NVF, NTF):
                tokens_out(n)
            act.wait_ge(c_filled, 1)
            act.activation(negc[:, :], PS[0:HF, 5, 0:SEQ], ACT.Copy, scale=-1.0).then_inc(negc_set, 1)
            act.wait_ge(dec_filled, 1)
            act.activation(decay[:, :], PS[0:NB * HF, 0:3, :].rearrange("p a b -> p (a b)")[:, 0:KEYS], ACT.Copy).then_inc(decay_set, 1)

            for s in range(NU + 2):
                if s < NU:
                    act.wait_ge(pa_max, s + 1)
                    if s >= 2:
                        act.wait_ge(pa_t, s - 1)
                    act.activation(probs[:, s % 2, 0:width(s)], PS[:, s % 2, 0:width(s)], ACT.Exp, bias=nmax[:, s % 2:s % 2 + 1],
                                   accum_out=psum_p[:, s % 2:s % 2 + 1]).then_inc(pa_exp, 1)
                if s >= 2:
                    fox, h, qb = UNITS[s - 2]
                    act.wait_ge(pa_pv, s - 1)
                    act.activation(cat[:, h if fox else 12 + h, qb * P:(qb + 1) * P], PS[:, 4 + s % 2, 0:P], ACT.Copy).then_inc(pa_out, 1)

            def keys_out(b, u, first=False):
                for g in range(9):
                    bank = 2 * ((u + g) % 2)
                    if g == 0 and not first:
                        act.wait_ge(d_scored, b)
                    act.wait_ge(kt_filled, b * 9 + (g + 1))
                    src = PS[:, bank, :].rearrange("p (h t) -> p h t", t=P)
                    if g < NPG:
                        act.activation(keysT[:, 0:4, g * P:(g + 1) * P], src, ACT.Copy).then_inc(kt_act, 1)
                    else:
                        act.activation(mkeysT[:, 0:2, :], PS[:, bank, :].rearrange("p (h t) -> p h t", t=MEM), ACT.Copy).then_inc(kt_act, 1)

            def decode_exp(b, first=False):
                act.wait_ge(d_max, b + 1)
                if not first:
                    act.wait_ge(d_t, b)
                    act.wait_ge(d_oc, b)
                act.activation(dprob, PS[:, 4:7, :].rearrange("p a b -> p (a b)")[:, 0:KEYS], ACT.Exp, bias=nmax[:, 2:3],
                               accum_out=psum_p[:, 2:3])
                act.activation(mprob, PS[:, 6, 64:64 + MEM], ACT.Exp, bias=nmax[:, 3:4],
                               accum_out=psum_p[:, 3:4]).then_inc(d_exp, 1)

            def probs_out(b):
                act.wait_ge(d_t, b + 1)
                act.activation(dprobT[:, 0:4, :], PS[:, 4, :].rearrange("p (g r) -> p g r", r=P), ACT.Copy).then_inc(d_tc, 1)

            def outputs_out(b):
                act.wait_ge(d_pv, b + 1)
                act.wait_ge(d_rcp, b + 1)
                act.activation(dout[:, 0, :], PS[:, 7, 0:P], ACT.Copy, scale=psum_p[:, 2:3])
                act.activation(dout[0:64, 1, :], PS[0:64, 7, P:2 * P], ACT.Copy, scale=psum_p[0:64, 2:3])
                act.activation(dout[:, 2, :], PS[:, 7, 2 * P:3 * P], ACT.Copy, scale=psum_p[:, 3:4]).then_inc(d_oc, 1)

            keys_out(0, 0, True)
            decode_exp(0, True)
            keys_out(1, 1)
            probs_out(0)
            outputs_out(0)
            with act.Fori(0, 3) as i:
                for u in range(2):
                    decode_exp(i * 2 + (u + 1))
                    keys_out(i * 2 + (u + 2), u)
                    probs_out(i * 2 + (u + 1))
                    outputs_out(i * 2 + (u + 1))
            decode_exp(NB - 1)
            probs_out(NB - 1)
            outputs_out(NB - 1)

            def block_squares(n):
                act.wait_ge(h_added, 3 * n + 3)
                for t, (t0, w) in enumerate(TILES):
                    if n or t:
                        act.wait_ge(h_ssq, 3 * n + t)
                    act.activation(sq_out[0:w, :], h_tok[0:w, t, n * P:(n + 1) * P], ACT.Square,
                                   accum_out=ssq_part[0:w, t, n:n + 1]).then_inc(h_ssq, 1)

            act.wait_ge(moe_prep, 1)
            for n in range(KC):
                act.wait_ge(wo_filled, n + 1)
                if n >= 2:
                    act.wait_ge(at_filled, n - 1)
                act.activation(attnT[:, n % 2, :], PS[:, n % 2, 0:T], ACT.Copy).then_inc(wo_drained, 1)
                if n >= 2:
                    block_squares(n - 2)
            block_squares(KC - 2)
            block_squares(KC - 1)
            act.wait_ge(h_rstd, 1)
            act.activation(rstd[:, 5:8], ssq[:, 5:8], ACT.Sqrt, bias=eps_t[:, :], scale=1.0 / D).then_inc(h_rstd, 1)
            act.wait_ge(h_rstd, 3)
            for t in range(2):
                act.activation(h_scaled[:, t, :], h_tok[:, t, :], ACT.Copy, scale=rstd[:, 5 + t:6 + t]).then_inc(h_scl, 1)
            for n, (o, i) in enumerate(((rw[:, :, 0:NG], rw[:, :, 0:NG]), (rw[:, :, 60:61], rw[:, :, 60:61]))):
                act.wait_ge(rt_sub, n + 1)
                act.activation(o, i, ACT.Exp).then_inc(rt_exp, 1)
            act.wait_ge(consts_set, N_CONSTS + 1)
            act.activation(h_scaled[0:NS, 2, :], h_tok[0:NS, 2, :], ACT.Copy, scale=rstd[0:NS, 7:8]).then_inc(h_scl, 1)
            def pair_act(p):
                act.wait_ge(units_used, p * UPP + 4)
                act.activation(hS[:, :], PS[:, 0, :], ACT.Silu).then_inc(pair_silu, 1)
                act.wait_ge(ph_filled, p + 1)
                act.activation(hT.rearrange("p k s -> p (k s)"), PS[:, 6, :], ACT.Copy).then_inc(pair_hT, 1)
                act.wait_ge(g_filled, p + 1)
                act.activation(gate_slot[:, :], PS[:, 7, 0:T], ACT.Copy).then_inc(g_copied, 1)
                for n in (0, 2):
                    act.wait_ge(yst_filled, p * 4 + (n + 1))
                    act.activation(yslot[:, n * 512:(n + 1) * 512], PS[:, YB[n], :], ACT.Copy).then_inc(yst_act, 1)

            act.wait_ge(h_out, 48)
            with act.Fori(0, PAIRS) as p:
                pair_act(p)

            act.wait_ge(overflow_set, 1)
            n_past = act.value_load(overflow[0:1, 0:1], min_val=0, max_val=2 * T)
            with act.If(n_past > 0):
                with act.Fori(0, NE) as e:
                    act.wait_ge(g_filled, e + (PAIRS + 1))
                    act.activation(gbc[:, :], PS[:, 6, 0:T], ACT.Copy).then_inc(g_copied, 1)
                    for j in range(FB):
                        act.wait_ge(mg_filled, e * 4 + (j + 1))
                        act.wait_ge(hs_done, e * 4 + (j + 1))
                        act.activation(g_hS[:, j % 2, :], PS[:, j % 2, 0:T], ACT.Silu).then_inc(pair_silu, 1)

        @block.vector
        def _(dve):
            steps = [0]

            def step(ins):
                steps[0] += 1
                ins.then_inc(dve_step, 1)
                dve.wait_ge(dve_step, steps[0])

            dve.memset(ssq[:, :], 1.0).then_inc(ssq_clear, 1)
            dve.wait_ge(cols_filled, 1)
            dve.tensor_copy(cols[:, :], PS[:, 7, 0:65]).then_inc(cols_set, 1)
            dve.wait_ge(cols_set, 1)
            dve.tensor_scalar(gq[:, 0:1], g_fq, SCALE, None, ALU.mult).then_inc(gains_set, 1)
            dve.tensor_scalar(gq[:, 2:3], g_mq, SCALE, None, ALU.mult).then_inc(gains_set, 1)
            dve.tensor_copy(gq[:, 1:2], g_fk).then_inc(gains_set, 1)
            dve.tensor_copy(gq[:, 3:4], g_mk).then_inc(gains_set, 1)

            dve.tensor_copy(gq[:, 4:5], g_hn).then_inc(gains_set, 1)
            step(dve.tensor_tensor(lbw[:, 2, :], lb0, lb1, ALU.max))
            dve.tensor_tensor(lbw[:, 0, :], lb0, lbw[:, 2, :], ALU.subtract)
            dve.tensor_tensor(lbw[:, 1, :], lb1, lbw[:, 2, :], ALU.subtract).then_inc(lb_diff, 1)

            def drain(f):
                n, c, m = FILLS[f]
                w = NORM[n][1]
                dst, g = (memT, G_MEM) if n < 2 else (xT, G_ATT)
                t0 = (n if n < 2 else n - 2) * P
                dve.wait_ge(tT_filled, f + 1)
                dve.tensor_tensor(dst[:, c:c + m, t0:t0 + w], fill_out(f, w),
                                  g[:, c:c + m].rearrange("p (c a) -> p c a", a=1).to_broadcast([P, m, w]),
                                  ALU.mult).then_inc(tT_drained, 1)

            for n, (src, m, c) in enumerate(NORM):
                dve.wait_ge(sqrt_done, n + 1)
                step(dve.reciprocal(rstd[0:m, c:c + 1], rstd[0:m, c:c + 1]))
                dve.tensor_scalar(src[0:m], src[0:m], rstd[0:m, c:c + 1], None, ALU.mult).then_inc(scaled, 1)
                if n == 1:
                    for f in range(8):
                        drain(f)
                if n >= 3:
                    for f in range(4 * n - 4, 4 * n):
                        drain(f)
            drain(16)

            dve.wait_ge(lfp_filled, 1)
            dve.tensor_copy(lfp[:, :, :, :].rearrange("p g b h -> p h b g"),
                            PS[:, 6, 0:HF * 64].rearrange("p (h b g) -> p h b g", h=HF, b=NB)).then_inc(lfp_drained, 1)
            dve.wait_ge(lfp_drained, 1)
            step(dve.memset(lfs[:, NPG - 1, :, :], 0.0))
            for g in range(NPG - 2, -1, -1):
                step(dve.tensor_tensor(lfs[:, g, :, :], lfs[:, g + 1, :, :], lfp[:, g + 1, :, :], ALU.add))
            dve.wait_ge(lb_exp, 1)
            step(dve.tensor_tensor(lbw[:, 0, :], lbw[:, 2, :], lbw[:, 3, :], ALU.add))
            step(dve.reciprocal(lbw[:, 1, :], lbw[:, 0, :]))
            dve.tensor_tensor(LB, lbw[:, 2, :], lbw[:, 1, :], ALU.mult).then_inc(lb_set, 1)
            dve.tensor_tensor(LB1, lbw[:, 3, :], lbw[:, 1, :], ALU.mult).then_inc(lb_set, 1)
            for n in range(2):
                dve.tensor_reduce(parity[:, n:n + 1], chunk_of[:, :].rearrange("p (a b) -> p b a", b=2)[:, n, :], AX.X, ALU.add)
            dve.memset(nmax[:, :], 0.0).then_inc(parity_set, 1)
            dve.memset(psum_p[:, 0:1], 0.0).then_inc(hg_done, 1)
            dve.memset(psum_p[:, 1:2], 0.0).then_inc(intra_used, 1)
            dve.wait_ge(lb_set, 2)

            def pr(a):
                return a[:, :, 0:SEQ].rearrange("p h (n t) -> p h n t", t=CH)

            def sa(a):
                return a[:, :, SEQ:T].rearrange("p h (n t) -> p h n t", t=NL)

            def packed(buf, j):
                return buf.rearrange("p h t -> p (h t)")[:, 0:2 * NCH * (CH - j)].rearrange("p (h n t) -> p h n t", h=2, n=NCH)

            S_OFF = [0, 64, 112, 144]

            def spacked(a, j):
                return a[:, S_OFF[j]:S_OFF[j] + 16 * (NL - j)].rearrange("p (h n t) -> p h n t", h=2, n=NB)

            with dve.Fori(0, 3) as g:
                n_step = 0

                def gstep(ins):
                    nonlocal n_step
                    n_step += 1
                    ins.then_inc(hg_step, 1)
                    dve.wait_ge(hg_step, g * G_STEPS + n_step)

                hg = ds(g * 2, 2)
                lb1b = lbw[:, 5, hg].rearrange("p (h a) -> p h a", a=1).to_broadcast([P, 2, T])
                lbb = lbw[:, 4, hg].rearrange("p (h a) -> p h a", a=1).to_broadcast([P, 2, T])
                dve.wait_ge(hg_prep, g + 1)
                dve.scalar_tensor_tensor(out=gQ, in0=raw[:, ds(g * 2 + HQ, 2), :], scalar=SCALE, in1=gQ, op0=ALU.mult, op1=ALU.mult)
                dve.tensor_tensor(gW[0], gW[0], lb1b, ALU.mult)
                gstep(dve.tensor_tensor(gF, gF, lb1b, ALU.mult))
                gstep(dve.tensor_tensor(gF, gF, lbb, ALU.add))

                def add_distance(j):
                    dve.wait_ge(intra_filled, g * 17 + (j + 1))
                    o = gO if j == 0 else gTmp
                    dve.tensor_tensor(pr(o)[:, :, :, j:CH], packed(PS[:, 6 + j % 2, :].rearrange("p (h t) -> p h t", h=2), j),
                                      pr(gV)[:, :, :, 0:CH - j], ALU.mult).then_inc(intra_used, 1)
                    dve.wait_ge(intra_used, g * 17 + (j + 2))
                    if j:
                        gstep(dve.tensor_tensor(pr(gO)[:, :, :, j:CH], pr(gO)[:, :, :, j:CH], pr(gTmp)[:, :, :, j:CH], ALU.add))

                for j in range(CH):
                    w, w0 = gW[j % 2], gW[(j + 1) % 2]
                    if j:
                        if j < NL:
                            dve.tensor_tensor(sa(w)[:, :, :, j:NL], sa(gF)[:, :, :, j:NL], sa(w0)[:, :, :, j - 1:NL - 1], ALU.mult)
                        gstep(dve.tensor_tensor(pr(w)[:, :, :, j:CH], pr(gF)[:, :, :, j:CH], pr(w0)[:, :, :, j - 1:CH - 1], ALU.mult))
                    dve.tensor_copy(pr(gKT)[:, :, :, CH - 1 - j:CH - j], pr(w)[:, :, :, CH - 1:CH])
                    if j < NL:
                        dve.tensor_copy(sa(gKT)[:, :, :, NL - 1 - j:NL - j], sa(w)[:, :, :, NL - 1:NL])
                        dve.tensor_tensor(spacked(gS, j), sa(gQ)[:, :, :, j:NL], sa(w)[:, :, :, j:NL], ALU.mult)
                    if j >= 2:
                        dve.wait_ge(intra_filled, g * 17 + (j - 1))
                    dve.tensor_tensor(packed(gQW[j % 2], j), pr(gQ)[:, :, :, j:CH], pr(w)[:, :, :, j:CH], ALU.mult).then_inc(qw_ready, 1)
                    if j:
                        add_distance(j - 1)
                add_distance(CH - 1)
                dve.wait_ge(intra_filled, g * 17 + 17)
                for j in range(NL):
                    o = gO if j == 0 else gTmp
                    ins = dve.tensor_tensor(sa(o)[:, :, :, j:NL], spacked(PS[:, 6, :], j), sa(gV)[:, :, :, 0:NL - j], ALU.mult)
                    if j == NL - 1:
                        ins.then_inc(intra_used, 1)
                        dve.wait_ge(intra_used, g * 17 + 18)
                    else:
                        gstep(ins)
                    if j:
                        gstep(dve.tensor_tensor(sa(gO)[:, :, :, j:NL], sa(gO)[:, :, :, j:NL], sa(gTmp)[:, :, :, j:NL], ALU.add))
                keep, start = gW
                gstep(dve.tensor_copy(keep, gF))
                gstep(dve.memset(start, 0.0))
                for v in (pr, sa):
                    dve.memset(v(keep)[:, :, :, 0:1], 0.0)
                    ins = dve.tensor_copy(v(start)[:, :, :, 0:1], v(gF)[:, :, :, 0:1])
                gstep(ins)
                flat = [a.rearrange("p h t -> p (h t)") for a in (gTmp, keep, start)]
                gstep(dve.tensor_tensor_scan(flat[0], flat[1], flat[2], 0.0, ALU.mult, ALU.add))
                dve.tensor_tensor(raw[:, ds(g * 2 + HQ, 2), :], gQ, gTmp, ALU.mult)
                dve.tensor_copy(decays[:, hg, 0:NCH], pr(gTmp)[:, :, :, CH - 1])
                dve.tensor_copy(decays[:, hg, NCH:NCH + NB], sa(gTmp)[:, :, :, NL - 1])
                dve.tensor_copy(raw[:, ds(g * 2 + HFG, 2), :], gKT)
                dve.tensor_copy(cat[:, ds(g * 2 + 6, 2), :], gO).then_inc(hg_done, 1)
                assert n_step == G_STEPS, n_step

            dve.wait_ge(hg_done, 4)
            n_st = 0

            def ststep(ins):
                nonlocal n_st
                n_st += 1
                ins.then_inc(st_step, 1)
                dve.wait_ge(st_step, n_st)

            def add_inter(h):
                dve.wait_ge(oi_filled, h + 1)
                o = cat[:, 6 + h, CH:T]
                dve.tensor_tensor(o, o, PS[:, 7, CH:T], ALU.add).then_inc(o_added, 1)

            for h in range(HG):
                if h:
                    add_inter(h - 1)
                for c in range(8):
                    dve.wait_ge(ds_filled, 10 * h + c + 1)
                    if c == 7 and h:
                        dve.wait_ge(stp_out, 16 * h)
                    for n in (2 * c, 2 * c + 1):
                        d = PS[:, 4 + c % 2, (n % 2) * P:(n % 2 + 1) * P]
                        if n == 0:
                            ins = dve.tensor_copy(states[:, 0, :], d)
                        else:
                            ins = dve.scalar_tensor_tensor(out=states[:, n, :], in0=states[:, n - 1, :], scalar=decays[:, h, n:n + 1],
                                                           in1=d, op0=ALU.mult, op1=ALU.add)
                        if n % 2 == 0:
                            ststep(ins)
                        else:
                            ins.then_inc(ds_used, 1)
                            dve.wait_ge(ds_used, 10 * h + c + 1)
                dve.wait_ge(os_filled, h + 1)
                for c in range(2):
                    sn = s_in[h % 2][:, 4 * c:4 * c + 4, :]
                    ststep(dve.tensor_tensor(sn, sn, decays[:, h, NCH + 4 * c:NCH + 4 * c + 4].rearrange("p (b a) -> p b a", a=1)
                                             .to_broadcast([P, 4, P]), ALU.mult))
                    dve.wait_ge(ds_filled, 10 * h + 9 + c)
                    dve.tensor_tensor(sn, sn, PS[:, 4 + c % 2, :].rearrange("p (b v) -> p b v", b=4), ALU.add).then_inc(ds_used, 1)
                dve.wait_ge(sig_done, h + 1)
                dve.tensor_tensor(raw[:, HGT + h, :], raw[:, HGT + h, :], sq[:, h % 2, :], ALU.mult).then_inc(gate_done, 1)
            add_inter(HG - 1)
            dve.memset(psum_p[:, :], 0.0).then_inc(lfs_done, 1)

            dve.wait_ge(gains_set, 5)
            dve.wait_ge(hn_sqrt, 1)
            dve.reciprocal(hn_r[:, :], hn_r[:, :]).then_inc(hn_rcp, 1)
            for n, (src, w, g) in enumerate(NORMS):
                dve.wait_ge(hn_rows, n + 1)
                dve.scalar_tensor_tensor(out=src, in0=src, scalar=gq[:, g:g + 1], in1=PS[:, 1 + n % 3, 0:w],
                                         op0=ALU.mult, op1=ALU.mult).then_inc(hn_done, 1)
                if n >= NN - HG:
                    dve.wait_ge(hn_done, n + 1)
                    h = n - (NN - HG)
                    step(dve.tensor_tensor(cat[:, 6 + h, :], cat[:, 6 + h, :], raw[:, HGT + h, :], ALU.mult))

            dve.wait_ge(lf_act, 3)
            dve.scalar_tensor_tensor(out=lfT[:, :], in0=ffz[:, :], scalar=0.0, in1=ffw[:, :],
                                     op0=ALU.min, op1=ALU.subtract).then_inc(lf_done, 1)
            dve.wait_ge(lft_filled, 1)
            step(dve.tensor_copy(lftok[:, 0:2, :], PS[:, 4, 0:2 * HF].rearrange("p (t h) -> p t h", h=HF)))
            dve.tensor_copy(lftok[0:NS, 2, :], PS[0:NS, 4, 2 * HF:3 * HF]).then_inc(lft_drained, 1)
            dve.wait_ge(lft_drained, 1)
            dve.tensor_tensor(lfm[:, :, :], lftok[0:NS, 2:3, :].to_broadcast([NS, NB, HF]),
                              batch_of[:, :].rearrange("p (b a) -> p b a", a=1).to_broadcast([NS, NB, HF]),
                              ALU.mult).then_inc(lfm_done, 1)

            for s in range(NU + 2):
                if 1 <= s <= NU:
                    u = s - 1
                    dve.wait_ge(pa_exp, u + 1)
                    step(dve.reciprocal(psum_p[:, u % 2:u % 2 + 1], psum_p[:, u % 2:u % 2 + 1]))
                    dve.tensor_scalar(probs[:, u % 2, 0:width(u)], probs[:, u % 2, 0:width(u)], psum_p[:, u % 2:u % 2 + 1], None,
                                      ALU.mult).then_inc(pa_prob, 1)
                if s >= 2:
                    u = s - 2
                    dve.wait_ge(pa_t, u + 1)
                    if u >= 2:
                        dve.wait_ge(pa_pv, u - 1)
                    dve.tensor_copy(probsT[:, u % 2, 0:width(u) // P, :],
                                    PS[:, 2 + u % 2, 0:width(u)].rearrange("p (a q) -> p a q", q=P)).then_inc(pa_tc, 1)
                if s < NU:
                    dve.wait_ge(pa_scored, s + 1)
                    if s >= 2:
                        dve.wait_ge(pa_exp, s - 1)
                    dve.tensor_reduce(nmax[:, s % 2:s % 2 + 1], PS[:, s % 2, 0:width(s)], AX.X, ALU.max, negate=True).then_inc(pa_max, 1)

            dve.memset(q_rows[:, :, :], 0.0).then_inc(q_clear, 1)
            dve.memset(sel_b[:, :, :], 0.0).then_inc(q_clear, 1)
            dve.wait_ge(q_clear, 2)

            def queries(b, first=False):
                if not first:
                    dve.wait_ge(d_scored, b)
                q = ds(b * NL + SEQ, NL)
                dve.tensor_copy(q_rows[:, 0:4, 0:NL], raw[:, FQ:FQ + 4, q])
                dve.tensor_copy(q_rows[:, 4:HF, NL:2 * NL], raw[:, FQ + 4:FQ + HF, q])
                dve.tensor_copy(q_rows[:, HF:HF + HM, 0:NL], raw[:, MQ:MQ + HM, q])
                dve.tensor_copy(causal_b.rearrange("p (a k) -> p a k", a=1), causal4[:, ds(b, 1), :])
                for j, m in ((0, 4), (1, HF - 4)):
                    ins = dve.tensor_copy(sel_b[:, 0:m, j * NL:(j + 1) * NL].rearrange("p (a h) q -> p a h q", a=1),
                                          sel48[:, ds(b, 1), 4 * j:4 * j + m, :])
                ins.then_inc(q_set, 1)

            def keys_out(b, u, gs):
                for g in gs:
                    bank = 2 * ((u + g) % 2) + 1
                    dve.wait_ge(kt_filled, b * 9 + (g + 1))
                    if g < NPG:
                        dve.tensor_copy(keysT[:, 4:6, g * P:(g + 1) * P],
                                        PS[:, bank, 0:2 * P].rearrange("p (h t) -> p h t", t=P)).then_inc(kt_dve, 1)
                    else:
                        dve.tensor_copy(mkeysT[:, 2:4, :], PS[:, bank, :].rearrange("p (h t) -> p h t", t=MEM)).then_inc(kt_dve, 1)

            def decode_max(b):
                dve.wait_ge(d_scored, b + 1)
                dve.tensor_reduce(nmax[:, 2:3], PS[:, 4:7, :].rearrange("p a b -> p (a b)")[:, 0:KEYS], AX.X, ALU.max, negate=True)
                dve.tensor_reduce(nmax[:, 3:4], PS[:, 6, 64:64 + MEM], AX.X, ALU.max, negate=True).then_inc(d_max, 1)

            def decode_sums(b):
                dve.wait_ge(d_exp, b + 1)
                dve.reciprocal(psum_p[:, 2:4], psum_p[:, 2:4]).then_inc(d_rcp, 1)

            def probs_out(b, first=False):
                dve.wait_ge(d_t, b + 1)
                dve.tensor_copy(dprobT[:, 4:NPG, :], PS[:, 5, :].rearrange("p (g r) -> p g r", r=P))
                dve.tensor_copy(dprobT[:, NPG:NPG + 2, :], PS[:, 6, 0:2 * P].rearrange("p (g r) -> p g r", r=P))
                dve.tensor_copy(dprobT[0:NS, NPG + 2, :], PS[0:NS, 6, 2 * P:3 * P]).then_inc(d_tc, 1)

            def heads_out(b):
                dve.wait_ge(d_ot, b + 1)
                o = ds(b * NL + SEQ, NL)
                dve.tensor_copy(cat[:, 0:4, o], PS[:, 7, 0:P].rearrange("p (h r) -> p h r", r=32)[:, :, 0:NL])
                dve.tensor_copy(cat[:, 4:HF, o], PS[:, 7, P:P + 64].rearrange("p (h r) -> p h r", r=32)[:, :, NL:2 * NL])
                dve.tensor_copy(cat[:, 12:16, o], PS[:, 7, 2 * P:3 * P].rearrange("p (h r) -> p h r", r=32)[:, :, 0:NL]).then_inc(d_out, 1)

            queries(0, True)
            keys_out(0, 0, range(9))
            decode_max(0)
            queries(1)
            keys_out(1, 1, range(2))
            decode_sums(0)
            keys_out(1, 1, range(2, 9))
            probs_out(0)
            with dve.Fori(0, 3) as i:
                for u in range(2):
                    decode_max(i * 2 + (u + 1))
                    queries(i * 2 + (u + 2))
                    heads_out(i * 2 + u)
                    keys_out(i * 2 + (u + 2), u, range(2))
                    decode_sums(i * 2 + (u + 1))
                    keys_out(i * 2 + (u + 2), u, range(2, 9))
                    probs_out(i * 2 + (u + 1))
            decode_max(NB - 1)
            heads_out(NB - 2)
            decode_sums(NB - 1)
            probs_out(NB - 1)
            heads_out(NB - 1)

            def block_gain(n):
                dve.wait_ge(ht_filled, n + 1)
                if n >= 2:
                    dve.wait_ge(lg_filled, n - 1)
                dve.tensor_scalar(xgain[:, n % 2, :], PS[:, 5 + n % 2, 0:T], G_FFN[:, n:n + 1], None, ALU.mult).then_inc(ht_drained, 1)

            dve.wait_ge(d_ot, NB)
            dve.memset(gates[:, :, :], 0.0)
            step(dve.memset(logits[:, :, :], 0.0))
            dve.memset(ssq_part[:, :, :], 0.0).then_inc(moe_prep, 1)
            dve.wait_ge(x_again, 48)
            for n in range(KC):
                dve.wait_ge(at_filled, n + 1)
                for t, (t0, w) in enumerate(TILES):
                    o = h_tok[0:w, t, n * P:(n + 1) * P]
                    dve.tensor_tensor(o, o, PS[0:w, 2 + n % 2, t * P:(t + 1) * P], ALU.add).then_inc(h_added, 1)
                if n == 2:
                    dve.wait_ge(bias_filled, 1)
                    dve.tensor_copy(b_all, PS[:, 7, 0:NG + NE])
                if n:
                    block_gain(n - 1)
            block_gain(KC - 1)
            dve.wait_ge(lg_filled, KC)
            dve.tensor_copy(lgT, PS[0:NG + NE, 4, 0:T]).then_inc(lgT_set, 1)
            dve.wait_ge(h_ssq, 3 * KC)
            dve.tensor_reduce(ssq[:, 5:8], ssq_part[:, :, :], AX.X, ALU.add).then_inc(h_rstd, 1)
            dve.wait_ge(h_rstd, 2)
            dve.reciprocal(rstd[:, 5:8], rstd[:, 5:8]).then_inc(h_rstd, 1)
            dve.wait_ge(h_rstd, 3)

            dve.wait_ge(lg_filled, KC + 1)
            for t, (t0, w) in enumerate(TILES):
                ins = dve.scalar_tensor_tensor(out=logits[0:w, t, :], in0=PS[0:w, 7, 64 + t * 64:64 + t * 64 + NG + NE],
                                               scalar=rstd[0:w, 5 + t:6 + t], in1=b_all[0:w, :], op0=ALU.mult, op1=ALU.add)
            step(ins)
            gl = logits[:, :, 0:NG]
            el = logits[:, :, NG:NG + NE].rearrange("p t (g e) -> p t g e", g=NG)

            def bc(a, n):
                return a.to_broadcast([P, 3, n])

            first = rw[:, :, 40:48]
            for n in range(EPG):
                ins = dve.memset(first[:, :, n:n + 1], float(EPG - n))
            step(ins)

            def one_hot(out, x, m, tmp):
                n = x.shape[2]
                step(dve.tensor_reduce(m, x, AX.X, ALU.max))
                step(dve.tensor_tensor(out, x, bc(m, n), ALU.is_equal))
                step(dve.tensor_tensor(out, out, first[:, :, 0:n], ALU.mult))
                step(dve.tensor_reduce(tmp, out, AX.X, ALU.max))
                step(dve.tensor_tensor(out, out, bc(tmp, n), ALU.is_equal))

            gm, g1, e_in, m1, o1, m2, o2, tmp = (rw[:, :, a:b] for a, b in
                                                 ((48, 49), (4, 8), (8, 16), (49, 50), (16, 24), (50, 51), (24, 32), (51, 52)))
            ge, e2, dd, ga, gb, gsum = (rw[:, :, a:b] for a, b in ((0, 4), (32, 40), (60, 61), (61, 62), (62, 63), (52, 53)))
            one_hot(g1, gl, gm, tmp)
            dve.tensor_tensor(ge, gl, bc(gm, NG), ALU.subtract).then_inc(rt_sub, 1)
            picked = choice[:, :, 0, :].rearrange("p t (g e) -> p t g e", g=NG)
            step(dve.tensor_tensor(picked, el, g1.rearrange("p t (g a) -> p t g a", a=1).to_broadcast([P, 3, NG, EPG]), ALU.mult))
            step(dve.tensor_reduce(e_in, picked.rearrange("p t g e -> p t e g"), AX.X, ALU.add))
            one_hot(o1, e_in, m1, tmp)
            step(dve.scalar_tensor_tensor(out=e2, in0=o1, scalar=NEG, in1=e_in, op0=ALU.mult, op1=ALU.add))
            one_hot(o2, e2, m2, tmp)
            dve.tensor_tensor(dd, m2, m1, ALU.subtract).then_inc(rt_sub, 1)
            dve.wait_ge(rt_exp, 2)
            step(dve.tensor_reduce(gsum, ge, AX.X, ALU.add))
            step(dve.tensor_scalar(ga, dd, 1.0, None, ALU.add))
            step(dve.tensor_tensor(ga, ga, gsum, ALU.mult))
            step(dve.reciprocal(ga, ga))
            step(dve.tensor_tensor(gb, ga, dd, ALU.mult))
            for n, o in enumerate((o1, o2)):
                c = choice[:, :, n, :].rearrange("p t (g e) -> p t g e", g=NG)
                for g in range(NG):
                    ins = dve.tensor_tensor(c[:, :, g, :], o, bc(g1[:, :, g:g + 1], EPG), ALU.mult)
            step(ins)
            step(dve.tensor_tensor(c1g, choice[:, :, 0, :], bc(ga, NE), ALU.mult))
            step(dve.tensor_tensor(rw[:, :, 0:NE], choice[:, :, 1, :], bc(gb, NE), ALU.mult))
            for t, (t0, w) in enumerate(TILES):
                ins = dve.tensor_tensor(gates[0:w, t, :], c1g[0:w, t, :], rw[0:w, t, 0:NE], ALU.add)
            ins.then_inc(gates_set, 1)
            dve.wait_ge(gates_set, 1)
            chosen = rw[:, :, NE:2 * NE]
            dve.tensor_tensor(chosen, choice[:, :, 0, :], choice[:, :, 1, :], ALU.add).then_inc(moe_prep, 1)
            dve.memset(over[:, :, :], 0.0)
            step(dve.memset(slot_of[:, :, :], 0.0))
            dve.wait_ge(moe_prep, 2)
            dve.wait_ge(rank_filled, 1)
            dve.tensor_copy(iota1, PS[:, 5, 128:128 + SLOTS])
            for t, (t0, w) in enumerate(TILES):
                ins = dve.tensor_tensor(slot_of[0:w, t, :], chosen[0:w, t, :], PS[0:w, 5, t * NE:(t + 1) * NE], ALU.mult)
            ins.then_inc(slots_set, 1)
            dve.wait_ge(slots_set, 1)

            def pick_pair(p):
                for t in range(3):
                    ins = dve.tensor_tensor(pick_tok[:, t, :, :], iota1.rearrange("p (a s) -> p a s", a=1).to_broadcast([P, 2, SLOTS]),
                                            slot_of[:, t, ds(p * 2, 2)].rearrange("p (x a) -> p x a", a=1).to_broadcast([P, 2, SLOTS]),
                                            ALU.is_equal)
                ins.then_inc(picked_set, 1)

            def gathered_out(p):
                for c in range(4):
                    dve.wait_ge(xg_filled, p * 4 + (c + 1))
                    dve.tensor_tensor(xgT[:, 4 * c:4 * c + 4, :], PS[:, 2 + c, :].rearrange("p (c s) -> p c s", s=2 * SLOTS),
                                      G_FFN[:, 4 * c:4 * c + 4].rearrange("p (c a) -> p c a", a=1).to_broadcast([P, 4, 2 * SLOTS]),
                                      ALU.mult).then_inc(xg_drained, 1)

            def pair_dve(p, first=False, last=False):
                if not first:
                    dve.wait_ge(g_filled, p)
                dve.wait_ge(picked_set, p + 1)
                for t in range(3):
                    ins = dve.tensor_tensor(pick_gate[:, t, :, :], pick_tok[:, t, :, :],
                                            gates[:, t, ds(p * 2, 2)].rearrange("p (x a) -> p x a", a=1).to_broadcast([P, 2, SLOTS]), ALU.mult)
                ins.then_inc(pg_set, 1)
                if not last:
                    dve.wait_ge(pg_set, p + 1)
                    pick_pair(p + 1)
                dve.wait_ge(pair_silu, p + 1)
                dve.wait_ge(units_used, p * UPP + 8)
                dve.tensor_tensor(hS[:, :], hS[:, :], PS[:, 1, :], ALU.mult).then_inc(pair_h, 1)
                if not last:
                    gathered_out(p + 1)
                for n in (1, 3):
                    dve.wait_ge(yst_filled, p * 4 + (n + 1))
                    dve.tensor_copy(yslot[:, n * 512:(n + 1) * 512], PS[:, YB[n], :]).then_inc(yst_dve, 1)
                for n in range(KC):
                    dve.wait_ge(part_filled, p * KC + (n + 1))
                    dve.tensor_tensor(yT[:, n, :], yT[:, n, :], PS[:, 2 + n % 4, 0:T], ALU.add).then_inc(part_added, 1)

            pick_pair(0)
            step(dve.tensor_scalar(over, slot_of, float(SLOTS), None, ALU.is_gt))
            step(dve.tensor_reduce(n_over[:, 0:1], over.rearrange("p t e -> p (t e)"), AX.X, ALU.add))
            dve.tensor_tensor(over, over, gates, ALU.mult).then_inc(slots_set, 1)
            dve.wait_ge(over_filled, 1)
            dve.tensor_copy(overflow[:, :], PS[:, 6, 0:1]).then_inc(overflow_set, 1)
            dve.wait_ge(h_out, 48)
            gathered_out(0)
            dve.memset(yT, 0.0).then_inc(moe_prep, 1)
            dve.wait_ge(moe_prep, 3)
            pair_dve(0, first=True)
            with dve.Fori(0, PAIRS - 2) as i:
                pair_dve(i + 1)
            pair_dve(PAIRS - 1, last=True)

            dve.wait_ge(h_again, 48)
            dve.wait_ge(overflow_set, 1)
            n_past = dve.value_load(overflow[0:1, 0:1], min_val=0, max_val=2 * T)
            with dve.If(n_past > 0):
                dve.wait_ge(part_added, PAIRS * KC)
                for t, (t0, w) in enumerate(TILES):
                    dve.tensor_scalar(g_scaled[0:w, t, :], h_back[0:w, t, :], rstd[0:w, 5 + t:6 + t], None, ALU.mult).then_inc(h_scl, 1)
                for f in range(HT_FILLS):
                    t, c, m = HTF[f]
                    t0, w = TILES[t]
                    dve.wait_ge(ht_filled, KC + f + 1)
                    dve.tensor_tensor(g_xnT[:, c:c + m, t0:t0 + w], ht_out(f),
                                      G_FFN[:, c:c + m].rearrange("p (c a) -> p c a", a=1).to_broadcast([P, m, w]),
                                      ALU.mult).then_inc(ht_drained, 1)
                for n, s in enumerate((hs_done, md_filled)):
                    dve.memset(rw[:, :, n:n + 1], 0.0).then_inc(s, 1)
                with dve.Fori(0, NE) as e:
                    dve.wait_ge(g_filled, e + PAIRS)
                    dve.tensor_copy(gcol[:, :, :], over[:, :, ds(e, 1)].to_broadcast([P, 3, P])).then_inc(gcol_set, 1)
                    dve.wait_ge(g_copied, e + (PAIRS + 1))
                    for j in range(FB):
                        dve.wait_ge(mu_filled, e * 4 + (j + 1))
                        dve.wait_ge(pair_silu, e * 4 + (PAIRS + j + 1))
                        dve.tensor_tensor(g_hS[:, j % 2, :], g_hS[:, j % 2, :], PS[:, 2 + j % 2, 0:T], ALU.mult).then_inc(hs_done, 1)
                        dve.wait_ge(hs_done, e * 4 + (j + 2))
                        dve.wait_ge(md_filled, e * 16 + 1)
                        dve.tensor_tensor(g_hT[:, j, :], g_hS[:, j % 2, :], gbc[:, :], ALU.mult).then_inc(pair_hT, 1)
                    for n in range(KC):
                        dve.wait_ge(md_filled, e * 16 + (n + 2))
                        dve.tensor_tensor(yT[:, n, :], yT[:, n, :], PS[:, 4 + n % 2, 0:T], ALU.add).then_inc(part_added, 1)
            for t, (t0, w) in enumerate(TILES):
                for c in range(4):
                    f = 4 * t + c
                    dve.wait_ge(yt_filled, f + 1)
                    o = h_back[0:w, t, c * 512:(c + 1) * 512]
                    dve.tensor_tensor(o, o, PS[0:w, f % 2, :], ALU.add).then_inc(y_done, 1)

        @block.tensor
        def _(pe):
            pe.wait_ge(consts_set, N_CONSTS)
            pe.wait_ge(rows_in, 144)
            pe.transpose(PS[:, 7, 0:65], rows[:, :], ident[0:65, 0:65]).then_inc(cols_filled, 1)
            pe.wait_ge(cols_set, 1)
            def tokens_transposed(f):
                n, c, m = FILLS[f]
                src, w, _ = NORM[n]
                pe.wait_ge(scaled, n + 1)
                if f >= 8:
                    pe.wait_ge(tT_drained, f - 7)
                for a in range(m):
                    last = pe.transpose(fill_out(f, w)[:, a, :], src[0:w, (c + a) * P:(c + a + 1) * P], ident[0:w, 0:w])
                last.then_inc(tT_filled, 1)

            for f in range(8):
                tokens_transposed(f)

            def project(bank, w, rhs, wt, c, m=P, between=None):
                for k in range(KC):
                    last = pe.matmul(PS[0:m, bank, 0:w], wt[:, k, c:c + m], rhs[:, k, :], start=(k == 0), stop=(k == KC - 1))
                    if between is not None and k < KC - 1:
                        between(k)
                last.then_inc(blk_filled, 1)

            def project_memory(j):
                if j % 3 == 0:
                    pe.wait_ge(w_in_slot[(j // 3) % 2], 16 * (1 + j // 6))
                project(j, MEM, memT, wslot[(j // 3) % 2], (j % 3) * P)

            pe.wait_ge(tT_drained, 8)
            for j in range(3):
                project_memory(j)
            pe.wait_ge(blk_drained, 3)
            for f in range(8, len(FILLS)):
                tokens_transposed(f)
            pe.wait_ge(tT_drained, 17)
            pe.wait_ge(lfpages_in, 16)
            pages_h = lfpages.rearrange("g (t h) -> g h t", h=HF)
            for h in range(HF):
                last = pe.transpose(PS[:, 6, h * 64:(h + 1) * 64], pages_h[:, h, :], ident[0:64, 0:64])
            last.then_inc(lfp_filled, 1)
            pe.wait_ge(lfp_drained, 1)
            for j in range(3, 8):
                project_memory(j)
            pe.wait_ge(blk_drained, 8)
            with pe.Fori(0, 3) as i:
                for half in (1, 0):
                    pe.wait_ge(w_in_slot[half], i * 16 + (48 - 16 * half))
                    for n in range(3):
                        pe.wait_ge(blk_drained, i * 6 + (ORDER.index(3 * half + n) + 3))
                        project(3 * half + n, T, xT, wslot[half], n * P)

            def intra(g, j):
                pe.wait_ge(qw_ready, g * CH + min(j + 1, CH))
                pe.wait_ge(intra_used, g * 17 + max(j, 1))
                rhs = gQW[j % 2].rearrange("p h t -> p (h t)")[:, 0:2 * NCH * (CH - j)] if j < CH else gS
                pe.matmul(PS[:, 6 + j % 2, 0:rhs.shape[1]], ones[:, :], rhs, start=True, stop=True).then_inc(intra_filled, 1)

            with pe.Fori(0, 3) as g:
                for half in (1, 0):
                    pe.wait_ge(w_in_slot[half], g * 16 + (48 + 48 - 16 * half))
                    for n in range(3):
                        b = ORDER.index(3 * half + n)
                        pe.wait_ge(blk_drained, g * 6 + (18 + b + 3))

                        def between(k, b=b):
                            at = ({7: 0, 10: 1, 13: 2} if b == 1 else {3: 0, 7: 1, 11: 2, 13: 3}).get(k)
                            if b and at is not None and (at < 3 or b >= 4):
                                intra(g, 3 * (b - 1) + max(b - 4, 0) + at)

                        project(3 * half + n, T, xT, wslot[half], n * P, between=between)

            def values_by_token(f):
                t, c, m = f // 2, (f % 2) * 4, 4 - 2 * (f % 2)
                t0, w = TILES[t]
                if f >= 2:
                    pe.wait_ge(vt_drained, f - 1)
                for a in range(m):
                    last = pe.transpose(PS[0:w, 6 + f % 2, a * P:(a + 1) * P], raw[:, HI + c + a, t0:t0 + w], ident[:, :])
                last.then_inc(vt_filled, 1)

            def keys_by_token(h):
                if h:
                    pe.wait_ge(kt2_drained, h)
                else:
                    pe.wait_ge(vt_drained, 6)
                for t, (t0, w) in enumerate(TILES):
                    last = pe.transpose(PS[0:w, 6, t * P:(t + 1) * P], raw[:, HFG + h, t0:t0 + w], ident[:, :])
                last.then_inc(kt2_filled, 1)

            def state_parts(h, c):
                q = 10 * h + c
                if q >= 2:
                    pe.wait_ge(ds_used, q - 1)
                if c == 0:
                    pe.wait_ge(kt2_drained, h + 1)
                if c < 8:
                    t, r = c // 4, 32 * (c % 4)
                    last = pe.matmul(PS[:, 4 + q % 2, 0:2 * P].rearrange("p (a v) -> p a v", a=2), ktil[r:r + 32, t, :],
                                     vpar[r:r + 32, :, t, h * P:(h + 1) * P], start=True, stop=True)
                else:
                    pe.wait_ge(sm_set, 2 * h + c - 7)
                    last = pe.matmul(PS[:, 4 + q % 2, :], ktil[0:NS, 2, :], vmask[c - 8].rearrange("p b v -> p (b v)"),
                                     start=True, stop=True)
                last.then_inc(ds_filled, 1)

            def inter_sample(h):
                pe.wait_ge(s_loaded[h % 2], 16 * (h // 2 + 1))
                if h:
                    pe.wait_ge(o_added, h)
                for b in range(NB):
                    c = SEQ + b * NL
                    for v in (slice(0, 64), slice(64, P)):
                        last = pe.matmul(PS[v, 7, c:c + NL], s_in[h % 2][:, b, v], raw[:, HQ + h, c:c + NL], start=True, stop=True)
                last.then_inc(os_filled, 1)

            def inter_prompt(h):
                pe.wait_ge(ds_used, 10 * h + 8)
                for n in range(1, NCH):
                    for v in (slice(0, 64), slice(64, P)):
                        last = pe.matmul(PS[v, 7, n * CH:(n + 1) * CH], states[:, n - 1, v], raw[:, HQ + h, n * CH:(n + 1) * CH],
                                         start=True, stop=True)
                last.then_inc(oi_filled, 1)

            def last_block(n):
                def between(k):
                    if n == 0 and 2 <= k < 14 and k % 2 == 0:
                        if k == 2:
                            pe.wait_ge(hg_done, 4)
                        values_by_token(k // 2 - 1)
                    h = n - 1
                    if 0 < h <= HG and k == 0:
                        inter_prompt(h - 1)
                    if 0 <= h < HG:
                        if k == 2:
                            keys_by_token(h)
                        if 4 <= k < 14:
                            state_parts(h, k - 4)
                        if k == 8:
                            inter_sample(h)
                if n < 4:
                    pe.wait_ge(blk_drained, 44)
                else:
                    pe.wait_ge(blk_drained, 44 + n - 3)
                if n in (0, 3):
                    pe.wait_ge(w_in_slot[1 - n // 3], 96 + 48 - 16 * (1 - n // 3))
                    slot = 1 - n // 3
                if n in (6, 8):
                    slot = (8 - n) // 2
                    pe.wait_ge(w_in_slot[slot], 144 + 16 * (1 - slot))
                slot, c = [(1, n), (0, n - 3), (1, n - 6), (0, n - 8)][(n >= 3) + (n >= 6) + (n >= 8)]
                project(n % 4, T, xT, wslot[slot], c * P, between=between)

            for n in range(10):
                last_block(n)
            pe.wait_ge(wff_in, 32)
            pe.wait_ge(blk_drained, 51)
            project(2, T, xT, w_ff, 0, HF)

            def tokens_out(n):
                dst, m, srcs = TOKF[n]
                if n >= 2:
                    pe.wait_ge(tk_drained, n - 1)
                for a, s in enumerate(srcs):
                    last = pe.transpose(PS[0:m, 6 + n % 2, a * P:(a + 1) * P], s, ident[:, :])
                last.then_inc(tk_filled, 1)

            for n, (src, w, g) in enumerate(NORMS):
                pe.wait_ge(hn_sq, n + 1)
                pe.matmul(PS[0:NN, 0, 0:w], row_of[:, NN - 1 - n:2 * NN - 1 - n], sq[:, n % 2, 0:w], start=(n == 0), stop=(n == NN - 1)).then_inc(hn_sum, 1)
            for n in range(NVF):
                tokens_out(n)
            pe.wait_ge(hn_rcp, 1)
            for n, (src, w, g) in enumerate(NORMS):
                if n >= 3:
                    pe.wait_ge(hn_done, n - 2)
                pe.matmul(PS[:, 1 + n % 3, 0:w], ident[0:NN, n:n + 1].to_broadcast([NN, P]), hn_r[:, 0:w], start=True, stop=True).then_inc(hn_rows, 1)

            pe.wait_ge(lf_done, 1)
            for t, (t0, n) in enumerate(TILES):
                last = pe.transpose(PS[0:n, 4, t * HF:(t + 1) * HF], lfT[:, t0:t0 + n], ident[0:HF, 0:HF])
            last.then_inc(lft_filled, 1)
            pe.wait_ge(hn_done, NN)
            for n in range(NVF, NTF):
                tokens_out(n)
            pe.wait_ge(lft_drained, 1)
            pe.matmul(PS[0:HF, 5, 0:P], lftok[:, 0, :], tri_le[:, :], start=True, stop=True)
            pe.matmul(PS[0:HF, 5, P:SEQ], lftok[:, 0, :], ones[:, :], start=True, stop=False)
            pe.matmul(PS[0:HF, 5, P:SEQ], lftok[:, 1, :], tri_le[:, :], start=False, stop=True).then_inc(c_filled, 1)
            pe.wait_ge(lfs_done, 1)
            pe.wait_ge(lfm_done, 1)
            pe.wait_ge(tk_drained, NTF)
            new = lfm[:, :, :].rearrange("p b h -> p (b h)")
            for g in range(NPG):
                o = PS[0:NB * HF, g // 4, (g % 4) * P:(g % 4 + 1) * P]
                pe.matmul(o, lfp[:, g, :, :].rearrange("p b h -> p (b h)"), tri_gt[:, :], start=True, stop=False)
                pe.matmul(o, lfs[:, g, :, :].rearrange("p b h -> p (b h)"), ones[:, :], start=False, stop=False)
                pe.matmul(o, new, ones[0:NS, :], start=False, stop=True)
            pe.matmul(PS[0:NB * HF, 2, 0:NS], new, tri_gt[0:NS, 0:NS], start=True, stop=True).then_inc(dec_filled, 1)

            pe.wait_ge(decay_set, 1)
            pe.wait_ge(negc_set, 1)
            for s in range(NU + 2):
                if s < NU:
                    fox, h, qb = UNITS[s]
                    if s >= 2:
                        pe.wait_ge(pa_exp, s - 1)
                    o = PS[:, s % 2, 0:width(s)]
                    q = raw[:, (FQ if fox else MQ) + h, qb * P:(qb + 1) * P]
                    k = raw[:, FK + h, 0:width(s)] if fox else mraw[:, h, :]
                    last = pe.matmul(o, q, k, start=True, stop=not fox)
                    if fox:
                        pe.matmul(o, ident[0:HF, h:h + 1].to_broadcast([HF, P]), negc[:, 0:width(s)], start=False, stop=False)
                        last = pe.matmul(PS[:, s % 2, qb * P:(qb + 1) * P], ident[:, :], causal[:, :], start=False, stop=True)
                    last.then_inc(pa_scored, 1)
                if 1 <= s <= NU:
                    u = s - 1
                    pe.wait_ge(pa_prob, u + 1)
                    if u >= 2:
                        pe.wait_ge(pa_tc, u - 1)
                    for a in range(width(u) // P):
                        last = pe.transpose(PS[:, 2 + u % 2, a * P:(a + 1) * P], probs[:, u % 2, a * P:(a + 1) * P], ident[:, :])
                    last.then_inc(pa_t, 1)
                if s >= 2:
                    u = s - 2
                    fox, h, qb = UNITS[u]
                    pe.wait_ge(pa_tc, u + 1)
                    if u >= 2:
                        pe.wait_ge(pa_out, u - 1)
                    na = width(u) // P
                    for a in range(na):
                        v = vtok[:, a, h * P:(h + 1) * P] if fox else mtok[:, a, MW + h * P:MW + (h + 1) * P]
                        last = pe.matmul(PS[:, 4 + u % 2, 0:P], v, probsT[:, u % 2, a, :], start=(a == 0), stop=(a == na - 1))
                    last.then_inc(pa_pv, 1)

            pe.wait_ge(pa_out, NU)

            def keys_in(b, u, first=False):
                for g in range(9):
                    bank = 2 * ((u + g) % 2)
                    if g < NPG:
                        pe.wait_ge(k_in[g], b * 16 + (32 if g < 5 else 16))
                    else:
                        pe.wait_ge(mk_loaded, b * 16 + 16)
                    if g >= 2 or not first:
                        pe.wait_ge(kt_act, b * 9 + (g - 1))
                        pe.wait_ge(kt_dve, b * 9 + (g - 1))
                    if g < NPG:
                        for h in range(HF):
                            last = pe.transpose(PS[:, bank + h // 4, (h % 4) * P:(h % 4 + 1) * P],
                                                kpage[g][:, h * P:(h + 1) * P], ident[:, :])
                    else:
                        for h in range(HM):
                            for a in range(2):
                                c = ((h % 2) * 2 + a) * P
                                last = pe.transpose(PS[:, bank + h // 2, c:c + P], mk_in[:, a, h * P:(h + 1) * P], ident[:, :])
                    last.then_inc(kt_filled, 1)

            def decode_scores(b, first=False):
                pe.wait_ge(kt_act, b * 9 + 9)
                pe.wait_ge(kt_dve, b * 9 + 9)
                pe.wait_ge(q_set, b + 1)
                if not first:
                    pe.wait_ge(d_tc, b * 2)
                for c in range(3):
                    w = 512 if c < 2 else NS
                    for h in range(HF):
                        i = h % 4
                        k = keysT[:, h, c * 512:c * 512 + w] if c < 2 else raw[:, FK + h, SEQ:T]
                        pe.matmul(PS[32 * i:32 * i + 32, 4 + c, 0:w], q_rows[:, h, :], k, start=(h < 4), stop=False)
                    for i in range(4):
                        pe.matmul(PS[32 * i:32 * i + 32, 4 + c, 0:w], sel_b[:, i, :], decay[:, c * 512:c * 512 + w],
                                  start=False, stop=(c < 2))
                for i in range(4):
                    pe.matmul(PS[32 * i:32 * i + 32, 6, 0:NS], rep4[:, :, :].rearrange("p h q -> p (h q)"), causal_b,
                              start=False, stop=True)
                for h in range(HM):
                    last = pe.matmul(PS[32 * h:32 * h + 32, 6, 64:64 + MEM], q_rows[:, HF + h, :], mkeysT[:, h, :],
                                     start=True, stop=True)
                last.then_inc(d_scored, 1)

            def decode_values(b, first=False):
                pe.wait_ge(d_exp, b + 1)
                for g in range(NPG):
                    pe.transpose(PS[:, 4 + g // 4, (g % 4) * P:(g % 4 + 1) * P], dprob[:, g * P:(g + 1) * P], ident[:, :])
                for a in range(2):
                    pe.transpose(PS[:, 6, a * P:(a + 1) * P], mprob[:, a * P:(a + 1) * P], ident[:, :])
                pe.transpose(PS[0:NS, 6, 2 * P:3 * P], dprob[:, PAST:KEYS], ident[:, :]).then_inc(d_t, 1)
                pe.wait_ge(d_tc, b * 2 + 2)
                pe.wait_ge(v_loaded, b * 144 + 144)
                if not first:
                    pe.wait_ge(d_out, b)
                for hs in (range(4), range(4, HF)):
                    for g in range(NPG + 1):
                        for h in hs:
                            i = h % 4
                            o = PS[32 * i:32 * i + 32, 7, (h // 4) * P:(h // 4 + 1) * P]
                            if g < NPG:
                                pe.matmul(o, dprobT[:, g, 32 * i:32 * i + 32], vpages[:, g, h * P:(h + 1) * P], start=(g == 0), stop=False)
                            else:
                                pe.matmul(o, dprobT[0:NS, NPG + 2, 32 * i:32 * i + 32], vtok[0:NS, 2, h * P:(h + 1) * P], start=False, stop=True)
                for a in range(2):
                    for h in range(HM):
                        last = pe.matmul(PS[32 * h:32 * h + 32, 7, 2 * P:3 * P], dprobT[:, NPG + a, 32 * h:32 * h + 32],
                                         mv_in[:, a, h * P:(h + 1) * P], start=(a == 0), stop=(a == 1))
                last.then_inc(d_pv, 1)

            def decode_heads(b):
                pe.wait_ge(d_oc, b + 1)
                pe.transpose(PS[:, 7, 0:P], dout[:, 0, :], ident[:, :])
                pe.transpose(PS[:, 7, P:P + 64], dout[0:64, 1, :], ident[0:64, 0:64])
                pe.transpose(PS[:, 7, 2 * P:3 * P], dout[:, 2, :], ident[:, :]).then_inc(d_ot, 1)

            keys_in(0, 0, True)
            decode_scores(0, True)
            keys_in(1, 1)
            decode_values(0, True)
            decode_scores(1)
            decode_heads(0)
            with pe.Fori(0, 3) as i:
                for u in range(2):
                    keys_in(i * 2 + (u + 2), u)
                    decode_values(i * 2 + (u + 1))
                    decode_scores(i * 2 + (u + 2))
                    decode_heads(i * 2 + (u + 1))
            decode_values(NB - 1)
            decode_heads(NB - 1)

            def by_token(n):
                pe.wait_ge(wo_drained, n + 1)
                if n >= 2:
                    pe.wait_ge(h_added, 3 * (n - 1))
                for t, (t0, w) in enumerate(TILES):
                    last = pe.transpose(PS[0:w, 2 + n % 2, t * P:(t + 1) * P], attnT[:, n % 2, t0:t0 + w], ident[:, :])
                last.then_inc(at_filled, 1)

            def block_transposed(n):
                pe.wait_ge(h_added, 3 * n + 3)
                if n >= 2:
                    pe.wait_ge(ht_drained, n - 1)
                for t, (t0, w) in enumerate(TILES):
                    last = pe.transpose(PS[:, 5 + n % 2, t0:t0 + w], h_tok[0:w, t, n * P:(n + 1) * P], ident[0:w, 0:w])
                last.then_inc(ht_filled, 1)

            def block_logits(n):
                pe.wait_ge(ht_drained, n + 1)
                last = pe.matmul(PS[0:NG + NE, 4, 0:T], w_rt[:, n, :], xgain[:, n % 2, :], start=(n == 0), stop=(n == KC - 1))
                last.then_inc(lg_filled, 1)

            pe.wait_ge(d_out, NB)
            for n in range(KC + 3):
                if n < KC:
                    pe.wait_ge(wo_in[(n // 2) % 3], 16 * (n // 6 + 1))
                    if n >= 2:
                        pe.wait_ge(wo_drained, n - 1)
                    for k in range(KC):
                        c = (n % 2) * P
                        last = pe.matmul(PS[:, n % 2, 0:T], wo_slot[(n // 2) % 3][:, k, c:c + P], cat[:, k, :], start=(k == 0), stop=(k == KC - 1))
                    last.then_inc(wo_filled, 1)
                if n == 2:
                    pe.wait_ge(rt_in, 64)
                    pe.matmul(PS[:, 7, 0:NG + NE], ones[0:1, :], b_rt, start=True, stop=True).then_inc(bias_filled, 1)
                if 1 <= n <= KC:
                    by_token(n - 1)
                if 2 <= n <= KC + 1:
                    block_transposed(n - 2)
                if n >= 3:
                    block_logits(n - 3)
            pe.wait_ge(lgT_set, 2)
            for t, (t0, w) in enumerate(TILES):
                last = pe.transpose(PS[0:w, 7, 64 + t * 64:64 + t * 64 + NG + NE], lgT[:, t0:t0 + w], ident[0:NG + NE, 0:NG + NE])
            last.then_inc(lg_filled, 1)
            pe.wait_ge(h_scl, 3)

            pe.wait_ge(moe_prep, 2)
            chosen = rw[:, :, NE:2 * NE]
            pe.matmul(PS[:, 5, 128:128 + SLOTS], ones[:, :], tri_le[:, 0:SLOTS], start=True, stop=True)
            for t, (t0, w) in enumerate(TILES):
                o = PS[0:w, 5, t * NE:(t + 1) * NE]
                for a in range(t):
                    pe.matmul(o, ones[:, 0:w], chosen[:, a, :], start=(a == 0), stop=False)
                last = pe.matmul(o, tri_le[0:w, 0:w], chosen[0:w, t, :], start=(t == 0), stop=True)
            last.then_inc(rank_filled, 1)

            def gather(p, chunks):
                for c in chunks:
                    o = PS[:, 2 + c // 4, (c % 4) * P:(c % 4 + 1) * P]
                    for t in range(3):
                        last = pe.matmul(o, h_scaled[:, t, c * P:(c + 1) * P], pick_tok[:, t, :, :].rearrange("p x s -> p (x s)"),
                                         start=(t == 0), stop=(t == 2))
                    if c % 4 == 3:
                        last.then_inc(xg_filled, 1)

            def pair_pe(p, first=False, last_pair=False):
                pe.wait_ge(xg_drained, p * 4 + 4)
                for which in range(2):
                    for half in range(2):
                        for x in range(2):
                            u = 4 * which + 2 * half + x
                            pe.wait_ge(unit_in[u % 6], p * 32 + (16 * (u // 6) + 16))
                        for k in range(KC // 2):
                            for x in range(2):
                                u = 4 * which + 2 * half + x
                                kk = half * KC // 2 + k
                                wt = unit[u % 6].rearrange("p (k n) -> p k n", n=FFW)
                                last = pe.matmul(PS[x * SLOTS:(x + 1) * SLOTS, which, :], xgT[:, kk, x * SLOTS:(x + 1) * SLOTS], wt[:, k, :],
                                                 start=(kk == 0), stop=(kk == KC - 1))
                                if k == KC // 2 - 1:
                                    last.then_inc(units_used, 1)
                if not last_pair:
                    pe.wait_ge(picked_set, p + 2)
                    if not first:
                        pe.wait_ge(part_added, p * KC)
                    gather(p + 1, range(8))
                pe.wait_ge(pg_set, p + 1)
                for t, (t0, w) in enumerate(TILES):
                    last = pe.matmul(PS[:, 7, t0:t0 + w], pick_gate[0:w, t, :, :].rearrange("p x s -> p (x s)"), ident[0:w, 0:w],
                                     start=True, stop=True)
                last.then_inc(g_filled, 1)
                pe.wait_ge(pair_h, p + 1)
                for k in range(FB):
                    last = pe.transpose(PS[:, 6, k * P:(k + 1) * P], hS[:, k * P:(k + 1) * P], ident[:, :])
                last.then_inc(ph_filled, 1)
                if not last_pair:
                    gather(p + 1, range(8, KC))
                pe.wait_ge(pair_hT, p + 1)
                pe.wait_ge(g_copied, p + 1)
                for half in range(2):
                    for x in range(2):
                        u = 8 + 2 * half + x
                        pe.wait_ge(unit_in[u % 6], p * 32 + 32)
                    for k in range(FB // 2):
                        kk = half * FB // 2 + k
                        for n in range(4):
                            for x in range(2):
                                wt = unit[(8 + 2 * half + x) % 6].rearrange("p (k n) -> p k n", n=D)
                                last = pe.matmul(PS[x * SLOTS:(x + 1) * SLOTS, YB[n], :], hT[:, kk, x * SLOTS:(x + 1) * SLOTS],
                                                 wt[:, k, n * 512:(n + 1) * 512], start=(kk == 0), stop=(kk == FB - 1))
                                if kk == FB - 1 and x == 1:
                                    last.then_inc(yst_filled, 1)
                                elif k == FB // 2 - 1 and n == 3:
                                    last.then_inc(units_used, 1)
                if not last_pair:
                    pe.wait_ge(xg_drained, p * 4 + 8)
                for n in range(KC):
                    if n % 4 == 0:
                        if (n // 4) % 2 == 0:
                            pe.wait_ge(yst_act, p * 2 + (n // 8 + 1))
                        else:
                            pe.wait_ge(yst_dve, p * 2 + (n // 8 + 1))
                    if n >= 4:
                        pe.wait_ge(part_added, p * KC + (n - 3))
                    last = pe.matmul(PS[:, 2 + n % 4, 0:T], yslot[:, n * P:(n + 1) * P], gate_slot[:, :], start=True, stop=True)
                    last.then_inc(part_filled, 1)

            pe.wait_ge(picked_set, 1)
            gather(0, range(KC))
            pe.wait_ge(slots_set, 2)
            pe.matmul(PS[:, 6, 0:2], ones[:, :], n_over, start=True, stop=True).then_inc(over_filled, 1)
            pe.wait_ge(overflow_set, 1)
            pair_pe(0, True)
            with pe.Fori(0, PAIRS - 2) as i:
                pair_pe(i + 1)
            pair_pe(PAIRS - 1, last_pair=True)

            pe.wait_ge(part_added, PAIRS * KC)
            n_past = pe.value_load(overflow[0:1, 0:1], min_val=0, max_val=2 * T)
            with pe.If(n_past > 0):
                for f, (t, c, m) in enumerate(HTF):
                    pe.wait_ge(h_scl, 3 + t + 1)
                    if f >= 2:
                        pe.wait_ge(ht_drained, KC + f - 1)
                    w = TILES[t][1]
                    for a in range(m):
                        last = pe.transpose(ht_out(f)[:, a, :], g_scaled[0:w, t, (c + a) * P:(c + a + 1) * P], ident[0:w, 0:w])
                    last.then_inc(ht_filled, 1)
                pe.wait_ge(ht_drained, KC + HT_FILLS)
                with pe.Fori(0, NE) as e:
                    pe.wait_ge(gcol_set, e + 1)
                    for t, (t0, w) in enumerate(TILES):
                        last = pe.matmul(PS[:, 6, t0:t0 + w], gcol[0:w, t, :], ident[0:w, 0:w], start=True, stop=True)
                    last.then_inc(g_filled, 1)
                    for j in range(FB):
                        for which, wt, sem_filled in ((0, wg_u, mg_filled), (1, wu_u, mu_filled)):
                            if j % 2 == 0:
                                pe.wait_ge(unit_in[j + which], e * 16 + (32 * PAIRS + 16))
                            if which == 0:
                                pe.wait_ge(pair_silu, e * 4 + (PAIRS + max(j - 1, 0)))
                            else:
                                pe.wait_ge(hs_done, e * 4 + max(j, 1))
                            for k in range(KC):
                                last = pe.matmul(PS[:, 2 * which + j % 2, 0:T], wt[j // 2][:, k, (j % 2) * P:(j % 2 + 1) * P],
                                                 g_xnT[:, k, :], start=(k == 0), stop=(k == KC - 1))
                            last.then_inc(sem_filled, 1)
                    pe.wait_ge(pair_hT, e * 4 + (PAIRS + 4))
                    for n in range(KC):
                        if n % 8 == 0:
                            pe.wait_ge(unit_in[4 + n // 8], e * 16 + (32 * PAIRS + 16))
                        pe.wait_ge(part_added, e * 16 + (PAIRS * KC + max(n - 1, 0)))
                        for k in range(FB):
                            last = pe.matmul(PS[:, 4 + n % 2, 0:T], wd_u[n // 8][:, k, (n % 8) * P:(n % 8 + 1) * P], g_hT[:, k, :],
                                             start=(k == 0), stop=(k == FB - 1))
                        last.then_inc(md_filled, 1)
                pe.wait_ge(part_added, (PAIRS + NE) * KC)
            for t, (t0, w) in enumerate(TILES):
                for c in range(4):
                    f = 4 * t + c
                    if f >= 2:
                        pe.wait_ge(y_done, f - 1)
                    for a in range(4):
                        last = pe.transpose(PS[0:w, f % 2, a * P:(a + 1) * P], yT[:, 4 * c + a, t0:t0 + w], ident[:, :])
                    last.then_inc(yt_filled, 1)


N_CONSTS = 26
G_STEPS = 42


_INS = ['x_prompt', 'x_sample', 'cache_fox_k', 'cache_fox_v', 'cache_fox_logf', 'cache_mem_k', 'cache_mem_v',
        'state_hgrn', 'page_table', 'mem_prompt', 'g_attn_norm', 'w_in', 'b_fox_f', 'g_fox_q', 'g_fox_k', 'lb_logits',
        'g_hgrn_out', 'g_mem_norm', 'w_mem_kv', 'g_mem_q', 'g_mem_k', 'w_out', 'g_ffn_norm', 'w_router_group',
        'b_router_group', 'w_router_expert', 'b_router_expert', 'w_gate_e', 'w_up_e', 'w_down_e']
_OUTS = [(1, 256, 2048), (8, 4, 2048), (1, 1, 256, 6, 128), (1, 1, 256, 6, 128), (1, 1, 256, 6), (1, 1, 6, 128, 128),
         (1, 1, 256, 4, 128), (1, 1, 256, 4, 128), (1, 8, 4, 6, 128), (1, 8, 4, 6, 128), (1, 8, 4, 6), (1, 8, 6, 128, 128)]


def kernel(**inputs):
    import numpy as _np
    import concourse.bacc as _bacc
    from concourse import mybir as _mybir
    from concourse.bass_utils import run_bass_kernel_spmd as _run

    nc = _bacc.Bacc("TRN2", target_bir_lowering=False, num_devices=1)
    arrays, args = {}, []
    for name in _INS:
        a = _np.ascontiguousarray(inputs[name])
        arrays[f"in_{name}_dram"] = a
        args.append(nc.dram_tensor(f"in_{name}_dram", a.shape, _mybir.dt.from_np(a.dtype), kind="ExternalInput").ap())
    for i, shape in enumerate(_OUTS):
        args.append(nc.dram_tensor(f"out_{i}_dram", shape, _mybir.dt.float32, kind="ExternalOutput").ap())
    build(nc, *args)
    r = _run(nc, [arrays], core_ids=[0])
    return tuple(r.results[0][f"out_{i}_dram"] for i in range(len(_OUTS)))
```
